# Optimizing a Trainium2 kernel written in Bass

```python
import jax, jax.numpy as jnp
from jax import lax
import numpy as np

D_MODEL = 1024
BATCH = 1
SEQ = 1024
DEPTH = 1

HEAD_DIM = 64
N_HEADS = 8
N_KV_HEADS = 2
GQA_GROUP = N_HEADS // N_KV_HEADS
ATTN_WIDTH = N_HEADS * HEAD_DIM
KV_WIDTH = N_KV_HEADS * HEAD_DIM
POOL_WIDTH = D_MODEL // 2
POOL_WINDOWS = (2, 4, 8, 16)
N_POOL_GROUPS = len(POOL_WINDOWS)
POOL_GROUP_DIM = POOL_WIDTH // N_POOL_GROUPS
MAX_POOL_WINDOW = max(POOL_WINDOWS)
IN_WIDTH = ATTN_WIDTH + 2 * KV_WIDTH + POOL_WIDTH
MIX_WIDTH = ATTN_WIDTH + POOL_WIDTH

WINDOW = 128
BLOCK = 128
ROT_DIM = HEAD_DIM // 4
ROPE_THETA = 500000.0
D_FF = 4 * D_MODEL
N_MOD = 6
EPS = 1e-6
MAX_START = 1024

kernel_name = "hybrid_swa_sink_pool_adaln_block"

def rms_norm(x, g):
    xf = x.astype(jnp.float32)
    y = xf * lax.rsqrt(jnp.mean(xf * xf, axis=-1, keepdims=True) + EPS)
    return (y * g.astype(jnp.float32)).astype(x.dtype)

def apply_partial_rope(x, cos, sin):
    half = ROT_DIM // 2
    x1 = x[..., :half]
    x2 = x[..., half:ROT_DIM]
    cos = cos.astype(x.dtype)
    sin = sin.astype(x.dtype)
    return jnp.concatenate([x1 * cos - x2 * sin, x2 * cos + x1 * sin, x[..., ROT_DIM:]], axis=-1)

def band_mask(n_blocks):
    n = jnp.arange(n_blocks)[:, None, None]
    i = jnp.arange(BLOCK)[None, :, None]
    j = jnp.arange(2 * BLOCK)[None, None, :]
    qpos = n * BLOCK + i
    kpos = (n - 1) * BLOCK + j
    return (kpos <= qpos) & (qpos - kpos < WINDOW) & (kpos >= 0)

def sliding_window_sink_attention(q, k, v, sinks):
    B, S = q.shape[0], q.shape[1]
    nb = S // BLOCK
    qb = q.reshape(B, nb, BLOCK, N_KV_HEADS, GQA_GROUP, HEAD_DIM)
    kb = k.reshape(B, nb, BLOCK, N_KV_HEADS, HEAD_DIM)
    vb = v.reshape(B, nb, BLOCK, N_KV_HEADS, HEAD_DIM)
    pad = ((0, 0), (1, 0), (0, 0), (0, 0), (0, 0))
    k_band = jnp.concatenate([jnp.pad(kb[:, :-1], pad), kb], axis=2)
    v_band = jnp.concatenate([jnp.pad(vb[:, :-1], pad), vb], axis=2)
    scores = jnp.einsum('bnqhgd,bnkhd->bnhgqk', qb, k_band).astype(jnp.float32)
    scores = scores * (HEAD_DIM ** -0.5)
    mask = band_mask(nb)[None, :, None, None]
    scores = jnp.where(mask, scores, jnp.float32(-1e30))
    sink = jnp.broadcast_to(sinks.astype(jnp.float32).reshape(1, 1, N_KV_HEADS, GQA_GROUP, 1, 1),
                            scores.shape[:-1] + (1,))
    probs = jax.nn.softmax(jnp.concatenate([scores, sink], axis=-1), axis=-1)[..., :-1]
    out = jnp.einsum('bnhgqk,bnkhd->bnqhgd', probs.astype(v.dtype), v_band)
    return out.reshape(B, S, ATTN_WIDTH)

def multiscale_pool(u):
    S = u.shape[1]
    uf = u.astype(jnp.float32)
    cs = jnp.cumsum(uf, axis=1)
    cs_pad = jnp.pad(cs, ((0, 0), (MAX_POOL_WINDOW, 0), (0, 0), (0, 0)))
    t = jnp.arange(S)
    means = []
    for g, w in enumerate(POOL_WINDOWS):
        win_sum = cs[:, :, g] - cs_pad[:, MAX_POOL_WINDOW - w:MAX_POOL_WINDOW - w + S, g]
        count = jnp.minimum(t + 1, w).astype(jnp.float32)[None, :, None]
        means.append(win_sum / count)
    mean = jnp.stack(means, axis=2)
    return (mean - uf).astype(u.dtype)

def setup_inputs(seed: int = 0) -> dict:
    key = jax.random.key(seed)
    ks = jax.random.split(key, 20)
    f32 = jnp.float32
    nrm = lambda k, shape, s: jax.random.normal(k, shape, f32) * s
    x = nrm(ks[0], (BATCH, SEQ, D_MODEL), 1.0)
    c = nrm(ks[1], (BATCH, D_MODEL), 1.0)
    start = jax.random.randint(ks[2], (BATCH, 1), 0, MAX_START, dtype=jnp.int32)
    positions = (start + jnp.arange(SEQ, dtype=jnp.int32)[None, :]).astype(jnp.int32)
    return {
        "x": x,
        "c": c,
        "positions": positions,
        "w_ada": nrm(ks[3], (DEPTH, D_MODEL, N_MOD * D_MODEL), 0.5 * D_MODEL ** -0.5),
        "b_ada": nrm(ks[4], (DEPTH, N_MOD * D_MODEL), 0.01),
        "norm1_g": 1.0 + nrm(ks[5], (DEPTH, D_MODEL), 0.05),
        "w_in": nrm(ks[6], (DEPTH, D_MODEL, IN_WIDTH), D_MODEL ** -0.5),
        "q_norm_g": 1.0 + nrm(ks[7], (DEPTH, HEAD_DIM), 0.05),
        "k_norm_g": 1.0 + nrm(ks[8], (DEPTH, HEAD_DIM), 0.05),
        "attn_sinks": nrm(ks[9], (DEPTH, N_HEADS), 0.5),
        "pool_w": nrm(ks[10], (DEPTH, N_POOL_GROUPS, POOL_GROUP_DIM, POOL_GROUP_DIM), POOL_GROUP_DIM ** -0.5),
        "pool_scale": 1.0 + nrm(ks[11], (DEPTH, POOL_WIDTH), 0.1),
        "w_o": nrm(ks[12], (DEPTH, MIX_WIDTH, D_MODEL), MIX_WIDTH ** -0.5),
        "norm2_g": 1.0 + nrm(ks[13], (DEPTH, D_MODEL), 0.05),
        "w_mlp_in": nrm(ks[14], (DEPTH, D_MODEL, D_FF), D_MODEL ** -0.5),
        "w_mlp_out": nrm(ks[15], (DEPTH, D_FF, D_MODEL), D_FF ** -0.5),
    }

def reference(x, c, positions, w_ada, b_ada, norm1_g, w_in, q_norm_g, k_norm_g, attn_sinks,
              pool_w, pool_scale, w_o, norm2_g, w_mlp_in, w_mlp_out):
    B, S, D = x.shape
    inv_freq = ROPE_THETA ** (-jnp.arange(0, ROT_DIM, 2, dtype=jnp.float32) / ROT_DIM)
    ang = positions.astype(jnp.float32)[..., None] * inv_freq
    cos, sin = jnp.cos(ang), jnp.sin(ang)
    cos_q, sin_q = cos[:, :, None, None, :], sin[:, :, None, None, :]
    cos_k, sin_k = cos[:, :, None, :], sin[:, :, None, :]
    c_act = jax.nn.silu(c)
    h_res = x
    for l in range(DEPTH):
        mod = (c_act @ w_ada[l] + b_ada[l])[:, None, :]
        sh1, sc1, g1, sh2, sc2, g2 = jnp.split(mod, N_MOD, axis=-1)

        h = rms_norm(h_res, norm1_g[l]) * (1.0 + sc1) + sh1
        proj = h @ w_in[l]
        q = proj[..., :ATTN_WIDTH].reshape(B, S, N_KV_HEADS, GQA_GROUP, HEAD_DIM)
        k = proj[..., ATTN_WIDTH:ATTN_WIDTH + KV_WIDTH].reshape(B, S, N_KV_HEADS, HEAD_DIM)
        v = proj[..., ATTN_WIDTH + KV_WIDTH:ATTN_WIDTH + 2 * KV_WIDTH].reshape(B, S, N_KV_HEADS, HEAD_DIM)
        u = proj[..., ATTN_WIDTH + 2 * KV_WIDTH:].reshape(B, S, N_POOL_GROUPS, POOL_GROUP_DIM)

        q = apply_partial_rope(rms_norm(q, q_norm_g[l]), cos_q, sin_q)
        k = apply_partial_rope(rms_norm(k, k_norm_g[l]), cos_k, sin_k)
        attn_out = sliding_window_sink_attention(q, k, v, attn_sinks[l])

        pooled = multiscale_pool(u)
        pool_out = jnp.einsum('bsgc,gcd->bsgd', pooled, pool_w[l])
        pool_out = pool_out.reshape(B, S, POOL_WIDTH) * pool_scale[l]

        mixed = jnp.concatenate([attn_out, pool_out], axis=-1) @ w_o[l]
        h_res = h_res + g1 * mixed

        h2 = rms_norm(h_res, norm2_g[l]) * (1.0 + sc2) + sh2
        ff = jnp.square(jax.nn.relu(h2 @ w_mlp_in[l])) @ w_mlp_out[l]
        h_res = h_res + g2 * ff
    return h_res


_drawn_inputs = setup_inputs


def setup_inputs(seed=0):
    import zlib

    import numpy as np

    out = dict(_drawn_inputs(seed))
    spreads = {}
    factors = {'b_ada': 3.505,
     'norm1_g': 5.162,
     'q_norm_g': 8.0,
     'k_norm_g': 8.0,
     'attn_sinks': 200.0,
     'pool_scale': 2.726,
     'norm2_g': 7.256}
    for name, (base, spread) in spreads.items():
        noise = np.random.default_rng([zlib.crc32(name.encode()), seed]).standard_normal(out[name].shape)
        drawn = base * np.exp(spread * noise) if base else spread * noise
        out[name] = __import__('jax').numpy.asarray(drawn.astype(out[name].dtype))
    for name, factor in factors.items():
        out[name] = (out[name] * factor).astype(out[name].dtype)
    return out
```

```python
from contextlib import ExitStack

import concourse.bass as bass
import numpy as np
from concourse import mybir

P = 128
F32 = mybir.dt.float32
F32R = mybir.dt.float32r
BF16 = mybir.dt.bfloat16
I32 = mybir.dt.int32
ALU = mybir.AluOpType
ACT = mybir.ActivationFunctionType
AX_X = mybir.AxisListType.X

HEAD_DIM = 64
POOL_WINDOWS = (2, 4, 8, 16)
ROT_DIM = HEAD_DIM // 4
HALF = ROT_DIM // 2
ROPE_THETA = 500000.0
EPS = 1e-6
MASKED = -1e30
FB = 256
RING = 4
SH1, SC1, G1, SH2, SC2, G2 = range(6)

TWO_PI_1 = 6.28125
TWO_PI_2 = 0.0019350051879882812
TWO_PI_3 = 2 * np.pi - TWO_PI_1 - TWO_PI_2
ROUND_MAGIC = 12582912.0
PI_LIMIT = 3.1415925


def bcast(ap, axis, n):
    a = ap.unsqueeze(axis)
    shape = list(a.shape)
    shape[axis] = n
    return a.to_broadcast(shape)


def build(nc, x, c, positions, w_ada, b_ada, norm1_g, w_in, q_norm_g, k_norm_g, attn_sinks,
          pool_w, pool_scale, w_o, norm2_g, w_mlp_in, w_mlp_out, out):
    S, D = x.shape[1], x.shape[2]
    IN = w_in.shape[2]
    FF = w_mlp_in.shape[2]
    NH = attn_sinks.shape[1]
    PW = pool_scale.shape[1]
    AW = NH * HEAD_DIM
    KVW = (IN - AW - PW) // 2
    NKV = KVW // HEAD_DIM
    G = NH // NKV
    NP = pool_w.shape[1]
    NT = S // P
    KD = D // P
    NB = FF // FB
    NF = FB // P
    NHN = NH + NKV
    QKV = AW + 2 * KVW
    SCALE = HEAD_DIM ** -0.5
    assert NT == 8 and KD == 8 and G == 4 and NKV == 2 and NP == 4 and D == 1024

    x_rows = x[0]
    out_rows = out[0]
    wada = w_ada[0].rearrange("(p k) n -> p k n", k=KD)
    win = w_in[0].rearrange("(k p) n -> p k n", p=P)
    wo = w_o[0].rearrange("(k p) n -> p k n", p=P)
    w1 = w_mlp_in[0].rearrange("(k p) n -> p k n", p=P)
    w2 = w_mlp_out[0]

    with ExitStack() as ctx:
        def sem(name):
            return ctx.enter_context(nc.semaphore(name))

        def sb(name, shape, dt=F32):
            return ctx.enter_context(nc.sbuf_tensor(name, shape, dt))

        ident = sb("ident", [P, P])
        identr = sb("identr", [P, P], F32R)
        ones = sb("ones", [P, P])
        small = sb("small", [P, 256])
        cols = sb("cols", [P, 72])
        a1, b1, a2, b2 = (small[:, 8 * j:8 * j + 8] for j in range(4))
        silu = small[:, 32:40]
        ctmp = small[:, 40:48]
        ssx = small[:, 48:56]
        rx = small[:, 56:64]
        ss2 = small[:, 64:72]
        r2 = small[:, 72:80]
        ssq = small[:, 80:90]
        rq = small[:, 90:100]
        sink = small[:, 100:108]
        nsink = small[:, 108:116]
        negm = small[:, 116:124]
        earg = small[:, 124:132]
        es = small[:, 132:140]
        den = small[:, 140:148]
        rden = small[:, 148:156]
        mx = small[:, 156:164]
        mhalf = small[:, 164:174]
        slots = sb("slots", [P, NT, D])
        raw = sb("raw", [P, RING, 1024])
        acc = sb("acc", [P, D])

        with ExitStack() as mix_ctx:
            def mb(name, shape, dt=F32):
                return mix_ctx.enter_context(nc.sbuf_tensor(name, shape, dt))
            wih = mb("w_in_hi", [P, KD, IN], F32R)
            wil = mb("w_in_lo", [P, KD, IN], F32R)
            xh = mb("xh", [P, 2, D])
            hTh = mb("hT_hi", [P, KD, P], F32R)
            hTl = mb("hT_lo", [P, KD, P], F32R)
            qkn = mb("qkn", [P, NHN, HEAD_DIM])
            q2 = mb("q2", [P, NH, 2, HEAD_DIM])
            k2 = mb("k2", [P, NKV, 2, 2, HEAD_DIM])
            qT = mb("qT", [P, NH, P], F32R)
            kT = mb("kT", [P, NKV, 2, 2, P], F32R)
            vv = mb("vv", [P, 4, NKV, 2, 2, HEAD_DIM], F32R)
            pr = mb("probs", [P, NKV, G, 2 * P])
            pTh = mb("pT_hi", [P, 2, G, P], F32R)
            pTl = mb("pT_lo", [P, 2, G, P], F32R)
            usb = mb("u_rows", [P, 2, PW])
            pooledT = mb("pooledT", [P, PW])
            poolw = mb("pool_w", [P, NP, P])
            bandc = mb("band_cur", [P, NP, P])
            bandp = mb("band_prev", [P, NP, P])
            maskr = mb("maskr", [P, 3 * P], F32R)
            gqk = mb("gqk", [P, 2, HEAD_DIM])
            trig = mb("trig", [P, NT, 4, HALF])
            rot = mb("rot", [P, 2, NHN, 2, HALF])
            junk = pooledT[:, :].bitcast(BF16)

        with ExitStack() as out_ctx:
            def ob(name, shape, dt=F32):
                return out_ctx.enter_context(nc.sbuf_tensor(name, shape, dt))
            woh = ob("w_o_hi", [P, KD, D], F32R)
            wol = ob("w_o_lo", [P, KD, D], F32R)
            g1b = ob("g1_rows", [P, D])
            mTh = ob("mixT_hi", [P, KD, P], F32R)
            mTl = ob("mixT_lo", [P, KD, P], F32R)
            hx = ob("hx", [P, D])
        with ExitStack() as mlp_ctx:
            def lb(name, shape, dt=F32):
                return mlp_ctx.enter_context(nc.sbuf_tensor(name, shape, dt))
            w1h = lb("w1_hi", [P, KD, FB], F32R)
            w1l = lb("w1_lo", [P, KD, FB], F32R)
            w2h = lb("w2_hi", [P, NF, D], F32R)
            w2l = lb("w2_lo", [P, NF, D], F32R)
            aTh = lb("aT_hi", [P, NF, S], F32R)
            aTl = lb("aT_lo", [P, NF, S], F32R)
            relu = lb("relu", [P, 2, 512])
            rsq = lb("relu_squared", [P, 2, 512])
        over_w_in = 2 * KD * IN
        sb("w_in_place", [P, over_w_in])
        h2h = sb("h2T_hi", [P, KD, S], F32R)
        h2l = sb("h2T_lo", [P, KD, S], F32R)
        g2b = sb("g2_rows", [P, D])
        junk2 = sb("junk2", [P, D], BF16)

        psum = ctx.enter_context(nc.psum_tensor("psum", [P, 8, 512], F32))

        def bank(j):
            return psum[:, j, :]

        def banks(j):
            return psum[:, j:j + 2, :].rearrange("p b n -> p (b n)")

        stream = []
        for k in range(KD):
            stream += [("sh1", k), ("sc1", k)]
            if k % 2:
                stream.append(("wu", k // 2))
        stream += [("wqkv", k) for k in range(KD)]
        for job in ("sh2", "sc2", "g1"):
            stream += [(job, k) for k in range(KD)]
        stream += [("wo", k) for k in range(KD)]
        for k in range(KD):
            stream += [("x", k), ("g2", k)]
        stream += [("w1", 0), ("w1", 1), ("w2", 0), ("w2", 1)]
        place = {piece: n for n, piece in enumerate(stream)}
        assert (len(stream) - 4) % RING == 0
        MLP_USE = (len(stream) - 4) // RING
        adaln_jobs = ("sh2", "sc2", "g1", "g2")
        mod_of = {"sh1": SH1, "sc1": SC1, "g1": G1, "sh2": SH2, "sc2": SC2, "g2": G2}

        raw_in = [sem(f"raw_in{s}") for s in range(RING)]
        params_in = sem("params_in")
        x_in = [sem("x_in0"), sem("x_in1")]
        out_done = sem("out_done")
        ident_made = sem("ident_made")
        rows_turned = sem("rows_turned")
        cols_ready = sem("cols_ready")
        exp_c = sem("exp_c")
        angles_ready = sem("angles_ready")
        trig_ready = sem("trig_ready")
        consts_made = sem("consts_made")
        poolw_ready = sem("poolw_ready")
        posf_ready = sem("posf_ready")
        mask_ready = sem("mask_ready")
        mod_summed = sem("mod_summed")
        job_summed = sem("job_summed")
        gate_biased = sem("gate_biased")
        mod_turned = sem("mod_turned")
        mod_taken = sem("mod_taken")
        wu_hi, wu_lo = sem("wu_hi"), sem("wu_lo")
        wqkv_hi, wqkv_lo = sem("wqkv_hi"), sem("wqkv_lo")
        wo_gated, wo_hi, wo_lo = sem("wo_gated"), sem("wo_hi"), sem("wo_lo")
        x_squared, x_root, x_scaled = sem("x_squared"), sem("x_root"), sem("x_scaled")
        x_turned, h_made, h_hi, h_lo = sem("x_turned"), sem("h_made"), sem("h_hi"), sem("h_lo")
        u_done, u_kept = sem("u_done"), sem("u_kept")
        band_done, pooled_kept, pout_done, pout_kept = sem("band_done"), sem("pooled_kept"), sem("pout_done"), sem("pout_kept")
        q_done, kv_done = sem("q_done"), sem("kv_done")
        q_squared, kv_squared, qk_sums, qk_root = sem("q_squared"), sem("kv_squared"), sem("qk_sums"), sem("qk_root")
        q_normed, k_normed, qk_gained, qk_roped = sem("q_normed"), sem("k_normed"), sem("qk_gained"), sem("qk_roped")
        qk_hi, qk_lo = sem("qk_hi"), sem("qk_lo")
        v_hi, v_lo = sem("v_hi"), sem("v_lo")
        q_turned, k_turned, qT_kept, kT_kept = sem("q_turned"), sem("k_turned"), sem("qT_kept"), sem("kT_kept")
        scored, max_ready, exped, den_ready, normed = (sem("scored"), sem("max_ready"), sem("exped"),
                                                       sem("den_ready"), sem("normed"))
        p_turned, pT_hi, pT_lo, pv_done, attn_kept = (sem("p_turned"), sem("pT_hi_ready"), sem("pT_lo_ready"),
                                                      sem("pv_done"), sem("attn_kept"))
        mix_hi, mix_lo = sem("mix_hi"), sem("mix_lo")
        wo_used = sem("wo_used")
        x2_ready, x2_squared, x2_root, x2_scaled = sem("x2_ready"), sem("x2_squared"), sem("x2_root"), sem("x2_scaled")
        x2_turned, h2_made, h2_hi, h2_lo = sem("x2_turned"), sem("h2_made"), sem("h2_hi"), sem("h2_lo")
        w1_hi, w1_lo = sem("w1_hi_ready"), sem("w1_lo_ready")
        w2_gated, w2_hi, w2_lo = sem("w2_gated"), sem("w2_hi_ready"), sem("w2_lo_ready")
        up_done, relu_kept, act_hi, act_sq, act_lo = (sem("up_done"), sem("relu_kept"), sem("act_hi"), sem("act_sq"),
                                                      sem("act_lo"))
        down_done, added = sem("down_done"), sem("added")
        own = {e: sem(f"own_{e}") for e in ("act", "dve", "pool")}

        block = ctx.enter_context(nc.Block())

        class Chain:

            def __init__(self, eng, s, base=0):
                self.eng, self.s, self.n, self.base = eng, s, 0, base

            def step(self, ins):
                ins.then_inc(self.s, 1)
                self.n += 1

            def wait(self):
                self.eng.wait_ge(self.s, self.base + self.n)

        def landed(eng, piece):
            n = place[piece]
            eng.wait_ge(raw_in[n % RING], 16 * (n // RING + 1))
            return raw[:, n % RING, :]

        def freed(eng, n):
            if n < RING:
                return
            kind, k = stream[n - RING]
            if kind in ("sh1", "sc1"):
                eng.wait_ge(mod_summed, 2 * k + 1 + (kind == "sc1"))
            elif kind in adaln_jobs:
                eng.wait_ge(job_summed, KD * adaln_jobs.index(kind) + k + 1)
            elif kind == "x":
                eng.wait_ge(x2_ready, k + 1)
            else:
                eng.wait_ge({"wu": wu_lo, "wqkv": wqkv_lo, "wo": wo_lo}[kind], k + 1)

        def source(kind, k):
            if kind == "wu":
                return win[:, 2 * k:2 * k + 2, QKV:IN]
            if kind == "wqkv":
                return win[:, k, 0:QKV]
            if kind == "wo":
                return wo[:, k, :]
            if kind == "x":
                return x_rows[k * P:(k + 1) * P, :]
            if kind == "w1":
                return w1[:, 4 * k:4 * k + 4, 0:FB]
            if kind == "w2":
                return w2[k * P:(k + 1) * P, :]
            m = mod_of[kind]
            return wada[:, k, m * D:(m + 1) * D]

        def target(kind, slot):
            a = raw[:, slot, :]
            if kind == "wu":
                return a.rearrange("p (k n) -> p k n", k=2)
            if kind == "wqkv":
                return a[:, 0:QKV]
            if kind == "w1":
                return a.rearrange("p (k n) -> p k n", k=4)
            return a

        @block.sync
        def _(sp):
            def load(n):
                kind, k = stream[n]
                freed(sp, n)
                sp.dma_start(target(kind, n % RING), source(kind, k)).then_inc(raw_in[n % RING], 16)

            def load_x(t):
                if t >= 2:
                    sp.wait_ge(h_lo, t - 1)
                sp.dma_start(xh[:, t % 2, :], x_rows[t * P:(t + 1) * P, :]).then_inc(x_in[t % 2], 16)

            first_job = place[("sh2", 0)]
            for n in range(first_job):
                load(n)
                if n == 10:
                    load_x(0)
            for t in range(NT):
                if t + 1 < NT:
                    load_x(t + 1)
                if t < 6:
                    for j in range(4):
                        load(first_job + 4 * t + j)
            for n in range(place[("wo", 0)], len(stream)):
                load(n)
            with sp.Fori(1, NB) as b:
                for j in range(2):
                    sp.wait_ge(w1_lo, 2 * b + j - 1)
                    sp.dma_start(target("w1", j), w1[:, 4 * j:4 * j + 4, bass.ds(b * FB, FB)]).then_inc(raw_in[j], 16)
                for j in range(2):
                    sp.wait_ge(w2_lo, 2 * b + j - 1)
                    sp.dma_start(target("w2", 2 + j), w2[bass.ds(b * FB + j * P, P), :]).then_inc(raw_in[2 + j], 16)
            for i in range(NT):
                sp.wait_ge(added, 16 * (NB - 1) + 2 * i + 2)
                sp.dma_start(out_rows[i * P:(i + 1) * P, :], slots[:, i, :]).then_inc(out_done, 16)
            sp.wait_ge(out_done, 16 * NT)

        rows = pr[:, 0, :, :].rearrange("p h n -> p (h n)")[:, 0:P]
        posi = pr[:, 1, :, :].rearrange("p h n -> p (h n)")[:, 0:P].bitcast(I32)
        scale_row = pr[:, 1, :, :].rearrange("p h n -> p (h n)")[:, 512:1024]
        cin = small[:, 192:200]
        acc_sc = q2[:, :, :, :].rearrange("p h a d -> p (h a d)")
        ang = qkn[:, :, :].rearrange("p h d -> p (h d)")[:, 2 * P:]
        ANG = NT * HALF

        @block.scalar
        def _(act):
            own_a = Chain(act, own["act"])
            act.dma_start(cin, c[0].rearrange("(p k) -> p k", k=KD)).then_inc(params_in, 16)
            act.dma_start(rows[0:48, :], b_ada[0].rearrange("(j p) -> j p", p=P)).then_inc(params_in, 16)
            act.dma_start(rows[48:56, :], norm1_g[0].rearrange("(j p) -> j p", p=P)).then_inc(params_in, 16)
            act.dma_start(rows[56:64, :], norm2_g[0].rearrange("(j p) -> j p", p=P)).then_inc(params_in, 16)
            act.dma_start(posi[64:72, :], positions[0].rearrange("(j p) -> j p", p=P)).then_inc(params_in, 16)
            act.dma_start(scale_row, pool_scale.to_broadcast([P, PW])).then_inc(params_in, 16)
            act.dma_start(poolw[:, :, :], pool_w[0].rearrange("g c d -> c g d")).then_inc(params_in, 16)
            act.dma_start(gqk[:, 0, :], q_norm_g.to_broadcast([P, HEAD_DIM])).then_inc(params_in, 16)
            act.dma_start(gqk[:, 1, :], k_norm_g.to_broadcast([P, HEAD_DIM])).then_inc(params_in, 16)
            act.dma_start(sink, attn_sinks.to_broadcast([P, NH])).then_inc(params_in, 16)
            act.wait_ge(params_in, 160)
            nc.scalar.activation(ctmp, cin, ACT.Exp, scale=-1.0).then_inc(exp_c, 1)
            act.wait_ge(angles_ready, 1)
            nc.scalar.activation(trig[:, :, 1, :], ang[:, 0:ANG].rearrange("p (t f) -> p t f", f=HALF),
                                 ACT.Sin).then_inc(trig_ready, 1)
            nc.scalar.activation(trig[:, :, 2, :], ang[:, 0:ANG].rearrange("p (t f) -> p t f", f=HALF),
                                 ACT.Sin).then_inc(trig_ready, 1)
            nc.scalar.activation(trig[:, :, 0, :], ang[:, ANG:2 * ANG].rearrange("p (t f) -> p t f", f=HALF),
                                 ACT.Sin).then_inc(trig_ready, 1)
            nc.scalar.activation(trig[:, :, 3, :], ang[:, ANG:2 * ANG].rearrange("p (t f) -> p t f", f=HALF),
                                 ACT.Sin).then_inc(trig_ready, 1)

            def square_x(t):
                act.wait_ge(x_in[t % 2], 16 * (t // 2 + 1))
                if t >= 1:
                    act.wait_ge(x_squared, t)
                nc.scalar.activation(junk, xh[:, t % 2, :], ACT.Square,
                                     accum_out=ssx[:, t:t + 1]).then_inc(x_squared, 1)

            def scale_x(t):
                act.wait_ge(x_root, t + 1)
                nc.scalar.activation(xh[:, t % 2, :], xh[:, t % 2, :], ACT.Copy,
                                     scale=rx[:, t:t + 1]).then_inc(x_scaled, 1)

            def hi_h(t):
                act.wait_ge(h_made, t + 1)
                if t >= 1:
                    act.wait_ge(kv_done, t)
                nc.scalar.copy(hTh[:, :, :], xh[:, t % 2, :].rearrange("p (k n) -> p k n", n=P)).then_inc(h_hi, 1)

            for j in range(KD // 2):
                a = landed(act, ("wu", j))
                nc.scalar.copy(wih[:, 2 * j:2 * j + 2, QKV:IN], a.rearrange("p (k n) -> p k n", k=2)).then_inc(wu_hi, 1)
                if j == 2:
                    square_x(0)
            scale_x(0)
            hi_h(0)
            for k in range(KD):
                a = landed(act, ("wqkv", k))
                nc.scalar.copy(wih[:, k, 0:QKV], a[:, 0:QKV]).then_inc(wqkv_hi, 1)

            def hi_pT(i, kv):
                act.wait_ge(p_turned, 2 * i + kv + 1)
                if 2 * i + kv >= 1:
                    act.wait_ge(pv_done, 2 * i + kv)
                nb = 1 if i == 0 else 2
                nc.scalar.copy(pTh[:, 0:nb, :, :].rearrange("p b h q -> p b (h q)"),
                               psum[:, 4:4 + nb, :]).then_inc(pT_hi, 1)

            def keep_attn(i, kv):
                act.wait_ge(pv_done, 2 * i + kv + 1)
                o = bank(0).rearrange("p (m e q) -> p m e q", e=2, q=P)
                dst = slots[:, i, :].rearrange("p (m q) -> p m q", q=P)
                for e in range(2):
                    r = slice(64 * e, 64 * e + 64)
                    ins = nc.scalar.copy(dst[r, 2 * kv:2 * kv + 2, :], o[r, :, e, :])
                ins.then_inc(attn_kept, 1)

            def exps(i, kv):
                act.wait_ge(max_ready, 2 * i + kv + 1)
                if i >= 1:
                    act.wait_ge(p_turned, 2 * (i - 1) + kv + 1)
                w = P if i == 0 else 2 * P
                for h in range(G):
                    hh = kv * G + h
                    nc.scalar.activation(pr[:, kv, h, 0:w], psum[:, 4 + h // 2, (h % 2) * 256:(h % 2) * 256 + w], ACT.Exp,
                                         bias=negm[:, hh:hh + 1], scale=SCALE, accum_out=den[:, hh:hh + 1])
                nc.scalar.activation(es[:, kv * G:kv * G + G], earg[:, kv * G:kv * G + G], ACT.Exp).then_inc(exped, 1)

            for t in range(NT + 2):
                if t < NT:
                    act.wait_ge(u_done, t + 1)
                    if t >= 2:
                        act.wait_ge(band_done, t)
                    nc.scalar.copy(usb[:, t % 2, :], bank(0)).then_inc(u_kept, 1)
                if 1 <= t <= NT:
                    act.wait_ge(pout_done, t)
                    nc.scalar.copy(slots[:, t - 1, D - PW:D], bank(7)).then_inc(pout_kept, 1)
                if t + 1 < NT:
                    square_x(t + 1)
                    scale_x(t + 1)
                if 1 <= t <= NT:
                    act.wait_ge(q_turned, t)
                    if t >= 2:
                        act.wait_ge(scored, 2 * (t - 1))
                    nc.scalar.copy(qT[:, :, :].rearrange("p h q -> p (h q)"), banks(1)).then_inc(qT_kept, 1)
                if t >= 2:
                    hi_pT(t - 2, 0)
                if t < NT:
                    act.wait_ge(q_done, t + 1)
                    if t >= 1:
                        act.wait_ge(q_turned, t)
                    sq = q2[:, :, :, :].rearrange("p h a d -> p (h a d)")
                    nc.scalar.activation(sq[:, 0:AW], bank(6), ACT.Square).then_inc(q_squared, 1)
                if t >= 2:
                    keep_attn(t - 2, 0)
                    hi_pT(t - 2, 1)
                if t < NT:
                    act.wait_ge(kv_done, t + 1)
                    nc.scalar.activation(sq[:, AW:AW + KVW], psum[:, 3, 0:KVW], ACT.Square).then_inc(kv_squared, 1)
                    if t >= 4:
                        act.wait_ge(pv_done, 2 * (t - 2))
                    nc.scalar.copy(vv[:, t % 4, :, 0, :, :],
                                   bcast(psum[:, 3, KVW:2 * KVW].rearrange("p (g d) -> p g d", g=NKV), 2, 2)).then_inc(v_hi, 1)
                if t + 1 < NT:
                    hi_h(t + 1)
                if 1 <= t <= NT:
                    exps(t - 1, 0)
                if t >= 2:
                    keep_attn(t - 2, 1)
                if t < NT:
                    act.wait_ge(band_done, t + 1)
                    act.wait_ge(x_squared, min(t + 2, NT))
                    nc.scalar.copy(pooledT[:, :], bank(7)).then_inc(pooled_kept, 1)
                if 1 <= t <= NT:
                    exps(t - 1, 1)
                if t < NT:
                    act.wait_ge(qk_roped, t + 1)
                    nc.scalar.copy(q2[:, :, 0, :].bitcast(F32R), qkn[:, 0:NH, :])
                    if t >= 1:
                        act.wait_ge(k_turned, t)
                    nc.scalar.copy(k2[:, :, 0, :, :].bitcast(F32R), bcast(qkn[:, NH:NHN, :], 2, 2)).then_inc(qk_hi, 1)
                if t == NT:
                    for k in range(KD):
                        act.wait_ge(wo_gated, k + 1)
                        nc.scalar.copy(woh[:, k, :], raw[:, place[("wo", k)] % RING, :]).then_inc(wo_hi, 1)

            def hi_mix(i):
                for h in range(2):
                    if i >= 1:
                        act.wait_ge(wo_used, 2 * (i - 1) + h + 1)
                    elif h == 0:
                        act.wait_ge(attn_kept, 2 * NT)
                        act.wait_ge(pout_kept, NT)
                    nc.scalar.copy(mTh[:, 4 * h:4 * h + 4, :],
                                   slots[:, i, 512 * h:512 * h + 512].rearrange("p (k n) -> p k n", n=P)).then_inc(mix_hi, 1)

            def norm_x2(i):
                act.wait_ge(x2_ready, i + 1)
                if i >= 1:
                    act.wait_ge(x2_squared, i)
                nc.scalar.activation(junk2[:, :], slots[:, i, :], ACT.Square,
                                     accum_out=ss2[:, i:i + 1]).then_inc(x2_squared, 1)
                act.wait_ge(x2_root, i + 1)
                if i >= 1:
                    act.wait_ge(h2_lo, i)
                nc.scalar.activation(hx[:, :], slots[:, i, :], ACT.Copy, scale=r2[:, i:i + 1]).then_inc(x2_scaled, 1)

            def hi_h2(i):
                act.wait_ge(h2_made, i + 1)
                nc.scalar.copy(h2h[:, :, i * P:(i + 1) * P], hx[:, :].rearrange("p (k n) -> p k n", n=P)).then_inc(h2_hi, 1)

            hi_mix(0)
            for i in range(NT):
                if i + 1 < NT:
                    hi_mix(i + 1)
                if i >= 1:
                    hi_h2(i - 1)
                norm_x2(i)
            hi_h2(NT - 1)

            def hi_w1(b, use):
                for j in range(2):
                    act.wait_ge(raw_in[j], 16 * use)
                    nc.scalar.copy(w1h[:, 4 * j:4 * j + 4, :], raw[:, j, :].rearrange("p (k n) -> p k n", k=4)).then_inc(w1_hi, 1)

            def mlp_block(b, last):
                if not (isinstance(b, int) and b == 0):
                    act.wait_ge(down_done, 2 * NT * b)
                for j in range(2):
                    act.wait_ge(w2_gated, 2 * b + j + 1)
                    nc.scalar.copy(w2h[:, j, :], raw[:, 2 + j, :]).then_inc(w2_hi, 1)
                for u in range(2 * NF):
                    act.wait_ge(up_done, 2 * NF * b + u + 1)
                    relu_slot_free(act, b, u)
                    nc.scalar.activation(relu[:, u % 2, :], bank(u), ACT.Relu).then_inc(relu_kept, 1)
                    act.wait_ge(relu_kept, 2 * NF * b + u + 1)
                    nc.scalar.activation(aTh[:, u % NF, (u // NF) * 512:(u // NF) * 512 + 512], relu[:, u % 2, :],
                                         ACT.Square).then_inc(act_hi, 1)
                if not last:
                    act.wait_ge(up_done, 2 * NF * b + 2 * NF)
                    hi_w1(b + 1, MLP_USE + 2 + b)

            def relu_slot_free(eng, b, u):
                if isinstance(b, int) and 2 * NF * b + u - 2 < 0:
                    return
                eng.wait_ge(act_sq, 2 * NF * b + u - 1)

            act.wait_ge(wo_used, 2 * NT)
            act.wait_ge(h2_lo, NT)
            hi_w1(0, MLP_USE + 1)
            mlp_block(0, False)
            with act.Fori(1, NB - 1) as b:
                mlp_block(b, False)
            mlp_block(NB - 1, True)

        @block.vector
        def _(dve):
            own_d = Chain(dve, own["dve"])
            v = nc.vector
            v.memset(ones[:, :], 1.0).then_inc(ident_made, 1)
            dve.wait_ge(params_in, 160)
            v.tensor_copy(rows[64:72, :], posi[64:72, :]).then_inc(posf_ready, 1)
            dve.wait_ge(exp_c, 1)
            own_d.step(v.tensor_scalar(ctmp, ctmp, 1.0, None, ALU.add))
            own_d.wait()
            own_d.step(v.reciprocal(ctmp, ctmp))
            own_d.wait()
            own_d.step(v.tensor_tensor(silu, cin, ctmp, ALU.mult))
            own_d.step(v.tensor_scalar(nsink, sink, -1.0, None, ALU.mult))
            v.tensor_tensor(poolw[:, :, :].rearrange("p g d -> p (g d)"), poolw[:, :, :].rearrange("p g d -> p (g d)"),
                            scale_row, ALU.mult).then_inc(poolw_ready, 1)
            own_d.wait()

            def add_piece(target_acc, piece, k, done):
                a = landed(dve, piece)
                if k == 0:
                    v.tensor_scalar(target_acc, a, silu[:, 0:1], None, ALU.mult).then_inc(done, 1)
                else:
                    v.scalar_tensor_tensor(out=target_acc, in0=a, scalar=silu[:, k:k + 1], in1=target_acc,
                                           op0=ALU.mult, op1=ALU.add).then_inc(done, 1)

            def angles():
                dve.wait_ge(rows_turned, 1)
                v.tensor_copy(cols[:, :], psum[:, 4, 0:72]).then_inc(cols_ready, 1)
                dve.wait_ge(cols_ready, 1)
                a0, a1_, a2_ = (ang[:, j * ANG:(j + 1) * ANG] for j in range(3))
                a3 = ang[:, 3 * ANG:4 * ANG]
                inv = (np.float32(ROPE_THETA) ** (-np.arange(0, ROT_DIM, 2, dtype=np.float32) / np.float32(ROT_DIM)))
                for f in range(HALF):
                    ins = v.tensor_scalar(a0.rearrange("p (t f) -> p t f", f=HALF)[:, :, f], cols[:, 64:72],
                                          float(inv[f]), None, ALU.mult)
                own_d.step(ins)
                own_d.wait()
                own_d.step(v.tensor_scalar(a1_, a0, float(1 / (2 * np.pi)), ROUND_MAGIC, ALU.mult, ALU.add))
                own_d.wait()
                own_d.step(v.tensor_scalar(a2_, a1_, -ROUND_MAGIC, None, ALU.add))
                own_d.wait()
                for part in (TWO_PI_1, TWO_PI_2, TWO_PI_3):
                    own_d.step(v.scalar_tensor_tensor(out=a0, in0=a2_, scalar=-part, in1=a0, op0=ALU.mult, op1=ALU.add))
                    own_d.wait()
                own_d.step(v.tensor_scalar(a0, a0, PI_LIMIT, -PI_LIMIT, ALU.min, ALU.max))
                own_d.wait()
                own_d.step(v.tensor_scalar(a3, a0, -1.0, None, ALU.mult))
                own_d.wait()
                own_d.step(v.tensor_tensor(a3, a3, a0, ALU.max))
                own_d.wait()
                v.tensor_scalar(a1_, a3, -1.0, float(np.pi / 2), ALU.mult, ALU.add).then_inc(angles_ready, 1)

            for k in range(KD):
                if k >= 1:
                    dve.wait_ge(mod_summed, 2 * k - 1)
                add_piece(acc[:, :], ("sh1", k), k, mod_summed)
                if k >= 1:
                    dve.wait_ge(mod_summed, 2 * k)
                add_piece(acc_sc, ("sc1", k), k, mod_summed)
                if k == 1:
                    angles()
            dve.wait_ge(mod_turned, 1)
            own_d.step(v.tensor_reduce(b1, banks(0).rearrange("p (k n) -> p k n", n=P), AX_X, ALU.add))
            v.tensor_reduce(a1, banks(2).rearrange("p (k n) -> p k n", n=P), AX_X, ALU.add).then_inc(mod_taken, 1)
            own_d.wait()
            own_d.step(v.tensor_tensor(b1, b1, cols[:, 8 * SH1:8 * SH1 + 8], ALU.add))
            dve.wait_ge(mod_taken, 1)
            own_d.step(v.tensor_tensor(a1, a1, cols[:, 8 * SC1:8 * SC1 + 8], ALU.add))
            own_d.wait()
            own_d.step(v.scalar_tensor_tensor(out=a1, in0=a1, scalar=1.0, in1=cols[:, 48:56], op0=ALU.add, op1=ALU.mult))
            own_d.wait()

            def make_h(t):
                dve.wait_ge(x_turned, t + 1)
                for k in range(KD):
                    ins = v.tensor_scalar(xh[:, t % 2, k * P:(k + 1) * P], banks(1)[:, k * P:(k + 1) * P],
                                          a1[:, k:k + 1], b1[:, k:k + 1], ALU.mult, ALU.add)
                ins.then_inc(h_made, 1)

            make_h(0)
            for k in range(KD):
                a = landed(dve, ("wqkv", k))
                dve.wait_ge(wqkv_hi, k + 1)
                v.tensor_tensor(wil[:, k, 0:QKV], a[:, 0:QKV], wih[:, k, 0:QKV].bitcast(F32), ALU.subtract).then_inc(wqkv_lo, 1)

            def lo_pT(i, kv):
                dve.wait_ge(pT_hi, 2 * i + kv + 1)
                nb = 1 if i == 0 else 2
                v.tensor_tensor(pTl[:, 0:nb, :, :].rearrange("p b h q -> p b (h q)"), psum[:, 4:4 + nb, :],
                                pTh[:, 0:nb, :, :].rearrange("p b h q -> p b (h q)").bitcast(F32),
                                ALU.subtract).then_inc(pT_lo, 1)

            def maxes(i, kv):
                dve.wait_ge(scored, 2 * i + kv + 1)
                w = P if i == 0 else 2 * P
                g = slice(kv * G, kv * G + G)
                own_d.step(v.tensor_reduce(mx[:, g], banks(4).rearrange("p (h n) -> p h n", h=G)[:, :, 0:w], AX_X, ALU.max))
                own_d.wait()
                own_d.step(v.scalar_tensor_tensor(out=negm[:, g], in0=mx[:, g], scalar=-SCALE, in1=nsink[:, g],
                                                  op0=ALU.mult, op1=ALU.min))
                own_d.wait()
                v.tensor_tensor(earg[:, g], sink[:, g], negm[:, g], ALU.add).then_inc(max_ready, 1)

            def dens(i, kv):
                g = slice(kv * G, kv * G + G)
                dve.wait_ge(exped, 2 * i + kv + 1)
                own_d.step(v.tensor_tensor(den[:, g], den[:, g], es[:, g], ALU.add))
                own_d.wait()
                if i >= 1:
                    dve.wait_ge(normed, 2 * (i - 1) + kv + 1)
                v.reciprocal(rden[:, g], den[:, g]).then_inc(den_ready, 1)

            for t in range(NT + 2):
                if 1 <= t <= NT:
                    dve.wait_ge(k_turned, t)
                    if t >= 2:
                        dve.wait_ge(scored, 2 * (t - 1))
                    v.tensor_copy(kT[:, :, :, (t - 1) % 2, :],
                                  bank(3).rearrange("p (g a n) -> p g a n", g=NKV, a=2)).then_inc(kT_kept, 1)
                if t >= 2:
                    lo_pT(t - 2, 0)
                    lo_pT(t - 2, 1)
                if t in (2, 4):
                    dst, m = (b2, SH2) if t == 2 else (a2, SC2)
                    dve.wait_ge(mod_turned, t // 2 + 1)
                    v.tensor_reduce(dst, banks(1).rearrange("p (k n) -> p k n", n=P), AX_X, ALU.add).then_inc(mod_taken, 1)
                    dve.wait_ge(mod_taken, t // 2 + 1)
                    own_d.step(v.tensor_tensor(dst, dst, cols[:, 8 * m:8 * m + 8], ALU.add))
                    own_d.wait()
                    if t == 4:
                        own_d.step(v.scalar_tensor_tensor(out=a2, in0=a2, scalar=1.0, in1=cols[:, 56:64],
                                                          op0=ALU.add, op1=ALU.mult))
                        own_d.wait()
                if t + 1 < NT:
                    make_h(t + 1)
                if t == NT:
                    dve.wait_ge(mod_turned, 4)
                    v.tensor_copy(g1b[:, :], banks(6)).then_inc(mod_taken, 1)
                    dve.wait_ge(mod_taken, 4)
                if 1 <= t <= NT:
                    maxes(t - 1, 0)
                if t < NT:
                    dve.wait_ge(q_squared, t + 1)
                    dve.wait_ge(kv_squared, t + 1)
                    v.tensor_reduce(ssq, q2[:, :, :, :].rearrange("p h a d -> p (h a d)")[:, 0:AW + KVW]
                                    .rearrange("p (h d) -> p h d", d=HEAD_DIM), AX_X, ALU.add).then_inc(qk_sums, 1)
                    dve.wait_ge(qk_root, t + 1)
                    if t >= 1:
                        dve.wait_ge(qk_lo, t)
                    v.tensor_tensor(qkn[:, 0:NH, :], bank(6).rearrange("p (h d) -> p h d", d=HEAD_DIM),
                                    bcast(rq[:, 0:NH], 2, HEAD_DIM), ALU.mult).then_inc(q_normed, 1)
                    dve.wait_ge(v_hi, t + 1)
                    v.tensor_tensor(qkn[:, NH:NHN, :], psum[:, 3, 0:KVW].rearrange("p (h d) -> p h d", d=HEAD_DIM),
                                    bcast(rq[:, NH:NHN], 2, HEAD_DIM), ALU.mult).then_inc(k_normed, 1)
                    v.tensor_tensor(vv[:, t % 4, :, 1, :, :],
                                    bcast(psum[:, 3, KVW:2 * KVW].rearrange("p (g d) -> p g d", g=NKV), 2, 2),
                                    vv[:, t % 4, :, 0, :, :].bitcast(F32), ALU.subtract).then_inc(v_lo, 1)
                if 1 <= t <= NT:
                    dens(t - 1, 0)
                    maxes(t - 1, 1)
                    dens(t - 1, 1)
                if t < 6:
                    for j in range(4):
                        n = 4 * t + j
                        if n >= 1:
                            dve.wait_ge(job_summed, n)
                        if n in (8, 16):
                            dve.wait_ge(mod_turned, n // 8 + 1)
                        add_piece(acc[:, :], (adaln_jobs[n // 8], n % 8), n % 8, job_summed)
                if t == 5:
                    for k in range(KD):
                        dve.wait_ge(job_summed, 24)
                        ins = v.scalar_tensor_tensor(out=acc[:, k * P:(k + 1) * P], in0=ident[:, :],
                                                     scalar=cols[:, 8 * G1 + k:8 * G1 + k + 1],
                                                     in1=acc[:, k * P:(k + 1) * P], op0=ALU.mult, op1=ALU.add)
                    ins.then_inc(gate_biased, 1)
                if t == NT:
                    for k in range(KD):
                        a = landed(dve, ("wo", k))
                        v.tensor_tensor(a, a, g1b[:, :], ALU.mult).then_inc(wo_gated, 1)

            def lo_mix(i):
                for h in range(2):
                    dve.wait_ge(mix_hi, 2 * i + h + 1)
                    v.tensor_tensor(mTl[:, 4 * h:4 * h + 4, :],
                                    slots[:, i, 512 * h:512 * h + 512].rearrange("p (k n) -> p k n", n=P),
                                    mTh[:, 4 * h:4 * h + 4, :].bitcast(F32), ALU.subtract).then_inc(mix_lo, 1)

            def make_h2(i):
                dve.wait_ge(x2_turned, i + 1)
                for k in range(KD):
                    ins = v.tensor_scalar(hx[:, k * P:(k + 1) * P], banks(4)[:, k * P:(k + 1) * P],
                                          a2[:, k:k + 1], b2[:, k:k + 1], ALU.mult, ALU.add)
                ins.then_inc(h2_made, 1)

            lo_mix(0)
            for i in range(NT):
                if i + 1 < NT:
                    lo_mix(i + 1)
                if i >= 1:
                    make_h2(i - 1)
                a = landed(dve, ("x", i))
                dve.wait_ge(wo_used, 2 * i + 2)
                v.tensor_tensor(slots[:, i, :], banks(2 * (i % 2)), a, ALU.add).then_inc(x2_ready, 1)
                if i == 0:
                    dve.wait_ge(mod_turned, 4)
                else:
                    dve.wait_ge(job_summed, 24 + i)
                add_piece(acc[:, :], ("g2", i), i, job_summed)
            for k in range(KD):
                dve.wait_ge(job_summed, 32)
                ins = v.scalar_tensor_tensor(out=acc[:, k * P:(k + 1) * P], in0=ident[:, :],
                                             scalar=cols[:, 8 * G2 + k:8 * G2 + k + 1],
                                             in1=acc[:, k * P:(k + 1) * P], op0=ALU.mult, op1=ALU.add)
            ins.then_inc(gate_biased, 1)
            make_h2(NT - 1)
            dve.wait_ge(mod_turned, 5)
            v.tensor_copy(g2b[:, :], banks(6)).then_inc(mod_taken, 1)

            def mlp_block(b):
                for u in range(2 * NF):
                    dve.wait_ge(relu_kept, 2 * NF * b + u + 1)
                    v.tensor_tensor(rsq[:, u % 2, :], relu[:, u % 2, :], relu[:, u % 2, :], ALU.mult).then_inc(act_sq, 1)
                    dve.wait_ge(act_sq, 2 * NF * b + u + 1)
                    dve.wait_ge(act_hi, 2 * NF * b + u + 1)
                    cut = slice((u // NF) * 512, (u // NF) * 512 + 512)
                    v.tensor_tensor(aTl[:, u % NF, cut], rsq[:, u % 2, :], aTh[:, u % NF, cut].bitcast(F32),
                                    ALU.subtract).then_inc(act_lo, 1)
                for n in range(2 * NT):
                    dve.wait_ge(down_done, 2 * NT * b + n + 1)
                    o = slots[:, n // 2, (n % 2) * 512:(n % 2) * 512 + 512]
                    v.tensor_tensor(o, bank(4 + n % 4), o, ALU.add).then_inc(added, 1)

            with dve.Fori(0, NB) as b:
                mlp_block(b)

        @block.gpsimd
        def _(pool):
            own_p = Chain(pool, own["pool"])
            g = nc.gpsimd
            own_p.step(g.memset(ident[:, :], 0.0))
            own_p.wait()
            g.affine_select(out=ident[:, :], in_=ident[:, :], compare_op=ALU.not_equal, fill=1.0, base=0,
                            pattern=[[-1, P]], channel_multiplier=1).then_inc(ident_made, 1)
            own_p.step(g.memset(mhalf, -0.5))
            pool.wait_ge(ident_made, 2)
            own_p.step(g.tensor_copy(identr[:, :], ident[:, :]))
            m = qkn[:, :, :].rearrange("p h d -> p (h d)")[:, 0:2 * P]
            own_p.step(g.memset(m, 0.0))
            own_p.wait()
            own_p.step(g.affine_select(out=m[:, 0:P], in_=m[:, 0:P], compare_op=ALU.is_gt, fill=MASKED, base=0,
                                       pattern=[[1, P]], channel_multiplier=-1))
            own_p.step(g.affine_select(out=m[:, P:2 * P], in_=m[:, P:2 * P], compare_op=ALU.is_ge, fill=MASKED, base=0,
                                       pattern=[[-1, P]], channel_multiplier=1))
            own_p.wait()
            g.tensor_copy(maskr[:, 0:2 * P], m[:, 0:2 * P]).then_inc(mask_ready, 1)
            g.tensor_copy(maskr[:, 2 * P:3 * P], m[:, 0:P]).then_inc(mask_ready, 1)

            def band_of(i, cut, base):
                w = POOL_WINDOWS[i]
                own_p.step(g.affine_select(out=cut, in_=cut, compare_op=ALU.is_ge, fill=0.0, base=base,
                                           pattern=[[1, P]], channel_multiplier=-1))
                own_p.wait()
                own_p.step(g.affine_select(out=cut, in_=cut, compare_op=ALU.is_ge, fill=0.0, base=w - 1 - base,
                                           pattern=[[-1, P]], channel_multiplier=1))
                own_p.wait()

            def less_token(i):
                own_p.step(g.tensor_tensor(bandc[:, i, :], bandc[:, i, :], ident[:, :], ALU.subtract))
                own_p.wait()

            own_p.step(g.memset(bandp[:, :, :], 0.0))
            for i, w in enumerate(POOL_WINDOWS):
                own_p.step(g.memset(bandc[:, i, :], 1.0 / w))
            own_p.wait()
            for i, w in enumerate(POOL_WINDOWS):
                for s in range(w - 1):
                    own_p.step(g.memset(bandc[:, i, s:s + 1], float(np.float32(1.0) / np.float32(s + 1))))
                own_p.wait()
                band_of(i, bandc[:, i, :], 0)
                less_token(i)
                own_p.step(g.memset(bandp[:, i, :], 1.0 / w))
                own_p.wait()
                band_of(i, bandp[:, i, :], P)
            own_p.step(g.tensor_copy(small[:, 200:201], small[:, 164:165]))
            pool.wait_ge(own["pool"], own_p.n)
            g.tensor_copy(small[:, 201:202], small[:, 164:165]).then_inc(consts_made, 1)

            for j in range(KD // 2):
                a = landed(pool, ("wu", j))
                pool.wait_ge(wu_hi, j + 1)
                g.tensor_tensor(wil[:, 2 * j:2 * j + 2, QKV:IN], a.rearrange("p (k n) -> p k n", k=2),
                                wih[:, 2 * j:2 * j + 2, QKV:IN].bitcast(F32), ALU.subtract).then_inc(wu_lo, 1)

            def root(dst, src, n, done):
                own_p.step(g.tensor_scalar(dst, src, 1.0 / n, EPS, ALU.mult, ALU.add))
                own_p.wait()
                g.tensor_tensor(dst, dst, mhalf[:, 0:dst.shape[1]], ALU.pow).then_inc(done, 1)

            def root_x(t):
                pool.wait_ge(x_squared, t + 1)
                root(rx[:, t:t + 1], ssx[:, t:t + 1], D, x_root)

            def lo_h(t):
                pool.wait_ge(h_hi, t + 1)
                g.tensor_tensor(hTl[:, :, :], xh[:, t % 2, :].rearrange("p (k n) -> p k n", n=P),
                                hTh[:, :, :].bitcast(F32), ALU.subtract).then_inc(h_lo, 1)

            def normalise(i, kv):
                pool.wait_ge(den_ready, 2 * i + kv + 1)
                w = P if i == 0 else 2 * P
                r = slice(kv * G, kv * G + G)
                g.tensor_tensor(pr[:, kv, :, 0:w], pr[:, kv, :, 0:w], bcast(rden[:, r], 2, w), ALU.mult).then_inc(normed, 1)

            root_x(0)
            lo_h(0)
            for t in range(NT + 2):
                if t + 1 < NT:
                    root_x(t + 1)
                    lo_h(t + 1)
                if t < NT:
                    pool.wait_ge(qk_sums, t + 1)
                    if t >= 1:
                        pool.wait_ge(k_normed, t)
                    root(rq, ssq, HEAD_DIM, qk_root)
                if 1 <= t <= NT:
                    normalise(t - 1, 0)
                if t < NT:
                    pool.wait_ge(k_normed, t + 1)
                    own_p.step(g.tensor_tensor(qkn[:, 0:NH, :], qkn[:, 0:NH, :], bcast(gqk[:, 0, :], 1, NH), ALU.mult))
                    own_p.step(g.tensor_tensor(qkn[:, NH:NHN, :], qkn[:, NH:NHN, :], bcast(gqk[:, 1, :], 1, NKV), ALU.mult))
                    own_p.wait()
                    if t == 0:
                        pool.wait_ge(trig_ready, 4)
                    part = qkn[:, :, 0:ROT_DIM].rearrange("p h (a f) -> p h a f", a=2)
                    for j in range(2):
                        own_p.step(g.tensor_tensor(rot[:, j, :, :, :], part, bcast(trig[:, t, 2 * j:2 * j + 2, :], 1, NHN),
                                                   ALU.mult))
                    own_p.wait()
                    own_p.step(g.tensor_tensor(part[:, :, 0, :], rot[:, 0, :, 0, :], rot[:, 0, :, 1, :], ALU.subtract))
                    g.tensor_tensor(part[:, :, 1, :], rot[:, 1, :, 0, :], rot[:, 1, :, 1, :], ALU.add).then_inc(qk_roped, 1)
                if 1 <= t <= NT:
                    normalise(t - 1, 1)
                if t < NT:
                    pool.wait_ge(qk_hi, t + 1)
                    g.tensor_tensor(q2[:, :, 1, :].bitcast(F32R), qkn[:, 0:NH, :], q2[:, :, 0, :], ALU.subtract)
                    for e in range(NKV):
                        ins = g.tensor_tensor(k2[:, e, 1, :, :].bitcast(F32R), bcast(qkn[:, NH + e, :], 1, 2),
                                              k2[:, e, 0, :, :], ALU.subtract)
                    ins.then_inc(qk_lo, 1)
                if t == 0:
                    pool.wait_ge(band_done, 1)
                    for i, w in enumerate(POOL_WINDOWS):
                        own_p.step(g.memset(bandc[:, i, :], 1.0 / w))
                        own_p.wait()
                        band_of(i, bandc[:, i, :], 0)
                        if i + 1 < NP:
                            less_token(i)
                    g.tensor_tensor(bandc[:, NP - 1, :], bandc[:, NP - 1, :], ident[:, :], ALU.subtract).then_inc(consts_made, 1)
                if t == NT:
                    for k in range(KD):
                        pool.wait_ge(wo_hi, k + 1)
                        g.tensor_tensor(wol[:, k, :], raw[:, place[("wo", k)] % RING, :], woh[:, k, :].bitcast(F32),
                                        ALU.subtract).then_inc(wo_lo, 1)

            def lo_h2(i):
                pool.wait_ge(h2_hi, i + 1)
                g.tensor_tensor(h2l[:, :, i * P:(i + 1) * P], hx[:, :].rearrange("p (k n) -> p k n", n=P),
                                h2h[:, :, i * P:(i + 1) * P].bitcast(F32), ALU.subtract).then_inc(h2_lo, 1)

            for i in range(NT):
                if i >= 1:
                    lo_h2(i - 1)
                pool.wait_ge(x2_squared, i + 1)
                root(r2[:, i:i + 1], ss2[:, i:i + 1], D, x2_root)
            lo_h2(NT - 1)

            def lo_w1(b):
                for j in range(2):
                    pool.wait_ge(w1_hi, 2 * b + j + 1)
                    g.tensor_tensor(w1l[:, 4 * j:4 * j + 4, :], raw[:, j, :].rearrange("p (k n) -> p k n", k=4),
                                    w1h[:, 4 * j:4 * j + 4, :].bitcast(F32), ALU.subtract).then_inc(w1_lo, 1)

            def prepare_w2(b, use):
                for j in range(2):
                    pool.wait_ge(raw_in[2 + j], 16 * use)
                    g.tensor_tensor(raw[:, 2 + j, :], raw[:, 2 + j, :], g2b[:, :], ALU.mult).then_inc(w2_gated, 1)
                for j in range(2):
                    pool.wait_ge(w2_hi, 2 * b + j + 1)
                    g.tensor_tensor(w2l[:, j, :], raw[:, 2 + j, :], w2h[:, j, :].bitcast(F32), ALU.subtract).then_inc(w2_lo, 1)

            lo_w1(0)
            pool.wait_ge(mod_taken, 5)
            prepare_w2(0, MLP_USE + 1)
            lo_w1(1)
            with pool.Fori(1, NB - 1) as b:
                prepare_w2(b, MLP_USE + 1 + b)
                lo_w1(b + 1)
            prepare_w2(NB - 1, MLP_USE + NB)

        @block.tensor
        def _(pe):
            mm = nc.tensor.matmul

            def tr(o, i, rows_=P):
                return nc.tensor.transpose(o, i, ident[0:rows_, 0:rows_])

            def three(o, wh, wl, ah, al, first, last):
                mm(o, wh, ah, start=first, stop=False)
                mm(o, wh, al, start=False, stop=False)
                return mm(o, wl, ah, start=False, stop=last)

            pe.wait_ge(ident_made, 2)
            pe.wait_ge(params_in, 160)
            pe.wait_ge(posf_ready, 1)
            tr(psum[:, 4, 0:72], rows[0:72, :], 72).then_inc(rows_turned, 1)
            pe.wait_ge(mod_summed, 2 * KD)
            for k in range(KD):
                tr(banks(0)[:, k * P:(k + 1) * P], acc[:, k * P:(k + 1) * P])
            for k in range(KD):
                ins = tr(banks(2)[:, k * P:(k + 1) * P], acc_sc[:, k * P:(k + 1) * P])
            ins.then_inc(mod_turned, 1)

            def turn_x(t):
                pe.wait_ge(x_scaled, t + 1)
                for k in range(KD):
                    ins = tr(banks(1)[:, k * P:(k + 1) * P], xh[:, t % 2, k * P:(k + 1) * P])
                ins.then_inc(x_turned, 1)

            def project(o, a, b):
                for k in range(KD):
                    ins = three(o, hTh[:, k, :], hTl[:, k, :], wih[:, k, a:b], wil[:, k, a:b], k == 0, k == KD - 1)
                return ins

            def turn_p(i, kv):
                pe.wait_ge(normed, 2 * i + kv + 1)
                if kv:
                    pe.wait_ge(pT_lo, 2 * i + 1)
                else:
                    pe.wait_ge(exped, 2 * i + 2)
                for blk in range(1 if i == 0 else 2):
                    for h in range(G):
                        ins = tr(psum[:, 4 + blk, h * P:(h + 1) * P], pr[:, kv, h, blk * P:(blk + 1) * P])
                ins.then_inc(p_turned, 1)

            def attend(i, kv):
                pe.wait_ge(pT_lo, 2 * i + kv + 1)
                pe.wait_ge(v_lo, i + 1)
                blocks = [i % 2] if i == 0 else [i % 2, (i - 1) % 2]
                for n, blk in enumerate(blocks):
                    s = (i - n) % 4
                    vh, vl = (vv[:, s, kv, a, :, :].rearrange("p b d -> p (b d)") for a in range(2))
                    ph, pl = (a[:, blk, :, :].rearrange("p h q -> p (h q)") for a in (pTh, pTl))
                    ins = three(bank(0), vh, vl, ph, pl, n == 0, n == len(blocks) - 1)
                ins.then_inc(pv_done, 1)

            def score(i, kv):
                if kv:
                    pe.wait_ge(exped, 2 * i + 1)
                elif i >= 1:
                    pe.wait_ge(pT_lo, 2 * i)
                for h in range(G):
                    w = P if i == 0 else 2 * P
                    o = psum[:, 4 + h // 2, (h % 2) * 256:(h % 2) * 256 + w]
                    m0 = P if i % 2 == 0 else 0
                    mm(o, identr[:, :], maskr[:, m0:m0 + w], start=True, stop=False)
                    for a in range(2):
                        if i == 0:
                            k_ = kT[:, kv, a, 0, :]
                        else:
                            k_ = kT[:, kv, a, :, :].rearrange("p b n -> p (b n)")
                        ins = mm(o, qT[:, kv * G + h, :], k_, start=False, stop=a == 1)
                ins.then_inc(scored, 1)

            pe.wait_ge(mod_taken, 1)
            turn_x(0)
            for t in range(NT + 2):
                if t < NT:
                    pe.wait_ge(h_lo, t + 1)
                    if t == 0:
                        pe.wait_ge(wu_lo, KD // 2)
                    if t >= 3:
                        pe.wait_ge(attn_kept, 2 * (t - 2))
                    project(bank(0), QKV, IN).then_inc(u_done, 1)
                if 1 <= t <= NT:
                    if t == 1:
                        pe.wait_ge(poolw_ready, 1)
                    pe.wait_ge(pooled_kept, t)
                    for j in range(NP):
                        ins = mm(psum[:, 7, j * P:(j + 1) * P], poolw[:, j, :], pooledT[:, j * P:(j + 1) * P],
                                 start=True, stop=True)
                    ins.then_inc(pout_done, 1)
                if 1 <= t <= NT:
                    pe.wait_ge(qk_lo, t)
                    if t < NT:
                        pe.wait_ge(h_made, t + 1)
                    for h in range(NH):
                        ins = tr(banks(1)[:, h * P:(h + 1) * P], q2[:, h, :, :].rearrange("p a d -> p (a d)"))
                    ins.then_inc(q_turned, 1)
                    pe.wait_ge(v_lo, t)
                    pe.wait_ge(k_normed, t)
                    for e in range(NKV):
                        for a in range(2):
                            ins = tr(psum[:, 3, (2 * e + a) * P:(2 * e + a + 1) * P],
                                     k2[:, e, a, :, :].rearrange("p b d -> p (b d)"))
                    ins.then_inc(k_turned, 1)
                if t == NT:
                    pe.wait_ge(q_normed, NT)
                    pe.wait_ge(pout_kept, NT)
                    pe.wait_ge(gate_biased, 1)
                    for n in range(2):
                        ins = mm(bank(6 + n), ones[:, :], acc[:, 512 * n:512 * n + 512], start=True, stop=True)
                    ins.then_inc(mod_turned, 1)
                if t >= 2:
                    turn_p(t - 2, 0)
                if t < NT:
                    if t == 0:
                        pe.wait_ge(wqkv_lo, KD)
                    if t >= 1:
                        pe.wait_ge(q_normed, t)
                    project(bank(6), 0, AW).then_inc(q_done, 1)
                if t >= 2:
                    if t < NT:
                        pe.wait_ge(u_kept, t + 1)
                    attend(t - 2, 0)
                    turn_p(t - 2, 1)
                if t < NT:
                    if t >= 1:
                        pe.wait_ge(kT_kept, t)
                    project(psum[:, 3, 0:2 * KVW], AW, QKV).then_inc(kv_done, 1)
                if t in (2, 4):
                    pe.wait_ge(qT_kept, t)
                    pe.wait_ge(job_summed, 4 * t)
                    for k in range(KD):
                        ins = tr(banks(1)[:, k * P:(k + 1) * P], acc[:, k * P:(k + 1) * P])
                    ins.then_inc(mod_turned, 1)
                    pe.wait_ge(mod_taken, t // 2 + 1)
                if t + 1 < NT:
                    if t >= 1:
                        pe.wait_ge(qT_kept, t)
                    else:
                        pe.wait_ge(h_made, 1)
                    turn_x(t + 1)
                if 1 <= t <= NT:
                    pe.wait_ge(qT_kept, t)
                    pe.wait_ge(kT_kept, t)
                    if t == 1:
                        pe.wait_ge(mask_ready, 2)
                    score(t - 1, 0)
                if t >= 2:
                    pe.wait_ge(attn_kept, 2 * (t - 2) + 1)
                    attend(t - 2, 1)
                if t < NT:
                    pe.wait_ge(u_kept, t + 1)
                    if t < 2:
                        pe.wait_ge(consts_made, t + 1)
                    if t >= 1:
                        pe.wait_ge(pout_kept, t)
                    for j in range(NP):
                        o = psum[:, 7, j * P:(j + 1) * P]
                        ins = mm(o, usb[:, t % 2, j * P:(j + 1) * P], bandc[:, j, :], start=True, stop=t == 0)
                        if t >= 1:
                            ins = mm(o, usb[:, (t - 1) % 2, j * P:(j + 1) * P], bandp[:, j, :], start=False, stop=True)
                    ins.then_inc(band_done, 1)
                if 1 <= t <= NT:
                    score(t - 1, 1)

            def turn_x2(i):
                pe.wait_ge(x2_scaled, i + 1)
                if i >= 1:
                    pe.wait_ge(h2_made, i)
                for k in range(KD):
                    ins = tr(banks(4)[:, k * P:(k + 1) * P], hx[:, k * P:(k + 1) * P])
                ins.then_inc(x2_turned, 1)

            pe.wait_ge(mod_taken, 4)
            for i in range(NT):
                if i >= 2:
                    pe.wait_ge(x2_ready, i - 1)
                elif i == 0:
                    pe.wait_ge(attn_kept, 2 * NT)
                    pe.wait_ge(qT_kept, NT)
                    pe.wait_ge(kT_kept, NT)
                for k in range(KD):
                    if i == 0:
                        pe.wait_ge(wo_lo, k + 1)
                    if k % 4 == 0:
                        pe.wait_ge(mix_lo, 2 * i + k // 4 + 1)
                    for n in range(2):
                        ins = three(bank(2 * (i % 2) + n), mTh[:, k, :], mTl[:, k, :], woh[:, k, 512 * n:512 * n + 512],
                                    wol[:, k, 512 * n:512 * n + 512], k == 0, k == KD - 1)
                    if k % 4 == 3:
                        ins.then_inc(wo_used, 1)
                if i >= 1:
                    turn_x2(i - 1)
            pe.wait_ge(gate_biased, 2)
            for n in range(2):
                ins = mm(bank(6 + n), ones[:, :], acc[:, 512 * n:512 * n + 512], start=True, stop=True)
            ins.then_inc(mod_turned, 1)
            turn_x2(NT - 1)

            def mlp_block(b, first):
                for u in range(2 * NF):
                    f, n = u % NF, u // NF
                    cut = slice(512 * n, 512 * n + 512)
                    if first:
                        if u == 0:
                            pe.wait_ge(x2_ready, NT)
                            pe.wait_ge(h2_lo, 4)
                        if u == NF:
                            pe.wait_ge(h2_lo, NT)
                    else:
                        pe.wait_ge(relu_kept, 2 * NF * (b - 1) + u + 1)
                    for k in range(KD):
                        if u == 0 and k % 4 == 0:
                            pe.wait_ge(w1_lo, 2 * b + k // 4 + 1)
                        ins = three(bank(u), w1h[:, k, f * P:(f + 1) * P], w1l[:, k, f * P:(f + 1) * P],
                                    h2h[:, k, cut], h2l[:, k, cut], k == 0, k == KD - 1)
                    ins.then_inc(up_done, 1)
                for n in range(2 * NT):
                    i, half = n // 2, n % 2
                    cut = slice(512 * half, 512 * half + 512)
                    if n == 0:
                        pe.wait_ge(act_lo, 2 * NF * b + NF)
                        pe.wait_ge(w2_lo, 2 * b + 2)
                    if n == NT:
                        pe.wait_ge(act_lo, 2 * NF * b + 2 * NF)
                    if first and n < 4:
                        if n == 0:
                            pe.wait_ge(mod_taken, 5)
                            pe.wait_ge(h2_made, NT)
                    else:
                        pe.wait_ge(added, 2 * NT * b + n - 3)
                    for f in range(NF):
                        ins = three(bank(4 + n % 4), aTh[:, f, i * P:(i + 1) * P], aTl[:, f, i * P:(i + 1) * P],
                                    w2h[:, f, cut], w2l[:, f, cut], f == 0, f == NF - 1)
                    ins.then_inc(down_done, 1)

            mlp_block(0, True)
            with pe.Fori(1, NB) as b:
                mlp_block(b, False)


_INS = ["x", "c", "positions", "w_ada", "b_ada", "norm1_g", "w_in", "q_norm_g", "k_norm_g", "attn_sinks",
        "pool_w", "pool_scale", "w_o", "norm2_g", "w_mlp_in", "w_mlp_out"]


def kernel(**inputs):
    import concourse.bacc as bacc
    from concourse.bass_utils import run_bass_kernel_spmd

    nc = bacc.Bacc("TRN2", target_bir_lowering=False, num_devices=1)
    arrays, args = {}, []
    for name in _INS:
        a = np.ascontiguousarray(inputs[name])
        arrays[f"in_{name}"] = a
        args.append(nc.dram_tensor(f"in_{name}", a.shape, mybir.dt.from_np(a.dtype), kind="ExternalInput").ap())
    shape = inputs["x"].shape
    result = nc.dram_tensor("out_0", shape, F32, kind="ExternalOutput").ap()
    build(nc, *args, result)
    r = run_bass_kernel_spmd(nc, [arrays], core_ids=[0])
    return r.results[0]["out_0"]
```

```python
from contextlib import ExitStack

import concourse.bass as bass
import numpy as np
from concourse import mybir

P = 128
F32 = mybir.dt.float32
F32R = mybir.dt.float32r
BF16 = mybir.dt.bfloat16
I32 = mybir.dt.int32
ALU = mybir.AluOpType
ACT = mybir.ActivationFunctionType
AX_X = mybir.AxisListType.X

HEAD_DIM = 64
POOL_WINDOWS = (2, 4, 8, 16)
ROT_DIM = HEAD_DIM // 4
HALF = ROT_DIM // 2
ROPE_THETA = 500000.0
EPS = 1e-6
MASKED = -1e30
FB = 256
RING = 4
SH1, SC1, G1, SH2, SC2, G2 = range(6)

TWO_PI_1 = 6.28125
TWO_PI_2 = 0.0019350051879882812
TWO_PI_3 = 2 * np.pi - TWO_PI_1 - TWO_PI_2
ROUND_MAGIC = 12582912.0
PI_LIMIT = 3.1415925


def bcast(ap, axis, n):
    a = ap.unsqueeze(axis)
    shape = list(a.shape)
    shape[axis] = n
    return a.to_broadcast(shape)


def build(nc, x, c, positions, w_ada, b_ada, norm1_g, w_in, q_norm_g, k_norm_g, attn_sinks,
          pool_w, pool_scale, w_o, norm2_g, w_mlp_in, w_mlp_out, out):
    S, D = x.shape[1], x.shape[2]
    IN = w_in.shape[2]
    FF = w_mlp_in.shape[2]
    NH = attn_sinks.shape[1]
    PW = pool_scale.shape[1]
    AW = NH * HEAD_DIM
    KVW = (IN - AW - PW) // 2
    NKV = KVW // HEAD_DIM
    G = NH // NKV
    NP = pool_w.shape[1]
    NT = S // P
    KD = D // P
    NB = FF // FB
    NF = FB // P
    NHN = NH + NKV
    QKV = AW + 2 * KVW
    SCALE = HEAD_DIM ** -0.5
    assert NT == 8 and KD == 8 and G == 4 and NKV == 2 and NP == 4 and D == 1024

    x_rows = x[0]
    out_rows = out[0]
    wada = w_ada[0].rearrange("(p k) n -> p k n", k=KD)
    win = w_in[0].rearrange("(k p) n -> p k n", p=P)
    wo = w_o[0].rearrange("(k p) n -> p k n", p=P)
    w1 = w_mlp_in[0].rearrange("(k p) n -> p k n", p=P)
    w2 = w_mlp_out[0]

    with ExitStack() as ctx:
        def sem(name):
            return ctx.enter_context(nc.semaphore(name))

        def sb(name, shape, dt=F32):
            return ctx.enter_context(nc.sbuf_tensor(name, shape, dt))

        ident = sb("ident", [P, P])
        identr = sb("identr", [P, P], F32R)
        ones = sb("ones", [P, P])
        small = sb("small", [P, 256])
        cols = sb("cols", [P, 72])
        a1, b1, a2, b2 = (small[:, 8 * j:8 * j + 8] for j in range(4))
        silu = small[:, 32:40]
        ctmp = small[:, 40:48]
        ssx = small[:, 48:56]
        rx = small[:, 56:64]
        ss2 = small[:, 64:72]
        r2 = small[:, 72:80]
        ssq = small[:, 80:90]
        rq = small[:, 90:100]
        sink = small[:, 100:108]
        nsink = small[:, 108:116]
        negm = small[:, 116:124]
        earg = small[:, 124:132]
        es = small[:, 132:140]
        den = small[:, 140:148]
        rden = small[:, 148:156]
        mx = small[:, 156:164]
        mhalf = small[:, 164:174]
        slots = sb("slots", [P, NT, D])
        raw = sb("raw", [P, RING, 1024])
        acc = sb("acc", [P, D])

        with ExitStack() as mix_ctx:
            def mb(name, shape, dt=F32):
                return mix_ctx.enter_context(nc.sbuf_tensor(name, shape, dt))
            wih = mb("w_in_hi", [P, KD, IN], F32R)
            wil = mb("w_in_lo", [P, KD, IN], F32R)
            xh = mb("xh", [P, 2, D])
            hTh = mb("hT_hi", [P, KD, P], F32R)
            hTl = mb("hT_lo", [P, KD, P], F32R)
            qkn = mb("qkn", [P, NHN, HEAD_DIM])
            q2 = mb("q2", [P, NH, 2, HEAD_DIM])
            k2 = mb("k2", [P, NKV, 2, 2, HEAD_DIM])
            qT = mb("qT", [P, NH, P], F32R)
            kT = mb("kT", [P, NKV, 2, 2, P], F32R)
            vv = mb("vv", [P, 4, NKV, 2, 2, HEAD_DIM], F32R)
            pr = mb("probs", [P, NKV, G, 2 * P])
            pTh = mb("pT_hi", [P, 2, G, P], F32R)
            pTl = mb("pT_lo", [P, 2, G, P], F32R)
            usb = mb("u_rows", [P, 2, PW])
            pooledT = mb("pooledT", [P, PW])
            poolw = mb("pool_w", [P, NP, P])
            bandc = mb("band_cur", [P, NP, P])
            bandp = mb("band_prev", [P, NP, P])
            maskr = mb("maskr", [P, 3 * P], F32R)
            gqk = mb("gqk", [P, 2, HEAD_DIM])
            trig = mb("trig", [P, NT, 4, HALF])
            rot = mb("rot", [P, 2, NHN, 2, HALF])
            junk = pooledT[:, :].bitcast(BF16)

        with ExitStack() as out_ctx:
            def ob(name, shape, dt=F32):
                return out_ctx.enter_context(nc.sbuf_tensor(name, shape, dt))
            woh = ob("w_o_hi", [P, KD, D], F32R)
            wol = ob("w_o_lo", [P, KD, D], F32R)
            g1b = ob("g1_rows", [P, D])
            mTh = ob("mixT_hi", [P, KD, P], F32R)
            mTl = ob("mixT_lo", [P, KD, P], F32R)
            hx = ob("hx", [P, D])
        with ExitStack() as mlp_ctx:
            def lb(name, shape, dt=F32):
                return mlp_ctx.enter_context(nc.sbuf_tensor(name, shape, dt))
            w1h = lb("w1_hi", [P, KD, FB], F32R)
            w1l = lb("w1_lo", [P, KD, FB], F32R)
            w2h = lb("w2_hi", [P, NF, D], F32R)
            w2l = lb("w2_lo", [P, NF, D], F32R)
            aTh = lb("aT_hi", [P, NF, S], F32R)
            aTl = lb("aT_lo", [P, NF, S], F32R)
            relu = lb("relu", [P, 2, 512])
            rsq = lb("relu_squared", [P, 2, 512])
        over_w_in = 2 * KD * IN
        sb("w_in_place", [P, over_w_in])
        h2T = sb("h2T", [P, NT, 2, KD, P], F32R)
        junk2 = sb("junk2", [P, D], BF16)
        g2b = sb("g2_rows", [P, D])

        psum = ctx.enter_context(nc.psum_tensor("psum", [P, 8, 512], F32))

        def bank(j):
            return psum[:, j, :]

        def banks(j):
            return psum[:, j:j + 2, :].rearrange("p b n -> p (b n)")

        stream = [("sh1", k) for k in range(KD)]
        stream += [("wu", 0), ("wu", 1)]
        stream += [("sc1", k) for k in range(KD)]
        stream += [("wu", 2), ("wu", 3)]
        stream += [("wqkv", k) for k in range(KD)]
        EARLY = len(stream)
        WIDE = RING + NT
        for job in ("sh2", "sc2", "g1"):
            stream += [(job, k) for k in range(KD)]
        stream += [("wo", k) for k in range(KD)]
        for k in range(KD):
            stream += [("x", k), ("g2", k)]
        stream += [("w1", 0), ("w1", 1), ("w2", 0), ("w2", 1)]
        place = {piece: n for n, piece in enumerate(stream)}
        assert EARLY % WIDE == RING and (len(stream) - EARLY) % RING == 0
        EARLY_USE = EARLY // WIDE + 1
        MLP_USE = EARLY_USE + (len(stream) - 4 - EARLY) // RING
        adaln_jobs = ("sh2", "sc2", "g1", "g2")
        mod_of = {"sh1": SH1, "sc1": SC1, "g1": G1, "sh2": SH2, "sc2": SC2, "g2": G2}

        def buffer_of(n):
            if n < EARLY:
                return n % WIDE, n // WIDE + 1, n - WIDE
            m = n - EARLY
            return m % RING, EARLY_USE + m // RING + 1, n - RING

        def piece_at(n):
            s = buffer_of(n)[0]
            return raw[:, s, :] if s < RING else slots[:, s - RING, :]

        raw_in = [sem(f"raw_in{s}") for s in range(WIDE)]
        c_in, params_in = sem("c_in"), sem("params_in")
        x_in = [sem("x_in0"), sem("x_in1")]
        out_done = sem("out_done")
        ident_made = sem("ident_made")
        rows_turned = sem("rows_turned")
        cols_ready = sem("cols_ready")
        exp_c = sem("exp_c")
        angles_ready = sem("angles_ready")
        trig_ready = sem("trig_ready")
        consts_made = sem("consts_made")
        poolw_ready = sem("poolw_ready")
        posf_ready = sem("posf_ready")
        mask_ready = sem("mask_ready")
        mod_summed = sem("mod_summed")
        job_summed = sem("job_summed")
        gate_biased = sem("gate_biased")
        mod_turned = sem("mod_turned")
        sc1_turned = sem("sc1_turned")
        mod_taken = sem("mod_taken")
        wu_hi, wu_lo = sem("wu_hi"), sem("wu_lo")
        wqkv_hi, wqkv_lo = sem("wqkv_hi"), sem("wqkv_lo")
        wo_hi, wo_lo_pool, wo_lo_dve = sem("wo_hi"), sem("wo_lo_pool"), sem("wo_lo_dve")
        x_squared, x_root, x_scaled = sem("x_squared"), sem("x_root"), sem("x_scaled")
        x_turned = sem("x_turned")
        h_made, h_hi, h_lo = sem("h_made"), sem("h_hi"), sem("h_lo")
        u_done, u_kept = sem("u_done"), sem("u_kept")
        band_done, pooled_kept, pout_done, pout_kept = sem("band_done"), sem("pooled_kept"), sem("pout_done"), sem("pout_kept")
        q_done, kv_done = sem("q_done"), sem("kv_done")
        q_squared, kv_squared, qk_sums, qk_root = sem("q_squared"), sem("kv_squared"), sem("qk_sums"), sem("qk_root")
        q_normed, k_normed, qk_gained, qk_roped = sem("q_normed"), sem("k_normed"), sem("qk_gained"), sem("qk_roped")
        qk_hi, qk_lo = sem("qk_hi"), sem("qk_lo")
        v_hi, v_lo = sem("v_hi"), sem("v_lo")
        q_turned, k_turned, qT_kept, kT_kept = sem("q_turned"), sem("k_turned"), sem("qT_kept"), sem("kT_kept")
        scored, max_ready, exped, den_ready, normed = (sem("scored"), sem("max_ready"), sem("exped"),
                                                       sem("den_ready"), sem("normed"))
        p_turned, pT_hi, pT_lo, pv_done, attn_kept = (sem("p_turned"), sem("pT_hi_ready"), sem("pT_lo_ready"),
                                                      sem("pv_done"), sem("attn_kept"))
        mix_hi, mix_lo = sem("mix_hi"), sem("mix_lo")
        wo_used = sem("wo_used")
        x2_gated = sem("x2_gated")
        x2_ready, x2_squared, x2_root, x2_scaled = sem("x2_ready"), sem("x2_squared"), sem("x2_root"), sem("x2_scaled")
        x2_turned, h2_made, h2_hi, h2_lo = sem("x2_turned"), sem("h2_made"), sem("h2_hi"), sem("h2_lo")
        w1_hi, w1_lo = sem("w1_hi_ready"), sem("w1_lo_ready")
        w2_gated, w2_hi, w2_lo = sem("w2_gated"), sem("w2_hi_ready"), sem("w2_lo_ready")
        up_done, relu_kept, act_hi, act_sq, act_lo = (sem("up_done"), sem("relu_kept"), sem("act_hi"), sem("act_sq"),
                                                      sem("act_lo"))
        down_done, added = sem("down_done"), sem("added")
        own = {e: sem(f"own_{e}") for e in ("act", "dve", "pool")}

        block = ctx.enter_context(nc.Block())

        class Chain:

            def __init__(self, eng, s, base=0):
                self.eng, self.s, self.n, self.base = eng, s, 0, base

            def step(self, ins):
                ins.then_inc(self.s, 1)
                self.n += 1

            def wait(self):
                self.eng.wait_ge(self.s, self.base + self.n)

        def landed(eng, piece):
            n = place[piece]
            buf, use, _ = buffer_of(n)
            eng.wait_ge(raw_in[buf], 16 * use)
            return piece_at(n)

        def freed(eng, n):
            before = buffer_of(n)[2]
            if before < 0:
                return
            kind, k = stream[before]
            if kind in ("sh1", "sc1"):
                eng.wait_ge(mod_summed, k + 1 + (KD if kind == "sc1" else 0) + (kind == "sc1" and k == KD - 1))
            elif kind in adaln_jobs:
                eng.wait_ge(job_summed, KD * adaln_jobs.index(kind) + k + 1)
            elif kind == "x":
                eng.wait_ge(x2_ready, k + 1)
            elif kind == "wo":
                eng.wait_ge(wo_lo_dve if k % 2 else wo_lo_pool, k // 2 + 1)
            else:
                eng.wait_ge({"wu": wu_lo, "wqkv": wqkv_lo}[kind], k + 1)

        def source(kind, k):
            if kind == "wu":
                return win[:, 2 * k:2 * k + 2, QKV:IN]
            if kind == "wqkv":
                return win[:, k, 0:QKV]
            if kind == "wo":
                return wo[:, k, :]
            if kind == "x":
                return x_rows[k * P:(k + 1) * P, :]
            if kind == "w1":
                return w1[:, 4 * k:4 * k + 4, 0:FB]
            if kind == "w2":
                return w2[k * P:(k + 1) * P, :]
            m = mod_of[kind]
            return wada[:, k, m * D:(m + 1) * D]

        def target(kind, a):
            if kind == "wu":
                return a.rearrange("p (k n) -> p k n", k=2)
            if kind == "wqkv":
                return a[:, 0:QKV]
            if kind == "w1":
                return a.rearrange("p (k n) -> p k n", k=4)
            return a

        rows = pr[:, 0, :, :].rearrange("p h n -> p (h n)")[:, 0:P]
        posi = pr[:, 1, :, :].rearrange("p h n -> p (h n)")[:, 0:P].bitcast(I32)
        scale_row = pr[:, 1, :, :].rearrange("p h n -> p (h n)")[:, 512:1024]
        cin = small[:, 192:200]
        acc_sc = q2[:, :, :, :].rearrange("p h a d -> p (h a d)")
        ang = qkn[:, :, :].rearrange("p h d -> p (h d)")[:, 2 * P:]
        ANG = NT * HALF

        @block.sync
        def _(sp):
            def load(n):
                kind, k = stream[n]
                freed(sp, n)
                sp.dma_start(target(kind, piece_at(n)), source(kind, k)).then_inc(raw_in[buffer_of(n)[0]], 16)

            def load_x(t):
                if t >= 2:
                    sp.wait_ge(h_lo, 2 * (t - 1))
                sp.dma_start(xh[:, t % 2, :], x_rows[t * P:(t + 1) * P, :]).then_inc(x_in[t % 2], 16)

            sp.dma_start(cin, c[0].rearrange("(p k) -> p k", k=KD)).then_inc(c_in, 16)
            first_job = place[("sh2", 0)]
            for n in range(first_job):
                load(n)
                if n == 7:
                    load_x(0)
            for t in range(NT):
                if t + 1 < NT:
                    load_x(t + 1)
                if t < 6:
                    for j in range(4):
                        load(first_job + 4 * t + j)
            for n in range(place[("wo", 0)], len(stream)):
                load(n)
            with sp.Fori(1, NB) as b:
                for j in range(2):
                    sp.wait_ge(w1_lo, 2 * b + j - 1)
                    sp.dma_start(target("w1", raw[:, j, :]), w1[:, 4 * j:4 * j + 4, bass.ds(b * FB, FB)]).then_inc(raw_in[j], 16)
                for j in range(2):
                    sp.wait_ge(w2_lo, 2 * b + j - 1)
                    sp.dma_start(target("w2", raw[:, 2 + j, :]), w2[bass.ds(b * FB + j * P, P), :]).then_inc(raw_in[2 + j], 16)
            for i in range(NT):
                sp.wait_ge(added, 16 * (NB - 1) + 2 * i + 2)
                sp.dma_start(out_rows[i * P:(i + 1) * P, :], slots[:, i, :]).then_inc(out_done, 16)
            sp.wait_ge(out_done, 16 * NT)

        @block.scalar
        def _(act):
            own_a = Chain(act, own["act"])
            act.wait_ge(c_in, 16)
            nc.scalar.activation(ctmp, cin, ACT.Exp, scale=-1.0).then_inc(exp_c, 1)
            act.dma_start(rows[0:48, :], b_ada[0].rearrange("(j p) -> j p", p=P)).then_inc(params_in, 16)
            act.dma_start(rows[48:56, :], norm1_g[0].rearrange("(j p) -> j p", p=P)).then_inc(params_in, 16)
            act.dma_start(rows[56:64, :], norm2_g[0].rearrange("(j p) -> j p", p=P)).then_inc(params_in, 16)
            act.dma_start(posi[64:72, :], positions[0].rearrange("(j p) -> j p", p=P)).then_inc(params_in, 16)
            act.dma_start(scale_row, pool_scale.to_broadcast([P, PW])).then_inc(params_in, 16)
            act.dma_start(poolw[:, :, :], pool_w[0].rearrange("g c d -> c g d")).then_inc(params_in, 16)
            act.dma_start(gqk[:, 0, :], q_norm_g.to_broadcast([P, HEAD_DIM])).then_inc(params_in, 16)
            act.dma_start(gqk[:, 1, :], k_norm_g.to_broadcast([P, HEAD_DIM])).then_inc(params_in, 16)
            act.dma_start(sink, attn_sinks.to_broadcast([P, NH])).then_inc(params_in, 16)
            def square_x(t):
                act.wait_ge(x_in[t % 2], 16 * (t // 2 + 1))
                if t >= 1:
                    act.wait_ge(x_squared, t)
                nc.scalar.activation(junk, xh[:, t % 2, :], ACT.Square,
                                     accum_out=ssx[:, t:t + 1]).then_inc(x_squared, 1)

            def scale_x(t):
                act.wait_ge(x_root, t + 1)
                nc.scalar.activation(xh[:, t % 2, :], xh[:, t % 2, :], ACT.Copy,
                                     scale=rx[:, t:t + 1]).then_inc(x_scaled, 1)

            def hi_h(t):
                if t >= 1:
                    act.wait_ge(kv_done, t)
                for h in range(2):
                    if t == 0 and h == 1:
                        hi_wu(3)
                    act.wait_ge(h_made, 2 * t + h + 1)
                    nc.scalar.copy(hTh[:, 4 * h:4 * h + 4, :], xh[:, t % 2, 512 * h:512 * h + 512]
                                   .rearrange("p (k n) -> p k n", n=P)).then_inc(h_hi, 1)

            def hi_wu(j):
                a = landed(act, ("wu", j))
                nc.scalar.copy(wih[:, 2 * j:2 * j + 2, QKV:IN], a.rearrange("p (k n) -> p k n", k=2)).then_inc(wu_hi, 1)

            square_x(0)
            scale_x(0)
            hi_wu(0)
            hi_wu(1)
            hi_wu(2)
            hi_h(0)
            for k in range(KD):
                a = landed(act, ("wqkv", k))
                nc.scalar.copy(wih[:, k, 0:QKV], a[:, 0:QKV]).then_inc(wqkv_hi, 1)
            act.wait_ge(angles_ready, 1)
            nc.scalar.activation(trig[:, :, 1, :], ang[:, 0:ANG].rearrange("p (t f) -> p t f", f=HALF),
                                 ACT.Sin).then_inc(trig_ready, 1)
            nc.scalar.activation(trig[:, :, 2, :], ang[:, 0:ANG].rearrange("p (t f) -> p t f", f=HALF),
                                 ACT.Sin).then_inc(trig_ready, 1)
            nc.scalar.activation(trig[:, :, 0, :], ang[:, ANG:2 * ANG].rearrange("p (t f) -> p t f", f=HALF),
                                 ACT.Sin).then_inc(trig_ready, 1)
            nc.scalar.activation(trig[:, :, 3, :], ang[:, ANG:2 * ANG].rearrange("p (t f) -> p t f", f=HALF),
                                 ACT.Sin).then_inc(trig_ready, 1)


            def hi_pT(i, kv):
                act.wait_ge(p_turned, 2 * i + kv + 1)
                if 2 * i + kv >= 1:
                    act.wait_ge(pv_done, 2 * i + kv)
                for blk in range(1 if i == 0 else 2):
                    nc.scalar.copy(pTh[:, blk, :, :].rearrange("p h q -> p (h q)"), bank(4 + blk)).then_inc(pT_hi, 1)

            def keep_attn(i, kv):
                act.wait_ge(pv_done, 2 * i + kv + 1)
                o = bank(0).rearrange("p (m e q) -> p m e q", e=2, q=P)
                dst = slots[:, i, :].rearrange("p (m q) -> p m q", q=P)
                for e in range(2):
                    r = slice(64 * e, 64 * e + 64)
                    ins = nc.scalar.copy(dst[r, 2 * kv:2 * kv + 2, :], o[r, :, e, :])
                ins.then_inc(attn_kept, 1)

            def exps(i, kv):
                act.wait_ge(max_ready, 2 * i + kv + 1)
                if i >= 1:
                    act.wait_ge(p_turned, 2 * (i - 1) + kv + 1)
                w = P if i == 0 else 2 * P
                for h in range(G):
                    hh = kv * G + h
                    nc.scalar.activation(pr[:, kv, h, 0:w], psum[:, 4 + h // 2, (h % 2) * 256:(h % 2) * 256 + w], ACT.Exp,
                                         bias=negm[:, hh:hh + 1], scale=SCALE, accum_out=den[:, hh:hh + 1])
                nc.scalar.activation(es[:, kv * G:kv * G + G], earg[:, kv * G:kv * G + G], ACT.Exp).then_inc(exped, 1)

            def hi_qk(i):
                act.wait_ge(qk_roped, i + 1)
                nc.scalar.copy(q2[:, :, 0, :].bitcast(F32R), qkn[:, 0:NH, :])
                if i >= 1:
                    act.wait_ge(k_turned, i)
                nc.scalar.copy(k2[:, :, 0, :, :].bitcast(F32R), bcast(qkn[:, NH:NHN, :], 2, 2)).then_inc(qk_hi, 1)

            def keep_pout(i):
                act.wait_ge(pout_done, i + 1)
                nc.scalar.copy(slots[:, i, D - PW:D], bank(7)).then_inc(pout_kept, 1)

            def keep_qT(i):
                act.wait_ge(q_turned, i + 1)
                if i >= 1:
                    act.wait_ge(scored, 2 * i)
                nc.scalar.copy(qT[:, :, :].rearrange("p h q -> p (h q)"), banks(1)).then_inc(qT_kept, 1)

            def hi_wo(k):
                a = landed(act, ("wo", k))
                nc.scalar.copy(woh[:, k, :], a).then_inc(wo_hi, 1)

            for t in range(NT):
                if t >= 2:
                    exps(t - 2, 0)
                if t >= 1:
                    hi_qk(t - 1)
                act.wait_ge(u_done, t + 1)
                if t >= 2:
                    act.wait_ge(band_done, t)
                nc.scalar.copy(usb[:, t % 2, :], bank(0)).then_inc(u_kept, 1)
                if t >= 1:
                    keep_pout(t - 1)
                if t + 1 < NT:
                    square_x(t + 1)
                if t >= 2:
                    exps(t - 2, 1)
                if t + 1 < NT:
                    scale_x(t + 1)
                if t >= 1:
                    keep_qT(t - 1)
                act.wait_ge(q_done, t + 1)
                if t >= 1:
                    act.wait_ge(q_turned, t)
                sq = q2[:, :, :, :].rearrange("p h a d -> p (h a d)")
                nc.scalar.activation(sq[:, 0:AW], bank(6), ACT.Square).then_inc(q_squared, 1)
                if t >= 2:
                    hi_pT(t - 2, 0)
                act.wait_ge(kv_done, t + 1)
                nc.scalar.activation(sq[:, AW:AW + KVW], psum[:, 3, 0:KVW], ACT.Square).then_inc(kv_squared, 1)
                if t >= 4:
                    act.wait_ge(pv_done, 2 * (t - 2))
                nc.scalar.copy(vv[:, t % 4, :, 0, :, :],
                               bcast(psum[:, 3, KVW:2 * KVW].rearrange("p (g d) -> p g d", g=NKV), 2, 2)).then_inc(v_hi, 1)
                if t + 1 < NT:
                    hi_h(t + 1)
                if t == NT - 1:
                    hi_wo(0)
                if t >= 2:
                    keep_attn(t - 2, 0)
                    hi_pT(t - 2, 1)
                if t == NT - 1:
                    hi_wo(1)
                act.wait_ge(band_done, t + 1)
                act.wait_ge(x_squared, min(t + 2, NT))
                nc.scalar.copy(pooledT[:, :], bank(7)).then_inc(pooled_kept, 1)
                if t >= 2:
                    keep_attn(t - 2, 1)
            hi_wo(2)

            def hi_mix(i, h):
                if h == 0:
                    act.wait_ge(attn_kept, 2 * i + 2)
                else:
                    act.wait_ge(pout_kept, i + 1)
                if i >= 1:
                    act.wait_ge(wo_used, 2 * (i - 1) + h + 1)
                nc.scalar.copy(mTh[:, 4 * h:4 * h + 4, :],
                               slots[:, i, 512 * h:512 * h + 512].rearrange("p (k n) -> p k n", n=P)).then_inc(mix_hi, 1)

            def square_x2(i):
                act.wait_ge(x2_ready, i + 1)
                if i >= 1:
                    act.wait_ge(x2_squared, i)
                nc.scalar.activation(junk2[:, :], slots[:, i, :], ACT.Square,
                                     accum_out=ss2[:, i:i + 1]).then_inc(x2_squared, 1)

            def scale_x2(i):
                act.wait_ge(x2_root, i + 1)
                if i >= 1:
                    act.wait_ge(h2_lo, 2 * i)
                nc.scalar.activation(hx[:, :], slots[:, i, :], ACT.Copy, scale=r2[:, i:i + 1]).then_inc(x2_scaled, 1)

            def hi_h2(i, h):
                act.wait_ge(h2_made, 2 * i + h + 1)
                nc.scalar.copy(h2T[:, i, 0, 4 * h:4 * h + 4, :],
                               hx[:, 512 * h:512 * h + 512].rearrange("p (k n) -> p k n", n=P)).then_inc(h2_hi, 1)

            hi_mix(0, 0)
            keep_pout(NT - 1)
            exps(NT - 2, 0)
            hi_qk(NT - 1)
            hi_wo(3)
            hi_mix(0, 1)
            exps(NT - 2, 1)
            keep_qT(NT - 1)
            hi_wo(4)
            hi_wo(5)
            hi_wo(6)
            hi_wo(7)
            hi_pT(NT - 2, 0)
            hi_mix(1, 0)
            hi_mix(1, 1)
            keep_attn(NT - 2, 0)
            hi_pT(NT - 2, 1)
            square_x2(0)
            scale_x2(0)
            hi_mix(2, 0)
            keep_attn(NT - 2, 1)
            exps(NT - 1, 0)
            hi_mix(2, 1)
            hi_h2(0, 0)
            exps(NT - 1, 1)
            hi_h2(0, 1)
            square_x2(1)
            scale_x2(1)
            hi_pT(NT - 1, 0)
            hi_mix(3, 0)
            hi_mix(3, 1)
            keep_attn(NT - 1, 0)
            hi_h2(1, 0)
            hi_pT(NT - 1, 1)
            square_x2(2)
            hi_h2(1, 1)
            scale_x2(2)

            def hi_w1(b, use):
                for j in range(2):
                    act.wait_ge(raw_in[j], 16 * use)
                    nc.scalar.copy(w1h[:, 4 * j:4 * j + 4, :], raw[:, j, :].rearrange("p (k n) -> p k n", k=4)).then_inc(w1_hi, 1)

            def mlp_block(b, last):
                if not (isinstance(b, int) and b == 0):
                    act.wait_ge(down_done, 2 * NT * b)
                for j in range(2):
                    act.wait_ge(w2_gated, 2 * b + j + 1)
                    nc.scalar.copy(w2h[:, j, :], raw[:, 2 + j, :]).then_inc(w2_hi, 1)
                for u in range(2 * NF):
                    act.wait_ge(up_done, 2 * NF * b + u + 1)
                    relu_slot_free(act, b, u)
                    nc.scalar.activation(relu[:, u % 2, :], bank(u), ACT.Relu).then_inc(relu_kept, 1)
                    act.wait_ge(relu_kept, 2 * NF * b + u + 1)
                    nc.scalar.activation(aTh[:, u % NF, (u // NF) * 512:(u // NF) * 512 + 512], relu[:, u % 2, :],
                                         ACT.Square).then_inc(act_hi, 1)
                if not last:
                    act.wait_ge(up_done, 2 * NF * b + 2 * NF)
                    hi_w1(b + 1, MLP_USE + 2 + b)

            def relu_slot_free(eng, b, u):
                if isinstance(b, int) and 2 * NF * b + u - 2 < 0:
                    return
                eng.wait_ge(act_sq, 2 * NF * b + u - 1)

            for i in range(3, NT):
                if i + 1 < NT:
                    hi_mix(i + 1, 0)
                if i == 3:
                    keep_attn(NT - 1, 1)
                if i == NT - 1:
                    act.wait_ge(wo_used, 2 * NT - 1)
                    hi_w1(0, MLP_USE + 1)
                hi_h2(i - 1, 0)
                if i + 1 < NT:
                    hi_mix(i + 1, 1)
                hi_h2(i - 1, 1)
                square_x2(i)
                scale_x2(i)
            hi_h2(NT - 1, 0)
            hi_h2(NT - 1, 1)
            act.wait_ge(wo_used, 2 * NT)
            mlp_block(0, False)
            with act.Fori(1, NB - 1) as b:
                mlp_block(b, False)
            mlp_block(NB - 1, True)

        @block.vector
        def _(dve):
            own_d = Chain(dve, own["dve"])
            v = nc.vector
            v.memset(ones[:, :], 1.0).then_inc(ident_made, 1)
            dve.wait_ge(exp_c, 1)
            own_d.step(v.tensor_scalar(ctmp, ctmp, 1.0, None, ALU.add))
            own_d.wait()
            own_d.step(v.reciprocal(ctmp, ctmp))
            own_d.wait()
            own_d.step(v.tensor_tensor(silu, cin, ctmp, ALU.mult))
            own_d.wait()

            def add_piece(target_acc, piece, k, done):
                a = landed(dve, piece)
                if k == 0:
                    v.tensor_scalar(target_acc, a, silu[:, 0:1], None, ALU.mult).then_inc(done, 1)
                else:
                    v.scalar_tensor_tensor(out=target_acc, in0=a, scalar=silu[:, k:k + 1], in1=target_acc,
                                           op0=ALU.mult, op1=ALU.add).then_inc(done, 1)

            def angles():
                a0, a1_, a2_ = (ang[:, j * ANG:(j + 1) * ANG] for j in range(3))
                a3 = ang[:, 3 * ANG:4 * ANG]
                inv = (np.float32(ROPE_THETA) ** (-np.arange(0, ROT_DIM, 2, dtype=np.float32) / np.float32(ROT_DIM)))
                for f in range(HALF):
                    ins = v.tensor_scalar(a0.rearrange("p (t f) -> p t f", f=HALF)[:, :, f], cols[:, 64:72],
                                          float(inv[f]), None, ALU.mult)
                own_d.step(ins)
                own_d.wait()
                own_d.step(v.tensor_scalar(a1_, a0, float(1 / (2 * np.pi)), ROUND_MAGIC, ALU.mult, ALU.add))
                own_d.wait()
                own_d.step(v.tensor_scalar(a2_, a1_, -ROUND_MAGIC, None, ALU.add))
                own_d.wait()
                for part in (TWO_PI_1, TWO_PI_2, TWO_PI_3):
                    own_d.step(v.scalar_tensor_tensor(out=a0, in0=a2_, scalar=-part, in1=a0, op0=ALU.mult, op1=ALU.add))
                    own_d.wait()
                own_d.step(v.tensor_scalar(a0, a0, PI_LIMIT, -PI_LIMIT, ALU.min, ALU.max))
                own_d.wait()
                own_d.step(v.tensor_scalar(a3, a0, -1.0, None, ALU.mult))
                own_d.wait()
                own_d.step(v.tensor_tensor(a3, a3, a0, ALU.max))
                own_d.wait()
                v.tensor_scalar(a1_, a3, -1.0, float(np.pi / 2), ALU.mult, ALU.add).then_inc(angles_ready, 1)

            for n in range(2 * KD):
                if n >= 1:
                    dve.wait_ge(mod_summed, n)
                if n < KD:
                    add_piece(acc[:, :], ("sh1", n), n, mod_summed)
                elif n < 2 * KD - 1:
                    add_piece(acc_sc, ("sc1", n - KD), n - KD, mod_summed)
                else:
                    a = landed(dve, ("sc1", KD - 1))
                    for h in range(2):
                        cut = slice(512 * h, 512 * h + 512)
                        v.scalar_tensor_tensor(out=acc_sc[:, cut], in0=a[:, cut], scalar=silu[:, KD - 1:KD],
                                               in1=acc_sc[:, cut], op0=ALU.mult, op1=ALU.add).then_inc(mod_summed, 1)
                if n == KD:
                    dve.wait_ge(params_in, 16 * 9)
                    v.tensor_copy(rows[64:72, :], posi[64:72, :]).then_inc(posf_ready, 1)
                    own_d.step(v.tensor_scalar(nsink, sink, -1.0, None, ALU.mult))
                    v.tensor_tensor(poolw[:, :, :].rearrange("p g d -> p (g d)"),
                                    poolw[:, :, :].rearrange("p g d -> p (g d)"), scale_row, ALU.mult).then_inc(poolw_ready, 1)
                if n == KD + 2:
                    dve.wait_ge(rows_turned, 1)
                    v.tensor_copy(cols[:, :], psum[:, 4, 0:72]).then_inc(cols_ready, 1)
                if n == 2 * KD - 4:
                    dve.wait_ge(cols_ready, 1)
                    dve.wait_ge(mod_turned, 1)
                    v.tensor_reduce(b1, banks(0).rearrange("p (k n) -> p k n", n=P), AX_X, ALU.add).then_inc(mod_taken, 1)
                    dve.wait_ge(mod_taken, 1)
                    own_d.step(v.tensor_tensor(b1, b1, cols[:, 8 * SH1:8 * SH1 + 8], ALU.add))
            def scale_1(h):
                c4 = slice(4 * h, 4 * h + 4)
                dve.wait_ge(sc1_turned, h + 1)
                own_d.step(v.tensor_reduce(a1[:, c4], bank(2 + h).rearrange("p (k n) -> p k n", n=P), AX_X, ALU.add))
                own_d.wait()
                own_d.step(v.tensor_tensor(a1[:, c4], a1[:, c4],
                                           cols[:, 8 * SC1 + 4 * h:8 * SC1 + 4 * h + 4], ALU.add))
                own_d.wait()
                own_d.step(v.scalar_tensor_tensor(out=a1[:, c4], in0=a1[:, c4], scalar=1.0,
                                                  in1=cols[:, 48 + 4 * h:52 + 4 * h], op0=ALU.add, op1=ALU.mult))
                own_d.wait()

            def make_h(t):
                dve.wait_ge(x_turned, t + 1)
                for k in range(KD):
                    if t == 0 and k % 4 == 0:
                        scale_1(k // 4)
                    ins = v.tensor_scalar(xh[:, t % 2, k * P:(k + 1) * P], banks(6 if t == 0 else 1)[:, k * P:(k + 1) * P],
                                          a1[:, k:k + 1], b1[:, k:k + 1], ALU.mult, ALU.add)
                    if k % 4 == 3:
                        ins.then_inc(h_made, 1)

            def lo_h(t):
                for h in range(2):
                    dve.wait_ge(h_hi, 2 * t + h + 1)
                    v.tensor_tensor(hTl[:, 4 * h:4 * h + 4, :],
                                    xh[:, t % 2, 512 * h:512 * h + 512].rearrange("p (k n) -> p k n", n=P),
                                    hTh[:, 4 * h:4 * h + 4, :].bitcast(F32), ALU.subtract).then_inc(h_lo, 1)

            make_h(0)
            lo_h(0)
            angles()
            for k in range(KD):
                a = landed(dve, ("wqkv", k))
                dve.wait_ge(wqkv_hi, k + 1)
                v.tensor_tensor(wil[:, k, 0:QKV], a[:, 0:QKV], wih[:, k, 0:QKV].bitcast(F32), ALU.subtract).then_inc(wqkv_lo, 1)

            def lo_pT(i, kv):
                nb = 1 if i == 0 else 2
                for blk in range(nb):
                    dve.wait_ge(pT_hi, kv + 1 if i == 0 else 2 * (2 * i + kv) - 2 + blk + 1)
                    ins = v.tensor_tensor(pTl[:, blk, :, :].rearrange("p h q -> p (h q)"), bank(4 + blk),
                                          pTh[:, blk, :, :].rearrange("p h q -> p (h q)").bitcast(F32), ALU.subtract)
                ins.then_inc(pT_lo, 1)

            def maxes(i, kv):
                dve.wait_ge(scored, 2 * i + kv + 1)
                w = P if i == 0 else 2 * P
                g = slice(kv * G, kv * G + G)
                own_d.step(v.tensor_reduce(mx[:, g], banks(4).rearrange("p (h n) -> p h n", h=G)[:, :, 0:w], AX_X, ALU.max))
                own_d.wait()
                own_d.step(v.scalar_tensor_tensor(out=negm[:, g], in0=mx[:, g], scalar=-SCALE, in1=nsink[:, g],
                                                  op0=ALU.mult, op1=ALU.min))
                own_d.wait()
                v.tensor_tensor(earg[:, g], sink[:, g], negm[:, g], ALU.add).then_inc(max_ready, 1)

            def dens(i, kv):
                g = slice(kv * G, kv * G + G)
                dve.wait_ge(exped, 2 * i + kv + 1)
                own_d.step(v.tensor_tensor(den[:, g], den[:, g], es[:, g], ALU.add))
                own_d.wait()
                if i >= 1:
                    dve.wait_ge(normed, 2 * (i - 1) + kv + 1)
                v.reciprocal(rden[:, g], den[:, g]).then_inc(den_ready, 1)

            def lo_qk(i):
                dve.wait_ge(qk_hi, i + 1)
                v.tensor_tensor(q2[:, :, 1, :].bitcast(F32R), qkn[:, 0:NH, :], q2[:, :, 0, :], ALU.subtract)
                for e in range(NKV):
                    ins = v.tensor_tensor(k2[:, e, 1, :, :].bitcast(F32R), bcast(qkn[:, NH + e, :], 1, 2),
                                          k2[:, e, 0, :, :], ALU.subtract)
                ins.then_inc(qk_lo, 1)

            def keep_kT(i):
                dve.wait_ge(k_turned, i + 1)
                if i >= 1:
                    dve.wait_ge(scored, 2 * i)
                v.tensor_copy(kT[:, :, :, i % 2, :],
                              bank(3).rearrange("p (g a n) -> p g a n", g=NKV, a=2)).then_inc(kT_kept, 1)

            def lo_wo(k):
                dve.wait_ge(wo_hi, k + 1)
                v.tensor_tensor(wol[:, k, :], piece_at(place[("wo", k)]), woh[:, k, :].bitcast(F32),
                                ALU.subtract).then_inc(wo_lo_dve, 1)

            def add_job_pieces(pieces):
                for n in pieces:
                    if n >= 1:
                        dve.wait_ge(job_summed, n)
                    if n in (8, 16):
                        dve.wait_ge(mod_turned, n // 8 + 1)
                    add_piece(acc[:, :], (adaln_jobs[n // 8], n % 8), n % 8, job_summed)

            early_pieces = ([], [], [], range(10, 12), range(14, 16), range(18, 20), range(22, 24), [])
            late_pieces = (range(0, 4), range(4, 8), range(8, 10), range(12, 14), range(16, 18), range(20, 22), [], [])
            for t in range(NT):
                if t >= 2:
                    maxes(t - 2, 0)
                add_job_pieces(early_pieces[t])
                if t >= 1:
                    lo_qk(t - 1)
                if t in (2, 4):
                    dst, m = (b2, SH2) if t == 2 else (a2, SC2)
                    dve.wait_ge(mod_turned, t // 2 + 1)
                    v.tensor_reduce(dst, banks(1).rearrange("p (k n) -> p k n", n=P), AX_X, ALU.add).then_inc(mod_taken, 1)
                    dve.wait_ge(mod_taken, t // 2 + 1)
                    own_d.step(v.tensor_tensor(dst, dst, cols[:, 8 * m:8 * m + 8], ALU.add))
                    own_d.wait()
                    if t == 4:
                        own_d.step(v.scalar_tensor_tensor(out=a2, in0=a2, scalar=1.0, in1=cols[:, 56:64],
                                                          op0=ALU.add, op1=ALU.mult))
                        own_d.wait()
                if t >= 2:
                    dens(t - 2, 0)
                    maxes(t - 2, 1)
                if t >= 1:
                    keep_kT(t - 1)
                if t >= 2:
                    dens(t - 2, 1)
                if t >= 1:
                    add_job_pieces(late_pieces[t])
                if t == 6:
                    for k in range(KD):
                        dve.wait_ge(job_summed, 24)
                        ins = v.scalar_tensor_tensor(out=acc[:, k * P:(k + 1) * P], in0=ident[:, :],
                                                     scalar=cols[:, 8 * G1 + k:8 * G1 + k + 1],
                                                     in1=acc[:, k * P:(k + 1) * P], op0=ALU.mult, op1=ALU.add)
                    ins.then_inc(gate_biased, 1)
                if t + 1 < NT:
                    make_h(t + 1)
                if t >= 2:
                    lo_pT(t - 2, 0)
                dve.wait_ge(q_squared, t + 1)
                dve.wait_ge(kv_squared, t + 1)
                v.tensor_reduce(ssq, q2[:, :, :, :].rearrange("p h a d -> p (h a d)")[:, 0:AW + KVW]
                                .rearrange("p (h d) -> p h d", d=HEAD_DIM), AX_X, ALU.add).then_inc(qk_sums, 1)
                if t + 1 < NT:
                    lo_h(t + 1)
                if t >= 2:
                    lo_pT(t - 2, 1)
                dve.wait_ge(qk_root, t + 1)
                if t >= 1:
                    dve.wait_ge(qk_lo, t)
                v.tensor_tensor(qkn[:, 0:NH, :], bank(6).rearrange("p (h d) -> p h d", d=HEAD_DIM),
                                bcast(rq[:, 0:NH], 2, HEAD_DIM), ALU.mult).then_inc(q_normed, 1)
                dve.wait_ge(v_hi, t + 1)
                v.tensor_tensor(qkn[:, NH:NHN, :], psum[:, 3, 0:KVW].rearrange("p (h d) -> p h d", d=HEAD_DIM),
                                bcast(rq[:, NH:NHN], 2, HEAD_DIM), ALU.mult).then_inc(k_normed, 1)
                v.tensor_tensor(vv[:, t % 4, :, 1, :, :],
                                bcast(psum[:, 3, KVW:2 * KVW].rearrange("p (g d) -> p g d", g=NKV), 2, 2),
                                vv[:, t % 4, :, 0, :, :].bitcast(F32), ALU.subtract).then_inc(v_lo, 1)
                if t == 0:
                    add_job_pieces(late_pieces[0])
            lo_wo(1)

            def lo_mix(i, h):
                dve.wait_ge(mix_hi, 2 * i + h + 1)
                v.tensor_tensor(mTl[:, 4 * h:4 * h + 4, :],
                                slots[:, i, 512 * h:512 * h + 512].rearrange("p (k n) -> p k n", n=P),
                                mTh[:, 4 * h:4 * h + 4, :].bitcast(F32), ALU.subtract).then_inc(mix_lo, 1)

            def make_h2(i, h):
                dve.wait_ge(x2_turned, 2 * i + h + 1)
                for j in range(4):
                    k = 4 * h + j
                    ins = v.tensor_scalar(hx[:, k * P:(k + 1) * P], bank(4 + h if i == NT - 1 else 3)[:, j * P:(j + 1) * P],
                                          a2[:, k:k + 1], b2[:, k:k + 1], ALU.mult, ALU.add)
                ins.then_inc(h2_made, 1)

            def make_x2(i):
                dve.wait_ge(wo_used, 2 * i + 2)
                v.tensor_tensor(slots[:, i, :], banks(1 if i % 2 else 6), g1b[:, :], ALU.mult).then_inc(x2_gated, 1)
                a = landed(dve, ("x", i))
                dve.wait_ge(x2_gated, i + 1)
                v.tensor_tensor(slots[:, i, :], slots[:, i, :], a, ALU.add).then_inc(x2_ready, 1)

            def add_g2(k):
                if k == 0:
                    dve.wait_ge(mod_turned, 4)
                else:
                    dve.wait_ge(job_summed, 24 + k)
                add_piece(acc[:, :], ("g2", k), k, job_summed)

            maxes(NT - 2, 0)
            lo_mix(0, 0)
            dens(NT - 2, 0)
            lo_qk(NT - 1)
            maxes(NT - 2, 1)
            lo_wo(3)
            lo_mix(0, 1)
            keep_kT(NT - 1)
            dens(NT - 2, 1)
            lo_wo(5)
            lo_wo(7)
            lo_pT(NT - 2, 0)
            dve.wait_ge(mod_turned, 4)
            v.tensor_copy(g1b[:, :], banks(1)).then_inc(mod_taken, 1)
            lo_mix(1, 0)
            dve.wait_ge(mod_taken, 4)
            make_x2(0)
            lo_mix(1, 1)
            lo_pT(NT - 2, 1)
            add_g2(0)
            lo_mix(2, 0)
            maxes(NT - 1, 0)
            dens(NT - 1, 0)
            make_h2(0, 0)
            maxes(NT - 1, 1)
            make_h2(0, 1)
            lo_mix(2, 1)
            dens(NT - 1, 1)
            make_x2(1)
            add_g2(1)
            lo_pT(NT - 1, 0)
            lo_mix(3, 0)
            make_h2(1, 0)
            make_x2(2)
            make_h2(1, 1)
            lo_pT(NT - 1, 1)
            lo_mix(3, 1)
            add_g2(2)
            for i in range(3, NT):
                if i + 1 < NT:
                    lo_mix(i + 1, 0)
                make_h2(i - 1, 0)
                if i + 1 < NT:
                    lo_mix(i + 1, 1)
                else:
                    for j in range(2):
                        dve.wait_ge(w1_hi, j + 1)
                        v.tensor_tensor(w1l[:, 4 * j:4 * j + 4, :], raw[:, j, :].rearrange("p (k n) -> p k n", k=4),
                                        w1h[:, 4 * j:4 * j + 4, :].bitcast(F32), ALU.subtract).then_inc(w1_lo, 1)
                make_h2(i - 1, 1)
                make_x2(i)
                add_g2(i)
            for k in range(KD):
                dve.wait_ge(job_summed, 32)
                ins = v.scalar_tensor_tensor(out=acc[:, k * P:(k + 1) * P], in0=ident[:, :],
                                             scalar=cols[:, 8 * G2 + k:8 * G2 + k + 1],
                                             in1=acc[:, k * P:(k + 1) * P], op0=ALU.mult, op1=ALU.add)
            ins.then_inc(gate_biased, 1)
            make_h2(NT - 1, 0)
            make_h2(NT - 1, 1)
            dve.wait_ge(mod_turned, 5)
            v.tensor_copy(g2b[:, :], banks(6)).then_inc(mod_taken, 1)

            def mlp_block(b):
                for u in range(2 * NF):
                    dve.wait_ge(relu_kept, 2 * NF * b + u + 1)
                    v.tensor_tensor(rsq[:, u % 2, :], relu[:, u % 2, :], relu[:, u % 2, :], ALU.mult).then_inc(act_sq, 1)
                    dve.wait_ge(act_sq, 2 * NF * b + u + 1)
                    dve.wait_ge(act_hi, 2 * NF * b + u + 1)
                    cut = slice((u // NF) * 512, (u // NF) * 512 + 512)
                    v.tensor_tensor(aTl[:, u % NF, cut], rsq[:, u % 2, :], aTh[:, u % NF, cut].bitcast(F32),
                                    ALU.subtract).then_inc(act_lo, 1)
                for n in range(2 * NT):
                    dve.wait_ge(down_done, 2 * NT * b + n + 1)
                    o = slots[:, n // 2, (n % 2) * 512:(n % 2) * 512 + 512]
                    v.tensor_tensor(o, bank(4 + n % 4), o, ALU.add).then_inc(added, 1)

            with dve.Fori(0, NB) as b:
                mlp_block(b)

        @block.gpsimd
        def _(pool):
            own_p = Chain(pool, own["pool"])
            g = nc.gpsimd
            own_p.step(g.memset(ident[:, :], 0.0))
            own_p.wait()
            g.affine_select(out=ident[:, :], in_=ident[:, :], compare_op=ALU.not_equal, fill=1.0, base=0,
                            pattern=[[-1, P]], channel_multiplier=1).then_inc(ident_made, 1)
            own_p.step(g.memset(mhalf, -0.5))
            pool.wait_ge(ident_made, 2)
            own_p.step(g.tensor_copy(identr[:, :], ident[:, :]))

            def lo_wu(j):
                a = landed(pool, ("wu", j))
                pool.wait_ge(wu_hi, j + 1)
                g.tensor_tensor(wil[:, 2 * j:2 * j + 2, QKV:IN], a.rearrange("p (k n) -> p k n", k=2),
                                wih[:, 2 * j:2 * j + 2, QKV:IN].bitcast(F32), ALU.subtract).then_inc(wu_lo, 1)

            m = qkn[:, :, :].rearrange("p h d -> p (h d)")[:, 0:2 * P]
            own_p.step(g.memset(m, 0.0))
            own_p.wait()
            own_p.step(g.affine_select(out=m[:, 0:P], in_=m[:, 0:P], compare_op=ALU.is_gt, fill=MASKED, base=0,
                                       pattern=[[1, P]], channel_multiplier=-1))
            own_p.step(g.affine_select(out=m[:, P:2 * P], in_=m[:, P:2 * P], compare_op=ALU.is_ge, fill=MASKED, base=0,
                                       pattern=[[-1, P]], channel_multiplier=1))
            own_p.wait()
            g.tensor_copy(maskr[:, 0:2 * P], m[:, 0:2 * P]).then_inc(mask_ready, 1)
            g.tensor_copy(maskr[:, 2 * P:3 * P], m[:, 0:P]).then_inc(mask_ready, 1)

            def band_of(i, cut, base):
                w, n = POOL_WINDOWS[i], cut.shape[1]
                own_p.step(g.affine_select(out=cut, in_=cut, compare_op=ALU.is_ge, fill=0.0, base=base,
                                           pattern=[[1, n]], channel_multiplier=-1))
                own_p.wait()
                own_p.step(g.affine_select(out=cut, in_=cut, compare_op=ALU.is_ge, fill=0.0, base=w - 1 - base,
                                           pattern=[[-1, n]], channel_multiplier=1))
                own_p.wait()

            def less_token(i, n):
                return g.tensor_tensor(bandc[:, i, 0:n], bandc[:, i, 0:n], ident[:, 0:n], ALU.subtract)

            own_p.step(g.memset(bandp[:, :, :], 0.0))
            for i, w in enumerate(POOL_WINDOWS):
                own_p.step(g.memset(bandc[:, i, :], 1.0 / w))
            own_p.wait()
            for i, w in enumerate(POOL_WINDOWS):
                for s in range(w - 1):
                    own_p.step(g.memset(bandc[:, i, s:s + 1], float(np.float32(1.0) / np.float32(s + 1))))
                own_p.wait()
                band_of(i, bandc[:, i, :], 0)
                own_p.step(less_token(i, P))
                own_p.wait()
                own_p.step(g.memset(bandp[:, i, :], 1.0 / w))
                own_p.wait()
                band_of(i, bandp[:, i, :], P)
            own_p.step(g.tensor_copy(small[:, 200:201], small[:, 164:165]))
            pool.wait_ge(own["pool"], own_p.n)
            g.tensor_copy(small[:, 201:202], small[:, 164:165]).then_inc(consts_made, 1)

            def normalise(i, kv):
                pool.wait_ge(den_ready, 2 * i + kv + 1)
                w = P if i == 0 else 2 * P
                r = slice(kv * G, kv * G + G)
                g.tensor_tensor(pr[:, kv, :, 0:w], pr[:, kv, :, 0:w], bcast(rden[:, r], 2, w), ALU.mult).then_inc(normed, 1)

            def root(dst, src, n, done):
                own_p.step(g.tensor_scalar(dst, src, 1.0 / n, EPS, ALU.mult, ALU.add))
                own_p.wait()
                g.tensor_tensor(dst, dst, mhalf[:, 0:dst.shape[1]], ALU.pow).then_inc(done, 1)

            def root_x(t):
                pool.wait_ge(x_squared, t + 1)
                root(rx[:, t:t + 1], ssx[:, t:t + 1], D, x_root)

            root_x(0)
            for j in range(KD // 2):
                lo_wu(j)

            def lo_wo(k):
                pool.wait_ge(wo_hi, k + 1)
                g.tensor_tensor(wol[:, k, :], piece_at(place[("wo", k)]), woh[:, k, :].bitcast(F32),
                                ALU.subtract).then_inc(wo_lo_pool, 1)

            for t in range(NT):
                if t >= 2:
                    normalise(t - 2, 0)
                if t + 1 < NT:
                    root_x(t + 1)
                if t >= 2:
                    normalise(t - 2, 1)
                pool.wait_ge(qk_sums, t + 1)
                if t >= 1:
                    pool.wait_ge(k_normed, t)
                root(rq, ssq, HEAD_DIM, qk_root)
                if t == NT - 1:
                    lo_wo(0)
                pool.wait_ge(k_normed, t + 1)
                own_p.step(g.tensor_tensor(qkn[:, 0:NH, :], qkn[:, 0:NH, :], bcast(gqk[:, 0, :], 1, NH), ALU.mult))
                own_p.step(g.tensor_tensor(qkn[:, NH:NHN, :], qkn[:, NH:NHN, :], bcast(gqk[:, 1, :], 1, NKV), ALU.mult))
                own_p.wait()
                if t == 0:
                    pool.wait_ge(trig_ready, 4)
                part = qkn[:, :, 0:ROT_DIM].rearrange("p h (a f) -> p h a f", a=2)
                for j in range(2):
                    own_p.step(g.tensor_tensor(rot[:, j, :, :, :], part, bcast(trig[:, t, 2 * j:2 * j + 2, :], 1, NHN),
                                               ALU.mult))
                own_p.wait()
                own_p.step(g.tensor_tensor(part[:, :, 0, :], rot[:, 0, :, 0, :], rot[:, 0, :, 1, :], ALU.subtract))
                g.tensor_tensor(part[:, :, 1, :], rot[:, 1, :, 0, :], rot[:, 1, :, 1, :], ALU.add).then_inc(qk_roped, 1)
                if t == 0:
                    pool.wait_ge(band_done, 1)
                    for i, w in enumerate(POOL_WINDOWS):
                        own_p.step(g.memset(bandc[:, i, 0:w], 1.0 / w))
                        own_p.wait()
                        band_of(i, bandc[:, i, 0:w], 0)
                        if i + 1 < NP:
                            own_p.step(less_token(i, w))
                            own_p.wait()
                    less_token(NP - 1, POOL_WINDOWS[-1]).then_inc(consts_made, 1)
            lo_wo(2)

            def root_x2(i):
                pool.wait_ge(x2_squared, i + 1)
                root(r2[:, i:i + 1], ss2[:, i:i + 1], D, x2_root)

            def lo_h2(i, h):
                pool.wait_ge(h2_hi, 2 * i + h + 1)
                g.tensor_tensor(h2T[:, i, 1, 4 * h:4 * h + 4, :],
                                hx[:, 512 * h:512 * h + 512].rearrange("p (k n) -> p k n", n=P),
                                h2T[:, i, 0, 4 * h:4 * h + 4, :].bitcast(F32), ALU.subtract).then_inc(h2_lo, 1)

            normalise(NT - 2, 0)
            lo_wo(4)
            normalise(NT - 2, 1)
            lo_wo(6)
            root_x2(0)
            normalise(NT - 1, 0)
            lo_h2(0, 0)
            lo_h2(0, 1)
            normalise(NT - 1, 1)
            root_x2(1)
            lo_h2(1, 0)
            root_x2(2)
            lo_h2(1, 1)
            for i in range(3, NT):
                lo_h2(i - 1, 0)
                lo_h2(i - 1, 1)
                if i + 1 < NT:
                    root_x2(i)

            def lo_w1(b):
                for j in range(2):
                    pool.wait_ge(w1_hi, 2 * b + j + 1)
                    g.tensor_tensor(w1l[:, 4 * j:4 * j + 4, :], raw[:, j, :].rearrange("p (k n) -> p k n", k=4),
                                    w1h[:, 4 * j:4 * j + 4, :].bitcast(F32), ALU.subtract).then_inc(w1_lo, 1)

            def prepare_w2(b, use):
                for j in range(2):
                    pool.wait_ge(raw_in[2 + j], 16 * use)
                    g.tensor_tensor(raw[:, 2 + j, :], raw[:, 2 + j, :], g2b[:, :], ALU.mult).then_inc(w2_gated, 1)
                for j in range(2):
                    pool.wait_ge(w2_hi, 2 * b + j + 1)
                    g.tensor_tensor(w2l[:, j, :], raw[:, 2 + j, :], w2h[:, j, :].bitcast(F32), ALU.subtract).then_inc(w2_lo, 1)

            root_x2(NT - 1)
            lo_h2(NT - 1, 0)
            lo_h2(NT - 1, 1)
            pool.wait_ge(mod_taken, 5)
            prepare_w2(0, MLP_USE + 1)
            lo_w1(1)
            with pool.Fori(1, NB - 1) as b:
                prepare_w2(b, MLP_USE + 1 + b)
                lo_w1(b + 1)
            prepare_w2(NB - 1, MLP_USE + NB)

        @block.tensor
        def _(pe):
            mm = nc.tensor.matmul

            def tr(o, i, rows_=P):
                return nc.tensor.transpose(o, i, ident[0:rows_, 0:rows_])

            def three(o, wh, wl, ah, al, first, last):
                mm(o, wh, ah, start=first, stop=False)
                mm(o, wh, al, start=False, stop=False)
                return mm(o, wl, ah, start=False, stop=last)

            def turn_x(t):
                pe.wait_ge(x_scaled, t + 1)
                for k in range(KD):
                    ins = tr(banks(6 if t == 0 else 1)[:, k * P:(k + 1) * P], xh[:, t % 2, k * P:(k + 1) * P])
                ins.then_inc(x_turned, 1)

            def turn_sums(o, sums):
                for k in range(o.shape[1] // P):
                    ins = tr(o[:, k * P:(k + 1) * P], sums[:, k * P:(k + 1) * P])
                return ins

            def project(o, a, b, t, u=False):
                for k in range(KD):
                    if u and k % 4 == 0:
                        pe.wait_ge(h_lo, 2 * t + k // 4 + 1)
                    if t == 0 and u:
                        pe.wait_ge(wu_lo, k // 2 + 1)
                    if t == 0 and not u:
                        pe.wait_ge(wqkv_lo, k + 1)
                    ins = three(o, hTh[:, k, :], hTl[:, k, :], wih[:, k, a:b], wil[:, k, a:b], k == 0, k == KD - 1)
                return ins

            def turn_p(i, kv):
                pe.wait_ge(normed, 2 * i + kv + 1)
                if kv:
                    pe.wait_ge(pT_lo, 2 * i + 1)
                else:
                    pe.wait_ge(exped, 2 * i + 2)
                for blk in range(1 if i == 0 else 2):
                    for h in range(G):
                        ins = tr(psum[:, 4 + blk, h * P:(h + 1) * P], pr[:, kv, h, blk * P:(blk + 1) * P])
                ins.then_inc(p_turned, 1)

            def attend(i, kv):
                pe.wait_ge(pT_lo, 2 * i + kv + 1)
                pe.wait_ge(v_lo, i + 1)
                blocks = [i % 2] if i == 0 else [i % 2, (i - 1) % 2]
                for n, blk in enumerate(blocks):
                    s = (i - n) % 4
                    vh, vl = (vv[:, s, kv, a, :, :].rearrange("p b d -> p (b d)") for a in range(2))
                    ph, pl = (a[:, blk, :, :].rearrange("p h q -> p (h q)") for a in (pTh, pTl))
                    ins = three(bank(0), vh, vl, ph, pl, n == 0, n == len(blocks) - 1)
                ins.then_inc(pv_done, 1)

            def score(i, kv):
                if kv:
                    pe.wait_ge(exped, 2 * i + 1)
                elif i >= 1:
                    pe.wait_ge(pT_lo, 2 * i)
                for h in range(G):
                    w = P if i == 0 else 2 * P
                    o = psum[:, 4 + h // 2, (h % 2) * 256:(h % 2) * 256 + w]
                    m0 = P if i % 2 == 0 else 0
                    mm(o, identr[:, :], maskr[:, m0:m0 + w], start=True, stop=False)
                    for a in range(2):
                        if i == 0:
                            k_ = kT[:, kv, a, 0, :]
                        else:
                            k_ = kT[:, kv, a, :, :].rearrange("p b n -> p (b n)")
                        ins = mm(o, qT[:, kv * G + h, :], k_, start=False, stop=a == 1)
                ins.then_inc(scored, 1)

            def project_u(t):
                if t >= 3:
                    pe.wait_ge(attn_kept, 2 * (t - 2))
                project(bank(0), QKV, IN, t, u=True).then_inc(u_done, 1)

            def pool_out(i):
                if i == 0:
                    pe.wait_ge(poolw_ready, 1)
                pe.wait_ge(pooled_kept, i + 1)
                for j in range(NP):
                    ins = mm(psum[:, 7, j * P:(j + 1) * P], poolw[:, j, :], pooledT[:, j * P:(j + 1) * P],
                             start=True, stop=True)
                ins.then_inc(pout_done, 1)

            def turn_qk(i):
                pe.wait_ge(qk_lo, i + 1)
                for h in range(NH):
                    ins = tr(banks(1)[:, h * P:(h + 1) * P], q2[:, h, :, :].rearrange("p a d -> p (a d)"))
                ins.then_inc(q_turned, 1)
                pe.wait_ge(v_lo, i + 1)
                for e in range(NKV):
                    for a in range(2):
                        ins = tr(psum[:, 3, (2 * e + a) * P:(2 * e + a + 1) * P],
                                 k2[:, e, a, :, :].rearrange("p b d -> p (b d)"))
                ins.then_inc(k_turned, 1)

            def pool_windows(t):
                pe.wait_ge(u_kept, t + 1)
                if t < 2:
                    pe.wait_ge(consts_made, t + 1)
                if t >= 1:
                    pe.wait_ge(pout_kept, t)
                for j in range(NP):
                    o = psum[:, 7, j * P:(j + 1) * P]
                    ins = mm(o, usb[:, t % 2, j * P:(j + 1) * P], bandc[:, j, :], start=True, stop=t == 0)
                    if t >= 1:
                        ins = mm(o, usb[:, (t - 1) % 2, j * P:(j + 1) * P], bandp[:, j, :], start=False, stop=True)
                ins.then_inc(band_done, 1)

            pe.wait_ge(ident_made, 2)
            turn_x(0)
            pe.wait_ge(params_in, 16 * 9)
            pe.wait_ge(posf_ready, 1)
            tr(psum[:, 4, 0:72], rows[0:72, :], 72).then_inc(rows_turned, 1)
            pe.wait_ge(mod_summed, KD)
            turn_sums(banks(0), acc).then_inc(mod_turned, 1)
            for h in range(2):
                pe.wait_ge(mod_summed, 2 * KD + h)
                turn_sums(bank(2 + h), acc_sc[:, 512 * h:512 * h + 512]).then_inc(sc1_turned, 1)
            for t in range(NT):
                project_u(t)
                if t in (2, 4):
                    pe.wait_ge(job_summed, 4 * t)
                    turn_sums(banks(1), acc).then_inc(mod_turned, 1)
                if t >= 2:
                    score(t - 2, 1)
                if t >= 1:
                    pool_out(t - 1)
                if t in (2, 4):
                    pe.wait_ge(mod_taken, t // 2 + 1)
                if t >= 1:
                    turn_qk(t - 1)
                if t >= 1:
                    pe.wait_ge(q_normed, t)
                project(bank(6), 0, AW, t).then_inc(q_done, 1)
                if t + 1 < NT:
                    if t >= 1:
                        pe.wait_ge(qT_kept, t)
                    turn_x(t + 1)
                if t >= 2:
                    turn_p(t - 2, 0)
                if t >= 1:
                    pe.wait_ge(kT_kept, t)
                project(psum[:, 3, 0:2 * KVW], AW, QKV, t).then_inc(kv_done, 1)
                if t >= 2:
                    pe.wait_ge(u_kept, t + 1)
                    attend(t - 2, 0)
                    turn_p(t - 2, 1)
                pool_windows(t)
                if t >= 2:
                    pe.wait_ge(attn_kept, 2 * (t - 2) + 1)
                    attend(t - 2, 1)
                if t >= 1:
                    pe.wait_ge(qT_kept, t)
                    pe.wait_ge(kT_kept, t)
                    if t == 1:
                        pe.wait_ge(mask_ready, 2)
                    score(t - 1, 0)

            def project_out(i, k):
                pair = 1 if i % 2 else 6
                if k == 0:
                    if i >= 2:
                        pe.wait_ge(x2_gated, i - 1)
                    elif i == 1:
                        pe.wait_ge(mod_taken, 4)
                    else:
                        pe.wait_ge(q_normed, NT)
                        pe.wait_ge(pout_kept, NT)
                if i == 0:
                    pe.wait_ge(wo_lo_dve if k % 2 else wo_lo_pool, k // 2 + 1)
                if k % 4 == 0:
                    pe.wait_ge(mix_lo, 2 * i + k // 4 + 1)
                for n in range(2):
                    ins = three(bank(pair + n), mTh[:, k, :], mTl[:, k, :], woh[:, k, 512 * n:512 * n + 512],
                                wol[:, k, 512 * n:512 * n + 512], k == 0, k == KD - 1)
                if k % 4 == 3:
                    ins.then_inc(wo_used, 1)

            def project_out_half(i, h):
                for k in range(4 * h, 4 * h + 4):
                    project_out(i, k)

            def turn_x2(i, h):
                if h == 0:
                    pe.wait_ge(x2_scaled, i + 1)
                if i == NT - 1:
                    pe.wait_ge(pT_lo, 2 * NT)
                elif i == 0 and h == 0:
                    pe.wait_ge(kT_kept, NT)
                else:
                    pe.wait_ge(h2_made, 2 * i + h)
                for j in range(4):
                    k = 4 * h + j
                    ins = tr(bank(4 + h if i == NT - 1 else 3)[:, j * P:(j + 1) * P], hx[:, k * P:(k + 1) * P])
                ins.then_inc(x2_turned, 1)

            def gate_rows(pair):
                for n in range(2):
                    ins = mm(bank(pair + n), ones[:, :], acc[:, 512 * n:512 * n + 512], start=True, stop=True)
                ins.then_inc(mod_turned, 1)

            def attend_late(i, kv):
                pe.wait_ge(attn_kept, 2 * i + kv)
                attend(i, kv)

            pool_out(NT - 1)
            score(NT - 2, 1)
            turn_qk(NT - 1)
            project_out_half(0, 0)
            turn_p(NT - 2, 0)
            pe.wait_ge(qT_kept, NT)
            pe.wait_ge(gate_biased, 1)
            gate_rows(1)
            project_out_half(0, 1)
            attend_late(NT - 2, 0)
            turn_p(NT - 2, 1)
            project_out_half(1, 0)
            attend_late(NT - 2, 1)
            pe.wait_ge(kT_kept, NT)
            score(NT - 1, 0)
            project_out_half(1, 1)
            turn_x2(0, 0)
            score(NT - 1, 1)
            turn_x2(0, 1)
            project_out_half(2, 0)
            turn_p(NT - 1, 0)
            project_out_half(2, 1)
            turn_x2(1, 0)
            attend_late(NT - 1, 0)
            turn_p(NT - 1, 1)
            turn_x2(1, 1)
            project_out_half(3, 0)
            attend_late(NT - 1, 1)
            project_out(3, 4)
            project_out(3, 5)
            turn_x2(2, 0)
            project_out(3, 6)
            project_out(3, 7)
            turn_x2(2, 1)
            for i in range(4, NT):
                project_out_half(i, 0)
                project_out(i, 4)
                project_out(i, 5)
                turn_x2(i - 1, 0)
                project_out(i, 6)
                project_out(i, 7)
                turn_x2(i - 1, 1)

            def mlp_block(b, first):
                for u in range(2 * NF):
                    f, n = u % NF, u // NF
                    if first:
                        if u == 0:
                            pe.wait_ge(attn_kept, 2 * NT)
                            pe.wait_ge(h2_lo, NT)
                        if u == 1:
                            pe.wait_ge(x2_gated, NT)
                        if u == NF:
                            pe.wait_ge(h2_lo, 2 * NT)
                        if u == 3:
                            pe.wait_ge(h2_made, 2 * (NT - 1))
                    else:
                        pe.wait_ge(relu_kept, 2 * NF * (b - 1) + u + 1)
                    for k in range(KD):
                        if first and u == 1 and k == 4:
                            turn_x2(NT - 1, 0)
                            turn_x2(NT - 1, 1)
                            pe.wait_ge(gate_biased, 2)
                            gate_rows(6)
                        if u == 0 and k % 4 == 0:
                            pe.wait_ge(w1_lo, 2 * b + k // 4 + 1)
                        ins = three(bank(u).rearrange("p (i s) -> p i s", s=P),
                                    w1h[:, k, f * P:(f + 1) * P], w1l[:, k, f * P:(f + 1) * P],
                                    h2T[:, 4 * n:4 * n + 4, 0, k, :], h2T[:, 4 * n:4 * n + 4, 1, k, :],
                                    k == 0, k == KD - 1)
                    ins.then_inc(up_done, 1)
                for n in range(2 * NT):
                    i, half = n // 2, n % 2
                    cut = slice(512 * half, 512 * half + 512)
                    if n == 0:
                        pe.wait_ge(act_lo, 2 * NF * b + NF)
                        pe.wait_ge(w2_lo, 2 * b + 2)
                    if n == NT:
                        pe.wait_ge(act_lo, 2 * NF * b + 2 * NF)
                    if first and n < 4:
                        if n == 0:
                            pe.wait_ge(mod_taken, 5)
                            pe.wait_ge(h2_made, 2 * NT)
                    else:
                        pe.wait_ge(added, 2 * NT * b + n - 3)
                    for f in range(NF):
                        ins = three(bank(4 + n % 4), aTh[:, f, i * P:(i + 1) * P], aTl[:, f, i * P:(i + 1) * P],
                                    w2h[:, f, cut], w2l[:, f, cut], f == 0, f == NF - 1)
                    ins.then_inc(down_done, 1)

            mlp_block(0, True)
            with pe.Fori(1, NB) as b:
                mlp_block(b, False)


_INS = ["x", "c", "positions", "w_ada", "b_ada", "norm1_g", "w_in", "q_norm_g", "k_norm_g", "attn_sinks",
        "pool_w", "pool_scale", "w_o", "norm2_g", "w_mlp_in", "w_mlp_out"]


def kernel(**inputs):
    import concourse.bacc as bacc
    from concourse.bass_utils import run_bass_kernel_spmd

    nc = bacc.Bacc("TRN2", target_bir_lowering=False, num_devices=1)
    arrays, args = {}, []
    for name in _INS:
        a = np.ascontiguousarray(inputs[name])
        arrays[f"in_{name}"] = a
        args.append(nc.dram_tensor(f"in_{name}", a.shape, mybir.dt.from_np(a.dtype), kind="ExternalInput").ap())
    shape = inputs["x"].shape
    result = nc.dram_tensor("out_0", shape, F32, kind="ExternalOutput").ap()
    build(nc, *args, result)
    r = run_bass_kernel_spmd(nc, [arrays], core_ids=[0])
    return r.results[0]["out_0"]
```

```python
from contextlib import ExitStack

import concourse.bass as bass
import numpy as np
from concourse import mybir

P = 128
F32 = mybir.dt.float32
F32R = mybir.dt.float32r
BF16 = mybir.dt.bfloat16
I32 = mybir.dt.int32
ALU = mybir.AluOpType
ACT = mybir.ActivationFunctionType
AX_X = mybir.AxisListType.X

HEAD_DIM = 64
POOL_WINDOWS = (2, 4, 8, 16)
ROT_DIM = HEAD_DIM // 4
HALF = ROT_DIM // 2
ROPE_THETA = 500000.0
EPS = 1e-6
MAX_WINDOW = max(POOL_WINDOWS)
MASKED = -1e30
FB = 256
RING = 4
SH1, SC1, G1, SH2, SC2, G2 = range(6)

TWO_PI_1 = 6.28125
TWO_PI_2 = 0.0019350051879882812
TWO_PI_3 = 2 * np.pi - TWO_PI_1 - TWO_PI_2
ROUND_MAGIC = 12582912.0
PI_LIMIT = 3.1415925


def bcast(ap, axis, n):
    a = ap.unsqueeze(axis)
    shape = list(a.shape)
    shape[axis] = n
    return a.to_broadcast(shape)


def build(nc, x, c, positions, w_ada, b_ada, norm1_g, w_in, q_norm_g, k_norm_g, attn_sinks,
          pool_w, pool_scale, w_o, norm2_g, w_mlp_in, w_mlp_out, out):
    S, D = x.shape[1], x.shape[2]
    IN = w_in.shape[2]
    FF = w_mlp_in.shape[2]
    NH = attn_sinks.shape[1]
    PW = pool_scale.shape[1]
    AW = NH * HEAD_DIM
    KVW = (IN - AW - PW) // 2
    NKV = KVW // HEAD_DIM
    G = NH // NKV
    NP = pool_w.shape[1]
    NT = S // P
    KD = D // P
    NB = FF // FB
    NF = FB // P
    BAND = P + MAX_WINDOW
    NHD = NH + 2 * NKV
    QKV = AW + 2 * KVW
    SCALE = HEAD_DIM ** -0.5
    assert NT == 8 and KD == 8 and G == 4 and NKV == 2 and NP == 4 and D == 1024

    x_rows = x[0]
    out_rows = out[0]
    wada = w_ada[0].rearrange("(p k) n -> p k n", k=KD)
    win = w_in[0].rearrange("(k p) n -> p k n", p=P)
    wo = w_o[0].rearrange("(k p) n -> p k n", p=P)
    w1 = w_mlp_in[0].rearrange("(k p) n -> p k n", p=P)
    w2 = w_mlp_out[0]

    with ExitStack() as ctx:
        def sem(name):
            return ctx.enter_context(nc.semaphore(name))

        def sb(name, shape, dt=F32):
            return ctx.enter_context(nc.sbuf_tensor(name, shape, dt))

        ident = sb("ident", [P, P])
        ones = sb("ones", [P, P])
        small = sb("small", [P, 256])
        cols = sb("cols", [P, 72])
        a1, b1, a2, b2 = (small[:, 8 * j:8 * j + 8] for j in range(4))
        silu = small[:, 32:40]
        ctmp = small[:, 40:48]
        ssx = small[:, 48:56]
        rx = small[:, 56:64]
        ss2 = small[:, 64:72]
        r2 = small[:, 72:80]
        ssq = small[:, 80:90]
        rq = small[:, 90:100]
        sink = small[:, 100:108]
        nsink = small[:, 108:116]
        negm = small[:, 116:124]
        earg = small[:, 124:132]
        es = small[:, 132:140]
        den = small[:, 140:148]
        rden = small[:, 148:156]
        mx = small[:, 156:164]
        mhalf = small[:, 164:174]
        slots = sb("slots", [P, NT, D])
        raw = sb("raw", [P, RING, 1024])
        acc = sb("acc", [P, D])

        with ExitStack() as mix_ctx:
            def mb(name, shape, dt=F32):
                return mix_ctx.enter_context(nc.sbuf_tensor(name, shape, dt))
            wih = mb("w_in_hi", [P, KD, IN], F32R)
            wil = mb("w_in_lo", [P, KD, IN], F32R)
            xh = mb("xh", [P, 2, D])
            hTh = mb("hT_hi", [P, KD, P], F32R)
            hTl = mb("hT_lo", [P, KD, P], F32R)
            qkn = mb("qkn", [P, NHD, HEAD_DIM])
            squares = mb("squares", [P, D])
            qT = mb("qT", [P, NH, P], F32R)
            kT = mb("kT", [P, NKV, 2, 2, P], F32R)
            vv = mb("vv", [P, 4, NKV, 2, HEAD_DIM], F32R)
            pr = mb("probs", [P, NKV, G, 2 * P])
            pTh = mb("pT_hi", [P, NKV, 2, G, P], F32R)
            pTl = mb("pT_lo", [P, NKV, 2, G, P], F32R)
            usb = mb("u_rows", [P, 2, PW])
            pooledT = mb("pooledT", [P, PW])
            poolw = mb("pool_w", [P, NP, P])
            band = mb("band", [P, NP, BAND])
            carry = mb("carry", [P, NP, MAX_WINDOW])
            mask = mb("mask", [P, 3 * P])
            gqk = mb("gqk", [P, 2, HEAD_DIM])
            trig = mb("trig", [P, NT, 4, HALF])
            rot = squares[:, AW + KVW:D].rearrange("p (j h a f) -> p j h a f", j=2, a=2, f=HALF)
            junk = pooledT[:, :].bitcast(BF16)

        with ExitStack() as out_ctx:
            def ob(name, shape, dt=F32):
                return out_ctx.enter_context(nc.sbuf_tensor(name, shape, dt))
            woh = ob("w_o_hi", [P, KD, D], F32R)
            wol = ob("w_o_lo", [P, KD, D], F32R)
            g1b = ob("g1_rows", [P, D])
            mTh = ob("mixT_hi", [P, KD, P], F32R)
            mTl = ob("mixT_lo", [P, KD, P], F32R)
            hx = ob("hx", [P, D])
        with ExitStack() as mlp_ctx:
            def lb(name, shape, dt=F32):
                return mlp_ctx.enter_context(nc.sbuf_tensor(name, shape, dt))
            w1h = lb("w1_hi", [P, KD, FB], F32R)
            w1l = lb("w1_lo", [P, KD, FB], F32R)
            w2h = lb("w2_hi", [P, NF, D], F32R)
            w2l = lb("w2_lo", [P, NF, D], F32R)
            aTh = lb("aT_hi", [P, NF, S], F32R)
            aTl = lb("aT_lo", [P, NF, S], F32R)
            relu = lb("relu", [P, 2, 512])
            rsq = lb("relu_squared", [P, 2, 512])
        over_w_in = 2 * KD * IN
        sb("w_in_place", [P, over_w_in])
        h2T = sb("h2T", [P, NT, 2, KD, P], F32R)
        junk2 = sb("junk2", [P, D], BF16)
        g2b = sb("g2_rows", [P, D])

        psum = ctx.enter_context(nc.psum_tensor("psum", [P, 8, 512], F32))

        windows = psum[:, 1:3, 0:2 * BAND].rearrange("p b (g s) -> p b g s", s=BAND)

        def bank(j):
            return psum[:, j, :]

        def banks(j):
            return psum[:, j:j + 2, :].rearrange("p b n -> p (b n)")

        stream = [("sh1", k) for k in range(KD)]
        stream += [("sc1", k) for k in range(KD)]
        stream += [("wu", k) for k in range(KD // 2)]
        stream += [("wqkv", k) for k in range(KD)]
        EARLY = len(stream)
        WIDE = RING + NT
        for job in ("sh2", "sc2", "g1"):
            stream += [(job, k) for k in range(KD)]
        stream += [("wo", k) for k in range(KD)]
        for k in range(KD):
            stream += [("x", k), ("g2", k)]
        stream += [("w1", 0), ("w1", 1), ("w2", 0), ("w2", 1)]
        place = {piece: n for n, piece in enumerate(stream)}
        assert EARLY % WIDE == RING and (len(stream) - EARLY) % RING == 0
        EARLY_USE = EARLY // WIDE + 1
        MLP_USE = EARLY_USE + (len(stream) - 4 - EARLY) // RING
        WO_POOL, WO_DVE = (0, 5, 6), (1, 2, 3, 4, 7)
        adaln_jobs = ("sh2", "sc2", "g1", "g2")
        mod_of = {"sh1": SH1, "sc1": SC1, "g1": G1, "sh2": SH2, "sc2": SC2, "g2": G2}

        def buffer_of(n):
            if n < EARLY:
                return n % WIDE, n // WIDE + 1, n - WIDE
            m = n - EARLY
            return m % RING, EARLY_USE + m // RING + 1, n - RING

        def piece_at(n):
            s = buffer_of(n)[0]
            return raw[:, s, :] if s < RING else slots[:, s - RING, :]

        raw_in = [sem(f"raw_in{s}") for s in range(WIDE)]
        c_in, params_in = sem("c_in"), sem("params_in")
        x_in = [sem("x_in0"), sem("x_in1")]
        out_done = sem("out_done")
        ident_made = sem("ident_made")
        rows_turned = sem("rows_turned")
        cols_ready = sem("cols_ready")
        exp_c = sem("exp_c")
        angles_ready = sem("angles_ready")
        trig_ready = sem("trig_ready")
        consts_made = sem("consts_made")
        poolw_ready = sem("poolw_ready")
        posf_ready = sem("posf_ready")
        mask_ready = sem("mask_ready")
        mod_summed = sem("mod_summed")
        job_summed = sem("job_summed")
        gate_biased = sem("gate_biased")
        mod_turned = sem("mod_turned")
        sc1_turned = sem("sc1_turned")
        mod_taken = sem("mod_taken")
        wu_hi, wu_lo = sem("wu_hi"), sem("wu_lo")
        wqkv_hi, wqkv_lo = sem("wqkv_hi"), sem("wqkv_lo")
        wo_hi = sem("wo_hi")
        wo_lo_pool, wo_lo_dve = sem("wo_lo_pool"), sem("wo_lo_dve")
        x_squared, x_root, x_scaled = sem("x_squared"), sem("x_root"), sem("x_scaled")
        x_turned = sem("x_turned")
        h_made, h_hi, h_lo = sem("h_made"), sem("h_hi"), sem("h_lo")
        u_done, u_kept = sem("u_done"), sem("u_kept")
        band_done, pooled_kept, pout_done, pout_kept = sem("band_done"), sem("pooled_kept"), sem("pout_done"), sem("pout_kept")
        carry_added, carry_kept = sem("carry_added"), sem("carry_kept")
        q_done, kv_done = sem("q_done"), sem("kv_done")
        q_squared, kv_squared, qk_sums, qk_root = sem("q_squared"), sem("kv_squared"), sem("qk_sums"), sem("qk_root")
        q_normed, k_normed, qk_roped = sem("q_normed"), sem("k_normed"), sem("qk_roped")
        qk_turned, qk_hi, qk_lo = sem("qk_turned"), sem("qk_hi"), sem("qk_lo")
        v_hi, v_lo = sem("v_hi"), sem("v_lo")
        scored, max_ready, exped, den_ready, normed = (sem("scored"), sem("max_ready"), sem("exped"),
                                                       sem("den_ready"), sem("normed"))
        p_turned, pT_hi, pT_lo, pv_done, attn_kept = (sem("p_turned"), sem("pT_hi_ready"), sem("pT_lo_ready"),
                                                      sem("pv_done"), sem("attn_kept"))
        attn_shifted = sem("attn_shifted")
        mix_hi, mix_lo = sem("mix_hi"), sem("mix_lo")
        wo_used = sem("wo_used")
        x2_gated = sem("x2_gated")
        x2_ready, x2_squared, x2_root, x2_scaled = sem("x2_ready"), sem("x2_squared"), sem("x2_root"), sem("x2_scaled")
        x2_turned, h2_made, h2_hi, h2_lo = sem("x2_turned"), sem("h2_made"), sem("h2_hi"), sem("h2_lo")
        w1_hi, w1_lo = sem("w1_hi_ready"), sem("w1_lo_ready")
        w2_gated, w2_hi, w2_lo = sem("w2_gated"), sem("w2_hi_ready"), sem("w2_lo_ready")
        up_done, relu_kept, act_hi, act_sq, act_lo = (sem("up_done"), sem("relu_kept"), sem("act_hi"), sem("act_sq"),
                                                      sem("act_lo"))
        down_done, added = sem("down_done"), sem("added")
        own = {e: sem(f"own_{e}") for e in ("act", "dve", "pool")}

        block = ctx.enter_context(nc.Block())

        def attn_bank(i, kv):
            return bank(7) if kv == 0 and i < NT - 2 else bank(0)

        def p_blocks(i, kv, blk=None):
            if blk is None:
                blk = 0 if i == 0 else 1
            return (kv if i == 0 else 2 * (2 * i + kv) - 2) + blk + 1

        class Chain:

            def __init__(self, eng, s, base=0):
                self.eng, self.s, self.n, self.base = eng, s, 0, base

            def step(self, ins):
                ins.then_inc(self.s, 1)
                self.n += 1

            def wait(self):
                self.eng.wait_ge(self.s, self.base + self.n)

        def landed(eng, piece):
            n = place[piece]
            buf, use, _ = buffer_of(n)
            eng.wait_ge(raw_in[buf], 16 * use)
            return piece_at(n)

        def wo_lo_made(eng, k):
            if k in WO_DVE:
                eng.wait_ge(wo_lo_dve, WO_DVE.index(k) + 1)
            else:
                eng.wait_ge(wo_lo_pool, WO_POOL.index(k) + 1)

        def freed(eng, n):
            before = buffer_of(n)[2]
            if before < 0:
                return
            kind, k = stream[before]
            if kind in ("sh1", "sc1"):
                eng.wait_ge(mod_summed, k + 1 + (KD if kind == "sc1" else 0) + (kind == "sc1" and k == KD - 1))
            elif kind in adaln_jobs:
                eng.wait_ge(job_summed, KD * adaln_jobs.index(kind) + k + 1)
            elif kind == "x":
                eng.wait_ge(x2_ready, k + 1)
            elif kind == "wo":
                wo_lo_made(eng, k)
            else:
                eng.wait_ge({"wu": wu_lo, "wqkv": wqkv_lo}[kind], k + 1)

        def source(kind, k):
            if kind == "wu":
                return win[:, 2 * k:2 * k + 2, QKV:IN]
            if kind == "wqkv":
                return win[:, k, 0:QKV]
            if kind == "wo":
                return wo[:, k, :]
            if kind == "x":
                return x_rows[k * P:(k + 1) * P, :]
            if kind == "w1":
                return w1[:, 4 * k:4 * k + 4, 0:FB]
            if kind == "w2":
                return w2[k * P:(k + 1) * P, :]
            m = mod_of[kind]
            return wada[:, k, m * D:(m + 1) * D]

        def target(kind, a):
            if kind == "wu":
                return a.rearrange("p (k n) -> p k n", k=2)
            if kind == "wqkv":
                return a[:, 0:QKV]
            if kind == "w1":
                return a.rearrange("p (k n) -> p k n", k=4)
            return a

        rows = pr[:, 0, :, :].rearrange("p h n -> p (h n)")[:, 0:P]
        posi = pr[:, 1, :, :].rearrange("p h n -> p (h n)")[:, 0:P].bitcast(I32)
        scale_row = pr[:, 1, :, :].rearrange("p h n -> p (h n)")[:, 512:1024]
        cin = small[:, 192:200]
        acc_sc = squares[:, :]
        ang = pr[:, 0, :, :].rearrange("p h n -> p (h n)")[:, 2 * P:4 * P]
        ANG = NT * HALF

        @block.sync
        def _(sp):
            def load(n):
                kind, k = stream[n]
                freed(sp, n)
                sp.dma_start(target(kind, piece_at(n)), source(kind, k)).then_inc(raw_in[buffer_of(n)[0]], 16)

            def load_x(t):
                if t >= 2:
                    sp.wait_ge(h_lo, 2 * (t - 1))
                sp.dma_start(xh[:, t % 2, :], x_rows[t * P:(t + 1) * P, :]).then_inc(x_in[t % 2], 16)

            sp.dma_start(cin, c[0].rearrange("(p k) -> p k", k=KD)).then_inc(c_in, 16)
            first_job = place[("sh2", 0)]
            for n in range(first_job):
                load(n)
                if n == 7:
                    load_x(0)
            for t in range(NT):
                if t + 1 < NT:
                    load_x(t + 1)
                if t < 6:
                    for j in range(4):
                        load(first_job + 4 * t + j)
            for n in range(place[("wo", 0)], len(stream)):
                load(n)
            with sp.Fori(1, NB) as b:
                for j in range(2):
                    sp.wait_ge(w1_lo, 2 * b + j - 1)
                    sp.dma_start(target("w1", raw[:, j, :]), w1[:, 4 * j:4 * j + 4, bass.ds(b * FB, FB)]).then_inc(raw_in[j], 16)
                for j in range(2):
                    sp.wait_ge(w2_lo, 2 * b + j - 1)
                    sp.dma_start(target("w2", raw[:, 2 + j, :]), w2[bass.ds(b * FB + j * P, P), :]).then_inc(raw_in[2 + j], 16)
            for i in range(NT):
                for h in range(2):
                    cut = slice(512 * h, 512 * h + 512)
                    sp.wait_ge(added, 16 * (NB - 1) + 2 * i + h + 1)
                    sp.dma_start(out_rows[i * P:(i + 1) * P, cut], slots[:, i, cut]).then_inc(out_done, 16)
            sp.wait_ge(out_done, 16 * 2 * NT)

        @block.scalar
        def _(act):
            act.wait_ge(c_in, 16)
            nc.scalar.activation(ctmp, cin, ACT.Exp, scale=-1.0).then_inc(exp_c, 1)
            act.dma_start(rows[0:48, :], b_ada[0].rearrange("(j p) -> j p", p=P)).then_inc(params_in, 16)
            act.dma_start(rows[48:56, :], norm1_g[0].rearrange("(j p) -> j p", p=P)).then_inc(params_in, 16)
            act.dma_start(rows[56:64, :], norm2_g[0].rearrange("(j p) -> j p", p=P)).then_inc(params_in, 16)
            act.dma_start(posi[64:72, :], positions[0].rearrange("(j p) -> j p", p=P)).then_inc(params_in, 16)
            act.dma_start(scale_row, pool_scale.to_broadcast([P, PW])).then_inc(params_in, 16)
            act.dma_start(poolw[:, :, :], pool_w[0].rearrange("g c d -> c g d")).then_inc(params_in, 16)
            act.dma_start(gqk[:, 0, :], q_norm_g.to_broadcast([P, HEAD_DIM])).then_inc(params_in, 16)
            act.dma_start(gqk[:, 1, :], k_norm_g.to_broadcast([P, HEAD_DIM])).then_inc(params_in, 16)
            act.dma_start(sink, attn_sinks.to_broadcast([P, NH])).then_inc(params_in, 16)
            def square_x(t):
                act.wait_ge(x_in[t % 2], 16 * (t // 2 + 1))
                if t >= 1:
                    act.wait_ge(x_squared, t)
                nc.scalar.activation(junk, xh[:, t % 2, :], ACT.Square,
                                     accum_out=ssx[:, t:t + 1]).then_inc(x_squared, 1)

            def scale_x(t):
                act.wait_ge(x_root, t + 1)
                nc.scalar.activation(xh[:, t % 2, :], xh[:, t % 2, :], ACT.Copy,
                                     scale=rx[:, t:t + 1]).then_inc(x_scaled, 1)

            def hi_h(t):
                if t >= 1:
                    act.wait_ge(kv_done, t)
                for h in range(2):
                    if t == 0 and h == 1:
                        hi_wu(3)
                    act.wait_ge(h_made, 2 * t + h + 1)
                    nc.scalar.copy(hTh[:, 4 * h:4 * h + 4, :], xh[:, t % 2, 512 * h:512 * h + 512]
                                   .rearrange("p (k n) -> p k n", n=P)).then_inc(h_hi, 1)

            def hi_wu(j):
                a = landed(act, ("wu", j))
                nc.scalar.copy(wih[:, 2 * j:2 * j + 2, QKV:IN], a.rearrange("p (k n) -> p k n", k=2)).then_inc(wu_hi, 1)

            square_x(0)
            scale_x(0)
            hi_wu(0)
            hi_wu(1)
            hi_wu(2)
            hi_h(0)
            for k in range(KD):
                a = landed(act, ("wqkv", k))
                nc.scalar.copy(wih[:, k, 0:QKV], a[:, 0:QKV]).then_inc(wqkv_hi, 1)

            def hi_pT(i, kv):
                act.wait_ge(p_turned, 2 * i + kv + 1)
                if i >= 1:
                    act.wait_ge(pv_done, 2 * i + kv - 1)
                for blk in range(1 if i == 0 else 2):
                    nc.scalar.copy(pTh[:, kv, blk, :, :].rearrange("p h q -> p (h q)"), bank(4 + blk)).then_inc(pT_hi, 1)

            def shift_attn(i, kv):
                act.wait_ge(pv_done, 2 * i + kv + 1)
                o = attn_bank(i, kv).rearrange("p (m e q) -> p m e q", e=2, q=P)
                dst = slots[:, i, :].rearrange("p (m q) -> p m q", q=P)
                for e in range(2):
                    ins = nc.scalar.copy(dst[64 * e:64 * e + 64, 2 * kv:2 * kv + 2, :],
                                         o[64 - 64 * e:128 - 64 * e, :, e, :])
                ins.then_inc(attn_shifted, 1)

            def exps(i, kv):
                act.wait_ge(max_ready, 2 * i + kv + 1)
                w = P if i == 0 else 2 * P
                for h in range(G):
                    hh = kv * G + h
                    nc.scalar.activation(pr[:, kv, h, 0:w], pr[:, kv, h, 0:w], ACT.Exp,
                                         bias=negm[:, hh:hh + 1], scale=SCALE, accum_out=den[:, hh:hh + 1])
                nc.scalar.activation(es[:, kv * G:kv * G + G], earg[:, kv * G:kv * G + G], ACT.Exp).then_inc(exped, 1)

            def hi_qk(i):
                act.wait_ge(qk_turned, i + 1)
                if i >= 1:
                    act.wait_ge(scored, 2 * i)
                for e in range(2):
                    r = slice(64 * e, 64 * e + 64)
                    nc.scalar.copy(qT[r, :, :].rearrange("p (m e) q -> p m e q", e=2)[:, :, e, :],
                                   bank(1)[r, :].rearrange("p (m q) -> p m q", q=P))
                nc.scalar.copy(kT[:, :, 0, i % 2, :],
                               psum[:, 2, 0:NKV * P].rearrange("p (g n) -> p g n", g=NKV)).then_inc(qk_hi, 1)

            def keep_pout(i):
                act.wait_ge(pout_done, i + 1)
                nc.scalar.copy(slots[:, i, D - PW:D], bank(7)).then_inc(pout_kept, 1)

            def hi_wo(k):
                a = landed(act, ("wo", k))
                nc.scalar.copy(woh[:, k, :], a).then_inc(wo_hi, 1)

            def hi_mix(i, h):
                if h == 0:
                    act.wait_ge(attn_kept, 2 * i + 2)
                else:
                    act.wait_ge(pout_kept, i + 1)
                if i >= 1:
                    act.wait_ge(wo_used, 2 * (i - 1) + h + 1)
                nc.scalar.copy(mTh[:, 4 * h:4 * h + 4, :],
                               slots[:, i, 512 * h:512 * h + 512].rearrange("p (k n) -> p k n", n=P)).then_inc(mix_hi, 1)

            for t in range(NT):
                if t >= 2:
                    exps(t - 2, 0)
                act.wait_ge(u_done, t + 1)
                if t >= 2:
                    act.wait_ge(band_done, t - 1)
                nc.scalar.copy(usb[:, t % 2, :], bank(0)).then_inc(u_kept, 1)
                if t >= 1:
                    keep_pout(t - 1)
                if t + 1 < NT:
                    square_x(t + 1)
                if t >= 1:
                    hi_qk(t - 1)
                if t >= 2:
                    exps(t - 2, 1)
                if t + 1 < NT:
                    scale_x(t + 1)
                act.wait_ge(q_done, t + 1)
                if t >= 1:
                    act.wait_ge(qk_sums, t)
                nc.scalar.activation(squares[:, 0:AW], bank(6), ACT.Square).then_inc(q_squared, 1)
                if t >= 2:
                    hi_pT(t - 2, 0)
                act.wait_ge(kv_done, t + 1)
                nc.scalar.activation(squares[:, AW:AW + KVW], psum[:, 3, 0:KVW], ACT.Square).then_inc(kv_squared, 1)
                if t >= 4:
                    act.wait_ge(pv_done, 2 * (t - 2))
                nc.scalar.copy(vv[:, t % 4, :, 0, :],
                               psum[:, 3, KVW:2 * KVW].rearrange("p (g d) -> p g d", g=NKV)).then_inc(v_hi, 1)
                if t == NT - 1:
                    hi_mix(0, 0)
                if t >= 2:
                    hi_pT(t - 2, 1)
                    shift_attn(t - 2, 0)
                if t + 1 < NT:
                    hi_h(t + 1)
                else:
                    hi_wo(0)
                act.wait_ge(band_done, t + 1)
                act.wait_ge(x_squared, min(t + 2, NT))
                nc.scalar.copy(pooledT[:, :].rearrange("p (b g s) -> p b g s", b=2, s=P),
                               windows[:, :, :, 0:P]).then_inc(pooled_kept, 1)
                if t == 0:
                    act.wait_ge(angles_ready, 1)
                    nc.scalar.activation(trig[:, :, 1, :], ang[:, 0:ANG].rearrange("p (t f) -> p t f", f=HALF),
                                         ACT.Sin).then_inc(trig_ready, 1)
                    nc.scalar.activation(trig[:, :, 2, :], ang[:, 0:ANG].rearrange("p (t f) -> p t f", f=HALF),
                                         ACT.Sin).then_inc(trig_ready, 1)
                    nc.scalar.activation(trig[:, :, 0, :], ang[:, ANG:2 * ANG].rearrange("p (t f) -> p t f", f=HALF),
                                         ACT.Sin).then_inc(trig_ready, 1)
                    nc.scalar.activation(trig[:, :, 3, :], ang[:, ANG:2 * ANG].rearrange("p (t f) -> p t f", f=HALF),
                                         ACT.Sin).then_inc(trig_ready, 1)
                if t >= 2:
                    shift_attn(t - 2, 1)
            hi_wo(1)

            def square_x2(i):
                act.wait_ge(x2_ready, i + 1)
                if i >= 1:
                    act.wait_ge(x2_squared, i)
                nc.scalar.activation(junk2[:, :], slots[:, i, :], ACT.Square,
                                     accum_out=ss2[:, i:i + 1]).then_inc(x2_squared, 1)

            def scale_x2(i):
                act.wait_ge(x2_root, i + 1)
                if i >= 1:
                    act.wait_ge(h2_lo, 2 * i)
                nc.scalar.activation(hx[:, :], slots[:, i, :], ACT.Copy, scale=r2[:, i:i + 1]).then_inc(x2_scaled, 1)

            def hi_h2(i, h):
                act.wait_ge(h2_made, 2 * i + h + 1)
                nc.scalar.copy(h2T[:, i, 0, 4 * h:4 * h + 4, :],
                               hx[:, 512 * h:512 * h + 512].rearrange("p (k n) -> p k n", n=P)).then_inc(h2_hi, 1)

            keep_pout(NT - 1)
            hi_wo(2)
            hi_wo(3)
            hi_mix(0, 1)
            exps(NT - 2, 0)
            hi_wo(4)
            hi_qk(NT - 1)
            hi_wo(5)
            exps(NT - 2, 1)
            hi_wo(6)
            hi_pT(NT - 2, 0)
            hi_wo(7)
            hi_mix(1, 0)
            hi_mix(1, 1)
            shift_attn(NT - 2, 0)
            hi_pT(NT - 2, 1)
            square_x2(0)
            scale_x2(0)
            hi_mix(2, 0)
            shift_attn(NT - 2, 1)
            exps(NT - 1, 0)
            hi_mix(2, 1)
            hi_h2(0, 0)
            exps(NT - 1, 1)
            hi_h2(0, 1)
            square_x2(1)
            scale_x2(1)
            hi_pT(NT - 1, 0)
            hi_mix(3, 0)
            hi_mix(3, 1)
            shift_attn(NT - 1, 0)
            hi_h2(1, 0)
            hi_pT(NT - 1, 1)
            square_x2(2)
            hi_h2(1, 1)
            scale_x2(2)

            def hi_w1(b, use):
                for j in range(2):
                    act.wait_ge(raw_in[j], 16 * use)
                    nc.scalar.copy(w1h[:, 4 * j:4 * j + 4, :], raw[:, j, :].rearrange("p (k n) -> p k n", k=4)).then_inc(w1_hi, 1)

            def mlp_block(b, last):
                if not (isinstance(b, int) and b == 0):
                    act.wait_ge(down_done, 2 * NT * b)
                for j in range(2):
                    act.wait_ge(w2_gated, 2 * b + j + 1)
                    nc.scalar.copy(w2h[:, j, :], raw[:, 2 + j, :]).then_inc(w2_hi, 1)
                for u in range(2 * NF):
                    act.wait_ge(up_done, 2 * NF * b + u + 1)
                    relu_slot_free(act, b, u)
                    nc.scalar.activation(relu[:, u % 2, :], bank(u), ACT.Relu).then_inc(relu_kept, 1)
                    act.wait_ge(relu_kept, 2 * NF * b + u + 1)
                    nc.scalar.activation(aTh[:, u % NF, (u // NF) * 512:(u // NF) * 512 + 512], relu[:, u % 2, :],
                                         ACT.Square).then_inc(act_hi, 1)
                if not last:
                    act.wait_ge(up_done, 2 * NF * b + 2 * NF)
                    hi_w1(b + 1, MLP_USE + 2 + b)

            def relu_slot_free(eng, b, u):
                if isinstance(b, int) and 2 * NF * b + u - 2 < 0:
                    return
                eng.wait_ge(act_sq, 2 * NF * b + u - 1)

            for i in range(3, NT):
                if i + 1 < NT:
                    hi_mix(i + 1, 0)
                if i == 3:
                    shift_attn(NT - 1, 1)
                if i == NT - 1:
                    act.wait_ge(wo_used, 2 * NT - 1)
                    hi_w1(0, MLP_USE + 1)
                hi_h2(i - 1, 0)
                if i + 1 < NT:
                    hi_mix(i + 1, 1)
                hi_h2(i - 1, 1)
                square_x2(i)
                scale_x2(i)
            hi_h2(NT - 1, 0)
            hi_h2(NT - 1, 1)
            act.wait_ge(wo_used, 2 * NT)
            mlp_block(0, False)
            with act.Fori(1, NB - 1) as b:
                mlp_block(b, False)
            mlp_block(NB - 1, True)

        @block.vector
        def _(dve):
            own_d = Chain(dve, own["dve"])
            v = nc.vector
            v.memset(ones[:, :], 1.0).then_inc(ident_made, 1)
            dve.wait_ge(exp_c, 1)
            own_d.step(v.tensor_scalar(ctmp, ctmp, 1.0, None, ALU.add))
            own_d.wait()
            own_d.step(v.reciprocal(ctmp, ctmp))
            own_d.wait()
            own_d.step(v.tensor_tensor(silu, cin, ctmp, ALU.mult))
            own_d.wait()

            def add_piece(target_acc, piece, k, done):
                a = landed(dve, piece)
                if k == 0:
                    v.tensor_scalar(target_acc, a, silu[:, 0:1], None, ALU.mult).then_inc(done, 1)
                else:
                    v.scalar_tensor_tensor(out=target_acc, in0=a, scalar=silu[:, k:k + 1], in1=target_acc,
                                           op0=ALU.mult, op1=ALU.add).then_inc(done, 1)

            def angles():
                a0, a1_, a2_ = (ang[:, j * ANG:(j + 1) * ANG] for j in range(3))
                a3 = ang[:, 3 * ANG:4 * ANG]
                inv = (np.float32(ROPE_THETA) ** (-np.arange(0, ROT_DIM, 2, dtype=np.float32) / np.float32(ROT_DIM)))
                for f in range(HALF):
                    ins = v.tensor_scalar(a0.rearrange("p (t f) -> p t f", f=HALF)[:, :, f], cols[:, 64:72],
                                          float(inv[f]), None, ALU.mult)
                own_d.step(ins)
                own_d.wait()
                own_d.step(v.tensor_scalar(a1_, a0, float(1 / (2 * np.pi)), ROUND_MAGIC, ALU.mult, ALU.add))
                own_d.wait()
                own_d.step(v.tensor_scalar(a2_, a1_, -ROUND_MAGIC, None, ALU.add))
                own_d.wait()
                for part in (TWO_PI_1, TWO_PI_2, TWO_PI_3):
                    own_d.step(v.scalar_tensor_tensor(out=a0, in0=a2_, scalar=-part, in1=a0, op0=ALU.mult, op1=ALU.add))
                    own_d.wait()
                own_d.step(v.tensor_scalar(a0, a0, PI_LIMIT, -PI_LIMIT, ALU.min, ALU.max))
                own_d.wait()
                own_d.step(v.tensor_scalar(a3, a0, -1.0, None, ALU.mult))
                own_d.wait()
                own_d.step(v.tensor_tensor(a3, a3, a0, ALU.max))
                own_d.wait()
                v.tensor_scalar(a1_, a3, -1.0, float(np.pi / 2), ALU.mult, ALU.add).then_inc(angles_ready, 1)

            for n in range(2 * KD):
                if n >= 1:
                    dve.wait_ge(mod_summed, n)
                if n < KD:
                    add_piece(acc[:, :], ("sh1", n), n, mod_summed)
                elif n < 2 * KD - 1:
                    add_piece(acc_sc, ("sc1", n - KD), n - KD, mod_summed)
                else:
                    a = landed(dve, ("sc1", KD - 1))
                    for h in range(2):
                        cut = slice(512 * h, 512 * h + 512)
                        v.scalar_tensor_tensor(out=acc_sc[:, cut], in0=a[:, cut], scalar=silu[:, KD - 1:KD],
                                               in1=acc_sc[:, cut], op0=ALU.mult, op1=ALU.add).then_inc(mod_summed, 1)
                if n == KD:
                    dve.wait_ge(params_in, 16 * 9)
                    v.tensor_copy(rows[64:72, :], posi[64:72, :]).then_inc(posf_ready, 1)
                    own_d.step(v.tensor_scalar(nsink, sink, -1.0, None, ALU.mult))
                    v.tensor_tensor(poolw[:, :, :].rearrange("p g d -> p (g d)"),
                                    poolw[:, :, :].rearrange("p g d -> p (g d)"), scale_row, ALU.mult).then_inc(poolw_ready, 1)
                if n == KD + 2:
                    dve.wait_ge(rows_turned, 1)
                    v.tensor_copy(cols[:, :], psum[:, 4, 0:72]).then_inc(cols_ready, 1)
                if n == 2 * KD - 4:
                    dve.wait_ge(cols_ready, 1)
                    dve.wait_ge(mod_turned, 1)
                    v.tensor_reduce(b1, banks(0).rearrange("p (k n) -> p k n", n=P), AX_X, ALU.add).then_inc(mod_taken, 1)
                    dve.wait_ge(mod_taken, 1)
                    own_d.step(v.tensor_tensor(b1, b1, cols[:, 8 * SH1:8 * SH1 + 8], ALU.add))
            def scale_1(h):
                c4 = slice(4 * h, 4 * h + 4)
                dve.wait_ge(sc1_turned, h + 1)
                own_d.step(v.tensor_reduce(a1[:, c4], bank(2 + h).rearrange("p (k n) -> p k n", n=P), AX_X, ALU.add))
                own_d.wait()
                own_d.step(v.tensor_tensor(a1[:, c4], a1[:, c4],
                                           cols[:, 8 * SC1 + 4 * h:8 * SC1 + 4 * h + 4], ALU.add))
                own_d.wait()
                own_d.step(v.scalar_tensor_tensor(out=a1[:, c4], in0=a1[:, c4], scalar=1.0,
                                                  in1=cols[:, 48 + 4 * h:52 + 4 * h], op0=ALU.add, op1=ALU.mult))
                own_d.wait()

            def make_h(t, h):
                if h == 0:
                    dve.wait_ge(x_turned, t + 1)
                for k in range(4 * h, 4 * h + 4):
                    ins = v.tensor_scalar(xh[:, t % 2, k * P:(k + 1) * P], banks(6 if t == 0 else 1)[:, k * P:(k + 1) * P],
                                          a1[:, k:k + 1], b1[:, k:k + 1], ALU.mult, ALU.add)
                ins.then_inc(h_made, 1)

            def lo_h(t, h):
                dve.wait_ge(h_hi, 2 * t + h + 1)
                v.tensor_tensor(hTl[:, 4 * h:4 * h + 4, :],
                                xh[:, t % 2, 512 * h:512 * h + 512].rearrange("p (k n) -> p k n", n=P),
                                hTh[:, 4 * h:4 * h + 4, :].bitcast(F32), ALU.subtract).then_inc(h_lo, 1)

            scale_1(0)
            make_h(0, 0)
            scale_1(1)
            lo_h(0, 0)
            make_h(0, 1)
            lo_h(0, 1)
            for k in range(KD):
                a = landed(dve, ("wqkv", k))
                dve.wait_ge(wqkv_hi, k + 1)
                v.tensor_tensor(wil[:, k, 0:QKV], a[:, 0:QKV], wih[:, k, 0:QKV].bitcast(F32), ALU.subtract).then_inc(wqkv_lo, 1)
            angles()

            def lo_pT(i, kv):
                nb = 1 if i == 0 else 2
                for blk in range(nb):
                    dve.wait_ge(pT_hi, p_blocks(i, kv, blk))
                    v.tensor_tensor(pTl[:, kv, blk, :, :].rearrange("p h q -> p (h q)"), bank(4 + blk),
                                    pTh[:, kv, blk, :, :].rearrange("p h q -> p (h q)").bitcast(F32),
                                    ALU.subtract).then_inc(pT_lo, 1)

            def add_attn(i, kv):
                dve.wait_ge(attn_shifted, 2 * i + kv + 1)
                o = attn_bank(i, kv).rearrange("p (m e q) -> p m e q", e=2, q=P)
                for e in range(2):
                    r = slice(64 * e, 64 * e + 64)
                    dst = slots[r, i, :].rearrange("p (m q) -> p m q", q=P)[:, 2 * kv:2 * kv + 2, :]
                    ins = v.tensor_tensor(dst, o[r, :, e, :], dst, ALU.add)
                ins.then_inc(attn_kept, 1)

            def maxes(i, kv):
                dve.wait_ge(scored, 2 * i + kv + 1)
                w = P if i == 0 else 2 * P
                g = slice(kv * G, kv * G + G)
                m0 = P if i % 2 == 0 else 0
                if i >= 1:
                    dve.wait_ge(p_turned, 2 * (i - 1) + kv + 1)
                elif kv == 0:
                    dve.wait_ge(mask_ready, 1)
                for h in range(G):
                    ins = v.tensor_tensor_reduce(out=pr[:, kv, h, 0:w], in0=banks(4)[:, 256 * h:256 * h + w],
                                                 in1=mask[:, m0:m0 + w], scale=1.0, scalar=-3e38, op0=ALU.add, op1=ALU.max,
                                                 accum_out=mx[:, kv * G + h:kv * G + h + 1])
                own_d.step(ins)
                own_d.wait()
                own_d.step(v.scalar_tensor_tensor(out=negm[:, g], in0=mx[:, g], scalar=-SCALE, in1=nsink[:, g],
                                                  op0=ALU.mult, op1=ALU.min))
                own_d.wait()
                v.tensor_tensor(earg[:, g], sink[:, g], negm[:, g], ALU.add).then_inc(max_ready, 1)

            def dens(i, kv):
                g = slice(kv * G, kv * G + G)
                dve.wait_ge(exped, 2 * i + kv + 1)
                own_d.step(v.tensor_tensor(den[:, g], den[:, g], es[:, g], ALU.add))
                own_d.wait()
                if i >= 1:
                    dve.wait_ge(normed, 2 * (i - 1) + kv + 1)
                v.reciprocal(rden[:, g], den[:, g]).then_inc(den_ready, 1)

            def lo_qk(i):
                dve.wait_ge(qk_hi, i + 1)
                for e in range(2):
                    r = slice(64 * e, 64 * e + 64)
                    hi, lo = (qT[rows_, :, :].rearrange("p (m e) q -> p m e q", e=2)[:, :, e, :]
                              for rows_ in (r, slice(64 - 64 * e, 128 - 64 * e)))
                    v.tensor_tensor(lo, bank(1)[r, :].rearrange("p (m q) -> p m q", q=P), hi.bitcast(F32), ALU.subtract)
                v.tensor_tensor(kT[:, :, 1, i % 2, :], psum[:, 2, 0:NKV * P].rearrange("p (g n) -> p g n", g=NKV),
                                kT[:, :, 0, i % 2, :].bitcast(F32), ALU.subtract).then_inc(qk_lo, 1)

            def lo_wo(k):
                dve.wait_ge(wo_hi, k + 1)
                v.tensor_tensor(wol[:, k, :], piece_at(place[("wo", k)]), woh[:, k, :].bitcast(F32),
                                ALU.subtract).then_inc(wo_lo_dve, 1)

            def lo_mix(i, h):
                dve.wait_ge(mix_hi, 2 * i + h + 1)
                v.tensor_tensor(mTl[:, 4 * h:4 * h + 4, :],
                                slots[:, i, 512 * h:512 * h + 512].rearrange("p (k n) -> p k n", n=P),
                                mTh[:, 4 * h:4 * h + 4, :].bitcast(F32), ALU.subtract).then_inc(mix_lo, 1)

            def add_carry(t):
                dve.wait_ge(pooled_kept, t + 1)
                c4 = carry[:, :, :].rearrange("p (b g) s -> p b g s", b=2)
                if t >= 1:
                    head = pooledT[:, :].rearrange("p (b g s) -> p b g s", b=2, s=P)[:, :, :, 0:MAX_WINDOW]
                    dve.wait_ge(carry_kept, t)
                    v.tensor_tensor(head, head, c4, ALU.add).then_inc(carry_added, 1)
                    dve.wait_ge(carry_added, t)
                v.tensor_copy(c4, windows[:, :, :, P:BAND]).then_inc(carry_kept, 1)

            def add_job_pieces(pieces):
                for n in pieces:
                    if n >= 1:
                        dve.wait_ge(job_summed, n)
                    if n in (8, 16):
                        dve.wait_ge(mod_turned, n // 8 + 1)
                    add_piece(acc[:, :], (adaln_jobs[n // 8], n % 8), n % 8, job_summed)

            early_pieces = ([], range(2, 5), range(7, 8), range(10, 12), range(14, 16), range(18, 20), range(22, 24), [])
            late_pieces = (range(0, 2), range(5, 7), range(8, 10), range(12, 14), range(16, 18), range(20, 22), [], [])
            for t in range(NT):
                if t >= 2:
                    maxes(t - 2, 0)
                add_job_pieces(early_pieces[t])
                if t in (2, 4):
                    dst, m = (b2, SH2) if t == 2 else (a2, SC2)
                    dve.wait_ge(mod_turned, t // 2 + 1)
                    v.tensor_reduce(dst, banks(1).rearrange("p (k n) -> p k n", n=P), AX_X, ALU.add).then_inc(mod_taken, 1)
                    dve.wait_ge(mod_taken, t // 2 + 1)
                    own_d.step(v.tensor_tensor(dst, dst, cols[:, 8 * m:8 * m + 8], ALU.add))
                    own_d.wait()
                    if t == 4:
                        own_d.step(v.scalar_tensor_tensor(out=a2, in0=a2, scalar=1.0, in1=cols[:, 56:64],
                                                          op0=ALU.add, op1=ALU.mult))
                        own_d.wait()
                if t >= 2:
                    dens(t - 2, 0)
                    maxes(t - 2, 1)
                if t >= 1:
                    lo_qk(t - 1)
                if t >= 2:
                    dens(t - 2, 1)
                if t >= 1:
                    add_job_pieces(late_pieces[t])
                if t == 6:
                    for k in range(KD):
                        dve.wait_ge(job_summed, 24)
                        ins = v.scalar_tensor_tensor(out=acc[:, k * P:(k + 1) * P], in0=ident[:, :],
                                                     scalar=cols[:, 8 * G1 + k:8 * G1 + k + 1],
                                                     in1=acc[:, k * P:(k + 1) * P], op0=ALU.mult, op1=ALU.add)
                    ins.then_inc(gate_biased, 1)
                if t + 1 < NT:
                    make_h(t + 1, 0)
                if t >= 2:
                    lo_pT(t - 2, 0)
                if t + 1 < NT:
                    make_h(t + 1, 1)
                dve.wait_ge(q_squared, t + 1)
                dve.wait_ge(kv_squared, t + 1)
                v.tensor_reduce(ssq, squares[:, 0:AW + KVW]
                                .rearrange("p (h d) -> p h d", d=HEAD_DIM), AX_X, ALU.add).then_inc(qk_sums, 1)
                if t == NT - 1:
                    lo_mix(0, 0)
                if t >= 2:
                    lo_pT(t - 2, 1)
                    add_attn(t - 2, 0)
                if t + 1 < NT:
                    lo_h(t + 1, 0)
                    lo_h(t + 1, 1)
                add_carry(t)
                if t >= 2:
                    add_attn(t - 2, 1)
                dve.wait_ge(qk_root, t + 1)
                if t >= 1:
                    dve.wait_ge(qk_turned, t)
                v.tensor_tensor(qkn[:, 0:NH, :], bank(6).rearrange("p (h d) -> p h d", d=HEAD_DIM),
                                bcast(rq[:, 0:NH], 2, HEAD_DIM), ALU.mult).then_inc(q_normed, 1)
                if t == NT - 1:
                    lo_wo(1)
                dve.wait_ge(v_hi, t + 1)
                for e in range(NKV):
                    ins = v.tensor_scalar(qkn[:, NH + 2 * e:NH + 2 * e + 2, :],
                                          bcast(psum[:, 3, HEAD_DIM * e:HEAD_DIM * (e + 1)], 1, 2),
                                          rq[:, NH + e:NH + e + 1], None, ALU.mult)
                ins.then_inc(k_normed, 1)
                v.tensor_tensor(vv[:, t % 4, :, 1, :],
                                psum[:, 3, KVW:2 * KVW].rearrange("p (g d) -> p g d", g=NKV),
                                vv[:, t % 4, :, 0, :].bitcast(F32), ALU.subtract).then_inc(v_lo, 1)
                if t == 0:
                    add_job_pieces(late_pieces[0])

            def make_h2(i, h):
                dve.wait_ge(x2_turned, 2 * i + h + 1)
                for j in range(4):
                    k = 4 * h + j
                    ins = v.tensor_scalar(hx[:, k * P:(k + 1) * P], bank(4 + h if i == NT - 1 else 3)[:, j * P:(j + 1) * P],
                                          a2[:, k:k + 1], b2[:, k:k + 1], ALU.mult, ALU.add)
                ins.then_inc(h2_made, 1)

            def make_x2(i):
                dve.wait_ge(wo_used, 2 * i + 2)
                v.tensor_tensor(slots[:, i, :], banks(1 if i % 2 else 6), g1b[:, :], ALU.mult).then_inc(x2_gated, 1)
                a = landed(dve, ("x", i))
                dve.wait_ge(x2_gated, i + 1)
                v.tensor_tensor(slots[:, i, :], slots[:, i, :], a, ALU.add).then_inc(x2_ready, 1)

            def add_g2(k):
                if k == 0:
                    dve.wait_ge(mod_turned, 4)
                else:
                    dve.wait_ge(job_summed, 24 + k)
                add_piece(acc[:, :], ("g2", k), k, job_summed)

            maxes(NT - 2, 0)
            lo_wo(2)
            lo_wo(3)
            dens(NT - 2, 0)
            maxes(NT - 2, 1)
            lo_mix(0, 1)
            lo_wo(4)
            lo_qk(NT - 1)
            dens(NT - 2, 1)
            lo_pT(NT - 2, 0)
            lo_wo(7)
            dve.wait_ge(mod_turned, 4)
            v.tensor_copy(g1b[:, :], banks(1)).then_inc(mod_taken, 1)
            lo_mix(1, 0)
            dve.wait_ge(mod_taken, 4)
            make_x2(0)
            add_attn(NT - 2, 0)
            lo_mix(1, 1)
            lo_pT(NT - 2, 1)
            add_g2(0)
            lo_mix(2, 0)
            maxes(NT - 1, 0)
            add_attn(NT - 2, 1)
            dens(NT - 1, 0)
            make_h2(0, 0)
            maxes(NT - 1, 1)
            make_h2(0, 1)
            lo_mix(2, 1)
            dens(NT - 1, 1)
            make_x2(1)
            add_g2(1)
            lo_pT(NT - 1, 0)
            lo_mix(3, 0)
            make_h2(1, 0)
            make_x2(2)
            add_attn(NT - 1, 0)
            make_h2(1, 1)
            lo_pT(NT - 1, 1)
            lo_mix(3, 1)
            add_g2(2)
            for i in range(3, NT):
                if i + 1 < NT:
                    lo_mix(i + 1, 0)
                if i == 3:
                    add_attn(NT - 1, 1)
                make_h2(i - 1, 0)
                if i + 1 < NT:
                    lo_mix(i + 1, 1)
                else:
                    for j in range(2):
                        dve.wait_ge(w1_hi, j + 1)
                        v.tensor_tensor(w1l[:, 4 * j:4 * j + 4, :], raw[:, j, :].rearrange("p (k n) -> p k n", k=4),
                                        w1h[:, 4 * j:4 * j + 4, :].bitcast(F32), ALU.subtract).then_inc(w1_lo, 1)
                make_h2(i - 1, 1)
                make_x2(i)
                add_g2(i)
            for k in range(KD):
                dve.wait_ge(job_summed, 32)
                ins = v.scalar_tensor_tensor(out=acc[:, k * P:(k + 1) * P], in0=ident[:, :],
                                             scalar=cols[:, 8 * G2 + k:8 * G2 + k + 1],
                                             in1=acc[:, k * P:(k + 1) * P], op0=ALU.mult, op1=ALU.add)
            ins.then_inc(gate_biased, 1)
            make_h2(NT - 1, 0)
            make_h2(NT - 1, 1)
            dve.wait_ge(mod_turned, 5)
            v.tensor_copy(g2b[:, :], banks(6)).then_inc(mod_taken, 1)

            def mlp_block(b):
                for u in range(2 * NF):
                    dve.wait_ge(relu_kept, 2 * NF * b + u + 1)
                    v.tensor_tensor(rsq[:, u % 2, :], relu[:, u % 2, :], relu[:, u % 2, :], ALU.mult).then_inc(act_sq, 1)
                    dve.wait_ge(act_sq, 2 * NF * b + u + 1)
                    dve.wait_ge(act_hi, 2 * NF * b + u + 1)
                    cut = slice((u // NF) * 512, (u // NF) * 512 + 512)
                    v.tensor_tensor(aTl[:, u % NF, cut], rsq[:, u % 2, :], aTh[:, u % NF, cut].bitcast(F32),
                                    ALU.subtract).then_inc(act_lo, 1)
                for n in range(2 * NT):
                    dve.wait_ge(down_done, 2 * NT * b + n + 1)
                    o = slots[:, n // 2, (n % 2) * 512:(n % 2) * 512 + 512]
                    v.tensor_tensor(o, bank(4 + n % 4), o, ALU.add).then_inc(added, 1)

            with dve.Fori(0, NB) as b:
                mlp_block(b)

        @block.gpsimd
        def _(pool):
            own_p = Chain(pool, own["pool"])
            g = nc.gpsimd
            own_p.step(g.memset(ident[:, :], 0.0))
            own_p.wait()
            g.affine_select(out=ident[:, :], in_=ident[:, :], compare_op=ALU.not_equal, fill=1.0, base=0,
                            pattern=[[-1, P]], channel_multiplier=1).then_inc(ident_made, 1)
            own_p.step(g.memset(mhalf, -0.5))
            pool.wait_ge(ident_made, 2)

            def lo_wu(j):
                a = landed(pool, ("wu", j))
                pool.wait_ge(wu_hi, j + 1)
                g.tensor_tensor(wil[:, 2 * j:2 * j + 2, QKV:IN], a.rearrange("p (k n) -> p k n", k=2),
                                wih[:, 2 * j:2 * j + 2, QKV:IN].bitcast(F32), ALU.subtract).then_inc(wu_lo, 1)

            own_p.step(g.memset(mask[:, 0:2 * P], 0.0))
            own_p.wait()
            own_p.step(g.affine_select(out=mask[:, 0:P], in_=mask[:, 0:P], compare_op=ALU.is_gt, fill=MASKED, base=0,
                                       pattern=[[1, P]], channel_multiplier=-1))
            own_p.step(g.affine_select(out=mask[:, P:2 * P], in_=mask[:, P:2 * P], compare_op=ALU.is_ge, fill=MASKED, base=0,
                                       pattern=[[-1, P]], channel_multiplier=1))
            own_p.wait()
            g.tensor_copy(mask[:, 2 * P:3 * P], mask[:, 0:P]).then_inc(mask_ready, 1)

            def band_of(i, cut, base):
                w, n = POOL_WINDOWS[i], cut.shape[1]
                own_p.step(g.affine_select(out=cut, in_=cut, compare_op=ALU.is_ge, fill=0.0, base=base,
                                           pattern=[[1, n]], channel_multiplier=-1))
                own_p.wait()
                own_p.step(g.affine_select(out=cut, in_=cut, compare_op=ALU.is_ge, fill=0.0, base=w - 1 - base,
                                           pattern=[[-1, n]], channel_multiplier=1))
                own_p.wait()

            def less_token(i, n):
                return g.tensor_tensor(band[:, i, 0:n], band[:, i, 0:n], ident[:, 0:n], ALU.subtract)

            own_p.step(g.memset(band[:, :, P:BAND], 0.0))
            for i, w in enumerate(POOL_WINDOWS):
                own_p.step(g.memset(band[:, i, 0:P], 1.0 / w))
            own_p.wait()
            for i, w in enumerate(POOL_WINDOWS):
                for s in range(w - 1):
                    own_p.step(g.memset(band[:, i, s:s + 1], float(np.float32(1.0) / np.float32(s + 1))))
                own_p.wait()
                band_of(i, band[:, i, 0:P], 0)
                own_p.step(less_token(i, P))
                own_p.wait()
                own_p.step(g.memset(band[:, i, P:BAND], 1.0 / w))
                own_p.wait()
                band_of(i, band[:, i, P:BAND], P)
            own_p.step(g.tensor_copy(small[:, 200:201], small[:, 164:165]))
            pool.wait_ge(own["pool"], own_p.n)
            g.tensor_copy(small[:, 201:202], small[:, 164:165]).then_inc(consts_made, 1)

            def normalise(i, kv):
                pool.wait_ge(den_ready, 2 * i + kv + 1)
                w = P if i == 0 else 2 * P
                r = slice(kv * G, kv * G + G)
                g.tensor_tensor(pr[:, kv, :, 0:w], pr[:, kv, :, 0:w], bcast(rden[:, r], 2, w), ALU.mult).then_inc(normed, 1)

            def root(dst, src, n, done):
                own_p.step(g.tensor_scalar(dst, src, 1.0 / n, EPS, ALU.mult, ALU.add))
                own_p.wait()
                g.tensor_tensor(dst, dst, mhalf[:, 0:dst.shape[1]], ALU.pow).then_inc(done, 1)

            def root_x(t):
                pool.wait_ge(x_squared, t + 1)
                root(rx[:, t:t + 1], ssx[:, t:t + 1], D, x_root)

            root_x(0)
            for j in range(KD // 2):
                lo_wu(j)

            def lo_wo(k):
                pool.wait_ge(wo_hi, k + 1)
                g.tensor_tensor(wol[:, k, :], piece_at(place[("wo", k)]), woh[:, k, :].bitcast(F32),
                                ALU.subtract).then_inc(wo_lo_pool, 1)

            for t in range(NT):
                if t >= 2:
                    normalise(t - 2, 0)
                if t + 1 < NT:
                    root_x(t + 1)
                if t >= 2:
                    normalise(t - 2, 1)
                pool.wait_ge(qk_sums, t + 1)
                if t >= 1:
                    pool.wait_ge(k_normed, t)
                root(rq, ssq, HEAD_DIM, qk_root)
                if t == NT - 1:
                    lo_wo(0)
                pool.wait_ge(k_normed, t + 1)
                own_p.step(g.tensor_tensor(qkn[:, 0:NH, :], qkn[:, 0:NH, :], bcast(gqk[:, 0, :], 1, NH), ALU.mult))
                own_p.step(g.tensor_tensor(qkn[:, NH:NHD, :], qkn[:, NH:NHD, :], bcast(gqk[:, 1, :], 1, 2 * NKV), ALU.mult))
                own_p.wait()
                if t == 0:
                    pool.wait_ge(trig_ready, 4)
                part = qkn[:, :, 0:ROT_DIM].rearrange("p h (a f) -> p h a f", a=2)
                for j in range(2):
                    own_p.step(g.tensor_tensor(rot[:, j, :, :, :], part, bcast(trig[:, t, 2 * j:2 * j + 2, :], 1, NHD),
                                               ALU.mult))
                own_p.wait()
                own_p.step(g.tensor_tensor(part[:, :, 0, :], rot[:, 0, :, 0, :], rot[:, 0, :, 1, :], ALU.subtract))
                g.tensor_tensor(part[:, :, 1, :], rot[:, 1, :, 0, :], rot[:, 1, :, 1, :], ALU.add).then_inc(qk_roped, 1)
                if t == 0:
                    pool.wait_ge(band_done, 1)
                    for i, w in enumerate(POOL_WINDOWS):
                        own_p.step(g.memset(band[:, i, 0:w], 1.0 / w))
                        own_p.wait()
                        band_of(i, band[:, i, 0:w], 0)
                        if i + 1 < NP:
                            own_p.step(less_token(i, w))
                            own_p.wait()
                    less_token(NP - 1, POOL_WINDOWS[-1]).then_inc(consts_made, 1)

            def root_x2(i):
                pool.wait_ge(x2_squared, i + 1)
                root(r2[:, i:i + 1], ss2[:, i:i + 1], D, x2_root)

            def lo_h2(i, h):
                pool.wait_ge(h2_hi, 2 * i + h + 1)
                g.tensor_tensor(h2T[:, i, 1, 4 * h:4 * h + 4, :],
                                hx[:, 512 * h:512 * h + 512].rearrange("p (k n) -> p k n", n=P),
                                h2T[:, i, 0, 4 * h:4 * h + 4, :].bitcast(F32), ALU.subtract).then_inc(h2_lo, 1)

            normalise(NT - 2, 0)
            lo_wo(5)
            lo_wo(6)
            normalise(NT - 2, 1)
            root_x2(0)
            normalise(NT - 1, 0)
            lo_h2(0, 0)
            lo_h2(0, 1)
            normalise(NT - 1, 1)
            root_x2(1)
            lo_h2(1, 0)
            root_x2(2)
            lo_h2(1, 1)
            for i in range(3, NT):
                lo_h2(i - 1, 0)
                lo_h2(i - 1, 1)
                if i + 1 < NT:
                    root_x2(i)

            def lo_w1(b):
                for j in range(2):
                    pool.wait_ge(w1_hi, 2 * b + j + 1)
                    g.tensor_tensor(w1l[:, 4 * j:4 * j + 4, :], raw[:, j, :].rearrange("p (k n) -> p k n", k=4),
                                    w1h[:, 4 * j:4 * j + 4, :].bitcast(F32), ALU.subtract).then_inc(w1_lo, 1)

            def prepare_w2(b, use):
                for j in range(2):
                    pool.wait_ge(raw_in[2 + j], 16 * use)
                    g.tensor_tensor(raw[:, 2 + j, :], raw[:, 2 + j, :], g2b[:, :], ALU.mult).then_inc(w2_gated, 1)
                for j in range(2):
                    pool.wait_ge(w2_hi, 2 * b + j + 1)
                    g.tensor_tensor(w2l[:, j, :], raw[:, 2 + j, :], w2h[:, j, :].bitcast(F32), ALU.subtract).then_inc(w2_lo, 1)

            root_x2(NT - 1)
            lo_h2(NT - 1, 0)
            lo_h2(NT - 1, 1)
            pool.wait_ge(mod_taken, 5)
            prepare_w2(0, MLP_USE + 1)
            lo_w1(1)
            with pool.Fori(1, NB - 1) as b:
                prepare_w2(b, MLP_USE + 1 + b)
                lo_w1(b + 1)
            prepare_w2(NB - 1, MLP_USE + NB)

        @block.tensor
        def _(pe):
            mm = nc.tensor.matmul

            def tr(o, i, rows_=P):
                return nc.tensor.transpose(o, i, ident[0:rows_, 0:rows_])

            def three(o, wh, wl, ah, al, first, last):
                mm(o, wh, ah, start=first, stop=False)
                mm(o, wh, al, start=False, stop=False)
                return mm(o, wl, ah, start=False, stop=last)

            def turn_x(t):
                pe.wait_ge(x_scaled, t + 1)
                for k in range(KD):
                    ins = tr(banks(6 if t == 0 else 1)[:, k * P:(k + 1) * P], xh[:, t % 2, k * P:(k + 1) * P])
                ins.then_inc(x_turned, 1)

            def keep_clock(n):
                for _ in range(n):
                    mm(psum[:, 5, 0:P], ident[:, :], ident[:, :], start=True, stop=True)

            def turn_sums(o, sums):
                for k in range(o.shape[1] // P):
                    ins = tr(o[:, k * P:(k + 1) * P], sums[:, k * P:(k + 1) * P])
                return ins

            def project(o, a, b, t, u=False):
                for k in range(KD):
                    if u and k % 4 == 0:
                        pe.wait_ge(h_lo, 2 * t + k // 4 + 1)
                    if t == 0 and u:
                        pe.wait_ge(wu_lo, k // 2 + 1)
                    if t == 0 and not u:
                        pe.wait_ge(wqkv_lo, k + 1)
                    ins = three(o, hTh[:, k, :], hTl[:, k, :], wih[:, k, a:b], wil[:, k, a:b], k == 0, k == KD - 1)
                return ins

            def turn_p(i, kv):
                pe.wait_ge(normed, 2 * i + kv + 1)
                if kv:
                    pe.wait_ge(pT_lo, p_blocks(i, 0))
                else:
                    pe.wait_ge(max_ready, 2 * i + 2)
                for blk in range(1 if i == 0 else 2):
                    for h in range(G):
                        ins = tr(psum[:, 4 + blk, h * P:(h + 1) * P], pr[:, kv, h, blk * P:(blk + 1) * P])
                ins.then_inc(p_turned, 1)

            def attend(i, kv):
                pe.wait_ge(v_lo, i + 1)
                blocks = 1 if i == 0 else 2
                for blk in range(blocks):
                    pe.wait_ge(pT_lo, p_blocks(i, kv, blk))
                    s = (i if blk == i % 2 else i - 1) % 4
                    both = vv[:, s, kv, :, :].rearrange("p a d -> p (a d)")
                    mm(attn_bank(i, kv), both, pTh[:, kv, blk, :, :].rearrange("p h q -> p (h q)"), start=blk == 0, stop=False)
                    ins = mm(attn_bank(i, kv), both, pTl[:, kv, blk, :, :].rearrange("p h q -> p (h q)"), start=False,
                             stop=blk == blocks - 1)
                ins.then_inc(pv_done, 1)

            def score(i, kv):
                if kv:
                    pe.wait_ge(max_ready, 2 * i + 1)
                elif i >= 1:
                    pe.wait_ge(pT_lo, p_blocks(i - 1, 1))
                for h in range(G):
                    w = P if i == 0 else 2 * P
                    o = psum[:, 4 + h // 2, (h % 2) * 256:(h % 2) * 256 + w]
                    for a in range(2):
                        if i == 0:
                            k_ = kT[:, kv, a, 0, :]
                        else:
                            k_ = kT[:, kv, a, :, :].rearrange("p b n -> p (b n)")
                        ins = mm(o, qT[:, kv * G + h, :], k_, start=a == 0, stop=a == 1)
                ins.then_inc(scored, 1)

            def project_u(t):
                if t >= 3:
                    pe.wait_ge(attn_kept, 2 * (t - 2))
                project(bank(0), QKV, IN, t, u=True).then_inc(u_done, 1)

            def pool_out(i):
                if i == 0:
                    pe.wait_ge(poolw_ready, 1)
                if i == 0:
                    pe.wait_ge(pooled_kept, 1)
                else:
                    pe.wait_ge(carry_added, i)
                    pe.wait_ge(pout_kept, i)
                if i >= 2:
                    pe.wait_ge(attn_kept, 2 * (i - 2) + 1)
                for j in range(NP):
                    ins = mm(psum[:, 7, j * P:(j + 1) * P], poolw[:, j, :], pooledT[:, j * P:(j + 1) * P],
                             start=True, stop=True)
                ins.then_inc(pout_done, 1)

            def turn_qk(i):
                pe.wait_ge(qk_roped, i + 1)
                pe.wait_ge(carry_kept, i + 1)
                for m in range(NH // 2):
                    tr(bank(1)[:, m * P:(m + 1) * P], qkn[:, 2 * m:2 * m + 2, :].rearrange("p h d -> p (h d)"))
                for e in range(NKV):
                    ins = tr(psum[:, 2, e * P:(e + 1) * P], qkn[:, NH + 2 * e:NH + 2 * e + 2, :].rearrange("p h d -> p (h d)"))
                ins.then_inc(qk_turned, 1)

            def pool_windows(t):
                pe.wait_ge(u_kept, t + 1)
                if t < 2:
                    pe.wait_ge(consts_made, t + 1)
                if t + 1 < NT:
                    pe.wait_ge(h_made, 2 * (t + 2))
                else:
                    pe.wait_ge(qk_lo, t)
                for j in range(NP):
                    ins = mm(windows[:, j // 2, j % 2, :], usb[:, t % 2, j * P:(j + 1) * P], band[:, j, :],
                             start=True, stop=True)
                ins.then_inc(band_done, 1)

            pe.wait_ge(ident_made, 2)
            turn_x(0)
            pe.wait_ge(params_in, 16 * 9)
            pe.wait_ge(posf_ready, 1)
            tr(psum[:, 4, 0:72], rows[0:72, :], 72).then_inc(rows_turned, 1)
            pe.wait_ge(mod_summed, KD)
            turn_sums(banks(0), acc).then_inc(mod_turned, 1)
            pe.wait_ge(mod_summed, 2 * KD - 3)
            keep_clock(10)
            for h in range(2):
                pe.wait_ge(mod_summed, 2 * KD + h)
                turn_sums(bank(2 + h), acc_sc[:, 512 * h:512 * h + 512]).then_inc(sc1_turned, 1)
            keep_clock(14)
            for t in range(NT):
                project_u(t)
                if t in (2, 4):
                    pe.wait_ge(job_summed, 4 * t)
                    pe.wait_ge(carry_kept, t)
                    turn_sums(banks(1), acc).then_inc(mod_turned, 1)
                if t >= 2:
                    score(t - 2, 1)
                if t in (2, 4):
                    pe.wait_ge(mod_taken, t // 2 + 1)
                if t >= 1:
                    turn_qk(t - 1)
                if t >= 1:
                    pe.wait_ge(q_normed, t)
                project(bank(6), 0, AW, t).then_inc(q_done, 1)
                if t + 1 < NT:
                    if t >= 1:
                        pe.wait_ge(qk_lo, t)
                    turn_x(t + 1)
                if t >= 2:
                    turn_p(t - 2, 0)
                if t >= 1:
                    pe.wait_ge(v_lo, t)
                project(psum[:, 3, 0:2 * KVW], AW, QKV, t).then_inc(kv_done, 1)
                if t >= 2:
                    turn_p(t - 2, 1)
                    pe.wait_ge(pout_kept, t)
                    attend(t - 2, 0)
                pool_windows(t)
                if t >= 2:
                    pe.wait_ge(u_kept, t + 1)
                    attend(t - 2, 1)
                if t >= 1:
                    pe.wait_ge(qk_lo, t)
                    score(t - 1, 0)
                pool_out(t)

            def project_out(i, k):
                pair = 1 if i % 2 else 6
                if k == 0:
                    if i >= 2:
                        pe.wait_ge(x2_gated, i - 1)
                    elif i == 1:
                        pe.wait_ge(mod_taken, 4)
                    else:
                        pe.wait_ge(q_normed, NT)
                        pe.wait_ge(pout_kept, NT)
                if i == 0:
                    wo_lo_made(pe, k)
                if k % 4 == 0:
                    pe.wait_ge(mix_lo, 2 * i + k // 4 + 1)
                for n in range(2):
                    ins = three(bank(pair + n), mTh[:, k, :], mTl[:, k, :], woh[:, k, 512 * n:512 * n + 512],
                                wol[:, k, 512 * n:512 * n + 512], k == 0, k == KD - 1)
                if k % 4 == 3:
                    ins.then_inc(wo_used, 1)

            def project_out_half(i, h):
                for k in range(4 * h, 4 * h + 4):
                    project_out(i, k)

            def turn_x2(i, h):
                if h == 0:
                    pe.wait_ge(x2_scaled, i + 1)
                if i == NT - 1:
                    pe.wait_ge(pT_lo, p_blocks(NT - 1, 1))
                elif i == 0 and h == 0:
                    pe.wait_ge(v_lo, NT)
                else:
                    pe.wait_ge(h2_made, 2 * i + h)
                for j in range(4):
                    k = 4 * h + j
                    ins = tr(bank(4 + h if i == NT - 1 else 3)[:, j * P:(j + 1) * P], hx[:, k * P:(k + 1) * P])
                ins.then_inc(x2_turned, 1)

            def gate_rows(pair):
                for n in range(2):
                    ins = mm(bank(pair + n), ones[:, :], acc[:, 512 * n:512 * n + 512], start=True, stop=True)
                ins.then_inc(mod_turned, 1)

            def attend_late(i, kv):
                pe.wait_ge(attn_kept, 2 * i + kv)
                attend(i, kv)

            project_out(0, 0)
            project_out(0, 1)
            score(NT - 2, 1)
            project_out(0, 2)
            turn_qk(NT - 1)
            project_out(0, 3)
            turn_p(NT - 2, 0)
            project_out(0, 4)
            project_out(0, 5)
            pe.wait_ge(qk_lo, NT)
            pe.wait_ge(gate_biased, 1)
            gate_rows(1)
            project_out(0, 6)
            project_out(0, 7)
            attend_late(NT - 2, 0)
            turn_p(NT - 2, 1)
            project_out_half(1, 0)
            attend_late(NT - 2, 1)
            score(NT - 1, 0)
            project_out_half(1, 1)
            turn_x2(0, 0)
            score(NT - 1, 1)
            turn_x2(0, 1)
            project_out_half(2, 0)
            turn_p(NT - 1, 0)
            project_out_half(2, 1)
            turn_x2(1, 0)
            attend_late(NT - 1, 0)
            turn_p(NT - 1, 1)
            turn_x2(1, 1)
            project_out_half(3, 0)
            attend_late(NT - 1, 1)
            project_out(3, 4)
            project_out(3, 5)
            turn_x2(2, 0)
            project_out(3, 6)
            project_out(3, 7)
            turn_x2(2, 1)
            for i in range(4, NT):
                project_out_half(i, 0)
                project_out(i, 4)
                project_out(i, 5)
                turn_x2(i - 1, 0)
                project_out(i, 6)
                project_out(i, 7)
                turn_x2(i - 1, 1)

            def mlp_block(b, first):
                for u in range(2 * NF):
                    f, n = u % NF, u // NF
                    if first:
                        if u == 0:
                            pe.wait_ge(attn_kept, 2 * NT)
                            pe.wait_ge(h2_lo, NT)
                        if u == 1:
                            pe.wait_ge(x2_gated, NT)
                        if u == NF:
                            pe.wait_ge(h2_lo, 2 * NT)
                        if u == 3:
                            pe.wait_ge(h2_made, 2 * (NT - 1))
                    else:
                        pe.wait_ge(relu_kept, 2 * NF * (b - 1) + u + 1)
                    for k in range(KD):
                        if first and u == 1 and k == 4:
                            turn_x2(NT - 1, 0)
                            turn_x2(NT - 1, 1)
                            pe.wait_ge(gate_biased, 2)
                            gate_rows(6)
                        if u == 0 and k % 4 == 0:
                            pe.wait_ge(w1_lo, 2 * b + k // 4 + 1)
                        ins = three(bank(u).rearrange("p (i s) -> p i s", s=P),
                                    w1h[:, k, f * P:(f + 1) * P], w1l[:, k, f * P:(f + 1) * P],
                                    h2T[:, 4 * n:4 * n + 4, 0, k, :], h2T[:, 4 * n:4 * n + 4, 1, k, :],
                                    k == 0, k == KD - 1)
                    ins.then_inc(up_done, 1)
                for n in range(2 * NT):
                    i, half = n // 2, n % 2
                    cut = slice(512 * half, 512 * half + 512)
                    if n == 0:
                        pe.wait_ge(act_lo, 2 * NF * b + NF)
                        pe.wait_ge(w2_lo, 2 * b + 2)
                    if n == NT:
                        pe.wait_ge(act_lo, 2 * NF * b + 2 * NF)
                    if first and n < 4:
                        if n == 0:
                            pe.wait_ge(mod_taken, 5)
                            pe.wait_ge(h2_made, 2 * NT)
                    else:
                        pe.wait_ge(added, 2 * NT * b + n - 3)
                    for f in range(NF):
                        ins = three(bank(4 + n % 4), aTh[:, f, i * P:(i + 1) * P], aTl[:, f, i * P:(i + 1) * P],
                                    w2h[:, f, cut], w2l[:, f, cut], f == 0, f == NF - 1)
                    ins.then_inc(down_done, 1)

            mlp_block(0, True)
            with pe.Fori(1, NB) as b:
                mlp_block(b, False)


_INS = ["x", "c", "positions", "w_ada", "b_ada", "norm1_g", "w_in", "q_norm_g", "k_norm_g", "attn_sinks",
        "pool_w", "pool_scale", "w_o", "norm2_g", "w_mlp_in", "w_mlp_out"]


def kernel(**inputs):
    import concourse.bacc as bacc
    from concourse.bass_utils import run_bass_kernel_spmd

    nc = bacc.Bacc("TRN2", target_bir_lowering=False, num_devices=1)
    arrays, args = {}, []
    for name in _INS:
        a = np.ascontiguousarray(inputs[name])
        arrays[f"in_{name}"] = a
        args.append(nc.dram_tensor(f"in_{name}", a.shape, mybir.dt.from_np(a.dtype), kind="ExternalInput").ap())
    shape = inputs["x"].shape
    result = nc.dram_tensor("out_0", shape, F32, kind="ExternalOutput").ap()
    build(nc, *args, result)
    r = run_bass_kernel_spmd(nc, [arrays], core_ids=[0])
    return r.results[0]["out_0"]
```
